# Optimizing a Trainium2 kernel written in Bass

```python
import math
import jax, jax.numpy as jnp
from jax import lax
import numpy as np

D_MODEL = 1024
BATCH = 1
SEQ = 256
DEPTH = 1

GRID_W = 64
CTX_LEN = 256

D_MIX = D_MODEL
D_FOURIER = D_MIX // 4
FOURIER_GROUPS = 4
D_FG = D_FOURIER // FOURIER_GROUPS
HEAD_DIM = 64
NA_HEADS = (D_MIX // 2) // HEAD_DIM
D_NA = NA_HEADS * HEAD_DIM
D_CONV = D_MIX - D_FOURIER - D_NA
CONV_WIDTH = 3
D_IN_PROJ = D_FOURIER + 3 * D_NA + 3 * D_CONV

NA_KH = 8
NA_KW = 16
NA_QB = 16
NA_KB = 32

N_GROUPS = 4
EXPERTS_PER_GROUP = 8
N_EXPERTS = N_GROUPS * EXPERTS_PER_GROUP
TOP_K = 2
D_EXPERT = 512

EPS = 1e-6
NEG_INF = -1e30


def rms_norm(x, gain):
    xf = x.astype(jnp.float32)
    y = xf * lax.rsqrt(jnp.mean(xf * xf, axis=-1, keepdims=True) + EPS)
    return (y * gain.astype(jnp.float32)).astype(x.dtype)

def split_in(u):
    o = [D_FOURIER, D_FOURIER + D_NA, D_FOURIER + 2 * D_NA, D_FOURIER + 3 * D_NA,
         D_FOURIER + 3 * D_NA + D_CONV, D_FOURIER + 3 * D_NA + 2 * D_CONV]
    f, q, k, v, gb, gc, h = jnp.split(u, o, axis=-1)
    heads = lambda t: t.reshape(*t.shape[:-1], NA_HEADS, HEAD_DIM)
    return f, heads(q), heads(k), heads(v), gb, gc, h

def fourier_mix(f):
    b, n, _ = f.shape
    fg = f.reshape(b, n, FOURIER_GROUPS, D_FG).astype(jnp.float32)
    out = jnp.fft.fft2(fg, axes=(1, 3), norm="ortho").real
    return out.reshape(b, n, D_FOURIER).astype(f.dtype)

def short_conv(h, w):
    return lax.conv_general_dilated(
        h, w[:, None, :].astype(h.dtype), window_strides=(1,), padding=((1, 1),),
        dimension_numbers=("NWC", "WIO", "NWC"), feature_group_count=h.shape[-1])

def na_latent(q, k, v, kc, vc, rpb):
    b, n, h, dh = q.shape
    rows = n // GRID_W
    kh = min(NA_KH, rows)
    ncb = GRID_W // NA_QB
    r = jnp.arange(rows)
    row_start = jnp.clip(r - kh // 2, 0, rows - kh)
    row_idx = row_start[:, None] + jnp.arange(kh)[None, :]
    cols = jnp.arange(GRID_W)
    col_start = jnp.clip(cols - NA_KW // 2, 0, GRID_W - NA_KW)
    band_start = jnp.clip(col_start[::NA_QB], 0, GRID_W - NA_KB)
    band_idx = band_start[:, None] + jnp.arange(NA_KB)[None, :]
    qcol = cols.reshape(ncb, NA_QB)
    qcs = col_start.reshape(ncb, NA_QB)
    kcol = band_idx[:, None, :]
    valid = (kcol >= qcs[..., None]) & (kcol < qcs[..., None] + NA_KW)
    roff = row_idx - r[:, None] + (NA_KH - 1)
    coff = jnp.clip(kcol - qcol[..., None] + (NA_KW - 1), 0, 2 * NA_KW - 2)
    bias = rpb[:, roff[:, None, None, :, None], coff[None, :, :, None, :]]

    qg = q.reshape(b, rows, ncb, NA_QB, h, dh)
    kg = k.reshape(b, rows, GRID_W, h, dh)
    vg = v.reshape(b, rows, GRID_W, h, dh)
    ri = row_idx[:, :, None, None]
    ci = band_idx[None, None]
    kb = kg[:, ri, ci]
    vb = vg[:, ri, ci]

    s_loc = jnp.einsum("brcqhd,brkcjhd->bhrcqkj", qg, kb).astype(jnp.float32)
    s_loc = jnp.where(valid[:, :, None, :], s_loc + bias.astype(jnp.float32), NEG_INF)
    s_ctx = jnp.einsum("brcqhd,blhd->bhrcql", qg, kc).astype(jnp.float32)
    kj = kh * NA_KB
    s = jnp.concatenate([s_loc.reshape(*s_loc.shape[:5], kj), s_ctx], axis=-1)
    p = jax.nn.softmax(s, axis=-1).astype(v.dtype)
    p_loc = p[..., :kj].reshape(s_loc.shape)
    p_ctx = p[..., kj:]
    o = (jnp.einsum("bhrcqkj,brkcjhd->brcqhd", p_loc, vb)
         + jnp.einsum("bhrcql,blhd->brcqhd", p_ctx, vc))
    return o.reshape(b, n, h * dh)

def na_context(qc, kc, vc):
    s = jnp.einsum("blhd,bmhd->bhlm", qc, kc).astype(jnp.float32)
    p = jax.nn.softmax(s, axis=-1).astype(vc.dtype)
    o = jnp.einsum("bhlm,bmhd->blhd", p, vc)
    return o.reshape(*o.shape[:2], D_NA)

def mix_out(f, attn, conv, w_fourier, w_out):
    return jnp.concatenate([fourier_mix(f) @ w_fourier, attn, conv], axis=-1) @ w_out

def hier_moe(t, w_rg, b_rg, w_re, b_re, w_gate, w_up, w_down):
    n_tok = t.shape[0]
    g_logits = (t @ w_rg + b_rg).astype(jnp.float32)
    g_prob = jax.nn.softmax(g_logits, axis=-1)
    g_idx = jnp.argmax(g_logits, axis=-1)
    g_w = jnp.take_along_axis(g_prob, g_idx[:, None], axis=-1)
    e_logits = (t @ w_re + b_re).astype(jnp.float32).reshape(n_tok, N_GROUPS, EXPERTS_PER_GROUP)
    e_sel = jnp.take_along_axis(e_logits, g_idx[:, None, None], axis=1)[:, 0]
    top_v, top_i = lax.top_k(e_sel, TOP_K)
    pair_w = g_w * jax.nn.softmax(top_v, axis=-1)
    expert_id = g_idx[:, None] * EXPERTS_PER_GROUP + top_i
    combine = jnp.sum(jax.nn.one_hot(expert_id, N_EXPERTS, dtype=jnp.float32)
                      * pair_w[..., None], axis=1).astype(t.dtype)
    y = jnp.zeros_like(t)
    for e in range(N_EXPERTS):
        he = jax.nn.silu(t @ w_gate[e]) * (t @ w_up[e])
        y = y + combine[:, e:e + 1] * (he @ w_down[e])
    return y

def trunk_layer(x, xc, mod_x, mod_c, norm1, norm2, w_in, w_fourier, w_conv, rpb, w_out,
                w_rg, b_rg, w_re, b_re, w_gate, w_up, w_down, last):
    b, n, d = x.shape
    l = xc.shape[1]
    sh1, sc1, g1, sh2, sc2, g2 = jnp.split(mod_x[:, None, :], 6, axis=-1)
    csh1, csc1, cg1, csh2, csc2, cg2 = jnp.split(mod_c, 6, axis=-1)
    scale = 1.0 / math.sqrt(HEAD_DIM)

    ux = (rms_norm(x, norm1) * (1 + sc1) + sh1) @ w_in
    uc = (rms_norm(xc, norm1) * (1 + csc1) + csh1) @ w_in
    fx, qx, kx, vx, bx, cx, hx = split_in(ux)
    fc, qc, kc, vc, bc, cc, hc = split_in(uc)
    attn_x = na_latent(qx * scale, kx, vx, kc, vc, rpb)
    conv_x = bx * short_conv(cx * hx, w_conv)
    x = x + g1 * mix_out(fx, attn_x, conv_x, w_fourier, w_out)
    if not last:
        attn_c = na_context(qc * scale, kc, vc)
        conv_c = bc * short_conv(cc * hc, w_conv)
        xc = xc + cg1 * mix_out(fc, attn_c, conv_c, w_fourier, w_out)

    hx2 = rms_norm(x, norm2) * (1 + sc2) + sh2
    if last:
        y = hier_moe(hx2.reshape(-1, d), w_rg, b_rg, w_re, b_re, w_gate, w_up, w_down)
        x = x + g2 * y.reshape(b, n, d)
    else:
        hc2 = rms_norm(xc, norm2) * (1 + csc2) + csh2
        tok = jnp.concatenate([hx2.reshape(-1, d), hc2.reshape(-1, d)], axis=0)
        y = hier_moe(tok, w_rg, b_rg, w_re, b_re, w_gate, w_up, w_down)
        x = x + g2 * y[:b * n].reshape(b, n, d)
        xc = xc + cg2 * y[b * n:].reshape(b, l, d)
    return x, xc

def first_inputs(seed: int = 0) -> dict:
    key = jax.random.key(seed)
    ks = jax.random.split(key, 24)
    d = D_MODEL
    nrm = lambda k, shape, s: jax.random.normal(k, shape, jnp.float32) * s
    return {
        "x": nrm(ks[0], (BATCH, SEQ, d), 1.0),
        "c": nrm(ks[1], (BATCH, d), 1.0),
        "ctx": nrm(ks[2], (BATCH, CTX_LEN, d), 1.0),
        "c_ctx": nrm(ks[3], (d,), 1.0),
        "w_ada": nrm(ks[4], (DEPTH, d, 6 * d), 0.5 * d ** -0.5),
        "b_ada": nrm(ks[5], (DEPTH, 6 * d), 0.02),
        "norm1": 1.0 + nrm(ks[6], (DEPTH, d), 0.05),
        "norm2": 1.0 + nrm(ks[7], (DEPTH, d), 0.05),
        "w_in": nrm(ks[8], (DEPTH, d, D_IN_PROJ), d ** -0.5),
        "w_fourier": nrm(ks[9], (DEPTH, D_FOURIER, D_FOURIER), D_FOURIER ** -0.5),
        "w_conv": nrm(ks[10], (DEPTH, CONV_WIDTH, D_CONV), CONV_WIDTH ** -0.5),
        "rpb": nrm(ks[11], (DEPTH, NA_HEADS, 2 * NA_KH - 1, 2 * NA_KW - 1), 0.1),
        "w_out": nrm(ks[12], (DEPTH, D_MIX, d), D_MIX ** -0.5),
        "w_rg": nrm(ks[13], (DEPTH, d, N_GROUPS), d ** -0.5),
        "b_rg": nrm(ks[14], (DEPTH, N_GROUPS), 0.01),
        "w_re": nrm(ks[15], (DEPTH, d, N_EXPERTS), d ** -0.5),
        "b_re": nrm(ks[16], (DEPTH, N_EXPERTS), 0.01),
        "w_gate": nrm(ks[17], (DEPTH, N_EXPERTS, d, D_EXPERT), d ** -0.5),
        "w_up": nrm(ks[18], (DEPTH, N_EXPERTS, d, D_EXPERT), d ** -0.5),
        "w_down": nrm(ks[19], (DEPTH, N_EXPERTS, D_EXPERT, d), D_EXPERT ** -0.5),
        "norm_final": 1.0 + nrm(ks[20], (d,), 0.05),
    }

def first_block(x, c, ctx, c_ctx, w_ada, b_ada, norm1, norm2, w_in, w_fourier, w_conv, rpb,
              w_out, w_rg, b_rg, w_re, b_re, w_gate, w_up, w_down, norm_final):
    xc = ctx
    sc = jax.nn.silu(c)
    scc = jax.nn.silu(c_ctx)
    for li in range(DEPTH):
        mod_x = sc @ w_ada[li] + b_ada[li]
        mod_c = scc @ w_ada[li] + b_ada[li]
        x, xc = trunk_layer(x, xc, mod_x, mod_c, norm1[li], norm2[li], w_in[li], w_fourier[li],
                            w_conv[li], rpb[li], w_out[li], w_rg[li], b_rg[li], w_re[li],
                            b_re[li], w_gate[li], w_up[li], w_down[li], li == DEPTH - 1)
    return rms_norm(x, norm_final)


DEPTH_2 = 4

N_HEADS = D_MODEL // HEAD_DIM
SWA_KV_HEADS = max(1, N_HEADS // 8)
N_MIXERS = 3
SB_BLOCK = 128
MOBA_BLOCK = 256
MOBA_TOPK = 3
MOBA_QCHUNK = 16
SWA_WINDOW = 128
ROPE_THETA = 10000.0
D_FF = -(-8 * D_MODEL // (3 * 256)) * 256


def rms_norm_2(x, gain):
    xf = x.astype(jnp.float32)
    var = jnp.mean(xf * xf, axis=-1, keepdims=True)
    return (xf * lax.rsqrt(var + EPS)).astype(x.dtype) * gain

def modulate(h, shift, scale):
    return h * (1.0 + scale) + shift

def split_heads(t, n):
    b, s, _ = t.shape
    return t.reshape(b, s, n, HEAD_DIM).transpose(0, 2, 1, 3)

def merge_heads(t):
    b, n, s, d = t.shape
    return t.transpose(0, 2, 1, 3).reshape(b, s, n * d)

def rope_tables(seq_len):
    inv_freq = 1.0 / (ROPE_THETA ** (jnp.arange(0, HEAD_DIM, 2, dtype=jnp.float32) / HEAD_DIM))
    ang = jnp.arange(seq_len, dtype=jnp.float32)[:, None] * inv_freq[None, :]
    return jnp.cos(ang), jnp.sin(ang)

def apply_rope(x, cos, sin):
    cos = cos.astype(x.dtype)
    sin = sin.astype(x.dtype)
    x1, x2 = jnp.split(x, 2, axis=-1)
    return jnp.concatenate([x1 * cos - x2 * sin, x2 * cos + x1 * sin], axis=-1)

def stick_breaking_attention(h, w_in, w_out):
    b, s_len, _ = h.shape
    q, k, v = jnp.split(h @ w_in, 3, axis=-1)
    q, k, v = split_heads(q, N_HEADS), split_heads(k, N_HEADS), split_heads(v, N_HEADS)
    nblk = s_len // SB_BLOCK
    q_blocks = q.reshape(b, N_HEADS, nblk, SB_BLOCK, HEAD_DIM).transpose(2, 0, 1, 3, 4)
    k_pos = jnp.arange(s_len)
    scale = HEAD_DIM ** -0.5

    def block(args):
        qb, bi = args
        q_pos = bi * SB_BLOCK + jnp.arange(SB_BLOCK)
        z = jnp.einsum('bhqd,bhkd->bhqk', qb, k).astype(jnp.float32) * scale
        past = k_pos[None, :] < q_pos[:, None]
        log_beta = jax.nn.log_sigmoid(z)
        log_keep = jnp.where(past, jax.nn.log_sigmoid(-z), 0.0)
        later = lax.cumsum(log_keep, axis=3, reverse=True) - log_keep
        a = jnp.where(past, jnp.exp(log_beta + later), 0.0)
        return jnp.einsum('bhqk,bhkd->bhqd', a.astype(v.dtype), v)

    o = lax.map(block, (q_blocks, jnp.arange(nblk)))
    o = o.transpose(1, 2, 0, 3, 4).reshape(b, N_HEADS, s_len, HEAD_DIM)
    return merge_heads(o) @ w_out

def moba_attention(h, w_in, qk_gain, w_out, cos, sin):
    b, s_len, _ = h.shape
    q, k, v = jnp.split(h @ w_in, 3, axis=-1)
    q, k, v = split_heads(q, N_HEADS), split_heads(k, N_HEADS), split_heads(v, N_HEADS)
    q = apply_rope(rms_norm_2(q, qk_gain[0]), cos, sin)
    k = apply_rope(rms_norm_2(k, qk_gain[1]), cos, sin)
    pad = (-s_len) % MOBA_BLOCK
    padw = ((0, 0), (0, 0), (0, pad), (0, 0))
    q, k, v = jnp.pad(q, padw), jnp.pad(k, padw), jnp.pad(v, padw)
    s_pad = s_len + pad
    nb = s_pad // MOBA_BLOCK
    topk = min(MOBA_TOPK, nb)
    k_blk = k.reshape(b, N_HEADS, nb, MOBA_BLOCK, HEAD_DIM)
    v_blk = v.reshape(b, N_HEADS, nb, MOBA_BLOCK, HEAD_DIM)
    k_mean = jnp.mean(k_blk.astype(jnp.float32), axis=3).astype(k.dtype)
    n_chunks = s_pad // MOBA_QCHUNK
    q_chunks = q.reshape(b, N_HEADS, n_chunks, MOBA_QCHUNK, HEAD_DIM).transpose(2, 0, 1, 3, 4)
    b_idx = jnp.arange(b)[:, None, None, None]
    h_idx = jnp.arange(N_HEADS)[None, :, None, None]
    blk_ids = jnp.arange(nb)
    in_blk = jnp.arange(MOBA_BLOCK)
    scale = HEAD_DIM ** -0.5

    def chunk(args):
        qc, ci = args
        q_pos = ci * MOBA_QCHUNK + jnp.arange(MOBA_QCHUNK)
        own = (ci * MOBA_QCHUNK) // MOBA_BLOCK
        gate = jnp.einsum('bhqd,bhnd->bhqn', qc, k_mean).astype(jnp.float32)
        gate = jnp.where(blk_ids < own, gate, -jnp.inf)
        top_val, top_idx = lax.top_k(gate, topk)
        sel_ok = jnp.isfinite(top_val)
        kg = k_blk[b_idx, h_idx, top_idx]
        vg = v_blk[b_idx, h_idx, top_idx]
        s_sel = jnp.einsum('bhqd,bhqnkd->bhqnk', qc, kg).astype(jnp.float32) * scale
        s_sel = jnp.where(sel_ok[..., None], s_sel, -jnp.inf)
        k_own = lax.dynamic_slice_in_dim(k, own * MOBA_BLOCK, MOBA_BLOCK, axis=2)
        v_own = lax.dynamic_slice_in_dim(v, own * MOBA_BLOCK, MOBA_BLOCK, axis=2)
        s_own = jnp.einsum('bhqd,bhkd->bhqk', qc, k_own).astype(jnp.float32) * scale
        own_pos = own * MOBA_BLOCK + in_blk
        s_own = jnp.where(own_pos[None, :] <= q_pos[:, None], s_own, -jnp.inf)
        qn = qc.shape[2]
        logits = jnp.concatenate([s_sel.reshape(b, N_HEADS, qn, topk * MOBA_BLOCK), s_own], axis=-1)
        p = jax.nn.softmax(logits, axis=-1).astype(v.dtype)
        p_sel = p[..., :topk * MOBA_BLOCK].reshape(b, N_HEADS, qn, topk, MOBA_BLOCK)
        p_own = p[..., topk * MOBA_BLOCK:]
        return (jnp.einsum('bhqnk,bhqnkd->bhqd', p_sel, vg)
                + jnp.einsum('bhqk,bhkd->bhqd', p_own, v_own))

    o = lax.map(chunk, (q_chunks, jnp.arange(n_chunks)))
    o = o.transpose(1, 2, 0, 3, 4).reshape(b, N_HEADS, s_pad, HEAD_DIM)[:, :, :s_len]
    return merge_heads(o) @ w_out

def swa_sink_attention(h, w_in, qk_gain, sinks, w_out, cos, sin):
    b, s_len, _ = h.shape
    qd, kvd = N_HEADS * HEAD_DIM, SWA_KV_HEADS * HEAD_DIM
    q, k, v = jnp.split(h @ w_in, [qd, qd + kvd], axis=-1)
    q, k, v = split_heads(q, N_HEADS), split_heads(k, SWA_KV_HEADS), split_heads(v, SWA_KV_HEADS)
    q = apply_rope(rms_norm_2(q, qk_gain[0]), cos, sin)
    k = apply_rope(rms_norm_2(k, qk_gain[1]), cos, sin)
    w = SWA_WINDOW
    nb = s_len // w
    g = N_HEADS // SWA_KV_HEADS
    qb = q.reshape(b, SWA_KV_HEADS, g, nb, w, HEAD_DIM)

    def band(t):
        tb = t.reshape(b, SWA_KV_HEADS, nb, w, HEAD_DIM)
        prev = jnp.pad(tb, ((0, 0), (0, 0), (1, 0), (0, 0), (0, 0)))[:, :, :-1]
        return jnp.concatenate([prev, tb], axis=3)

    kb, vb = band(k), band(v)
    s = jnp.einsum('bkgnqd,bknsd->bkgnqs', qb, kb).astype(jnp.float32) * (HEAD_DIM ** -0.5)
    q_off = jnp.arange(w)[:, None] + w
    k_off = jnp.arange(2 * w)[None, :]
    rel = q_off - k_off
    in_win = (rel >= 0) & (rel < SWA_WINDOW)
    valid = in_win[None] & ((jnp.arange(nb)[:, None, None] > 0) | (k_off >= w)[None])
    s = jnp.where(valid, s, -jnp.inf)
    sink = sinks.astype(jnp.float32).reshape(SWA_KV_HEADS, g)[None, :, :, None, None, None]
    m = jnp.maximum(jnp.max(s, axis=-1, keepdims=True), sink)
    e = jnp.exp(s - m)
    p = e / (jnp.sum(e, axis=-1, keepdims=True) + jnp.exp(sink - m))
    o = jnp.einsum('bkgnqs,bknsd->bkgnqd', p.astype(v.dtype), vb)
    o = o.reshape(b, N_HEADS, s_len, HEAD_DIM)
    return merge_heads(o) @ w_out

def swiglu(h, w_gate, w_up, w_down):
    return (jax.nn.silu(h @ w_gate) * (h @ w_up)) @ w_down

def second_inputs(seed: int = 0) -> dict:
    key = jax.random.key(seed)
    ks = jax.random.split(key, 20)
    d = D_MODEL
    hd = N_HEADS * HEAD_DIM
    n_sb, n_moba, n_swa = (DEPTH_2 + 2) // 3, (DEPTH_2 + 1) // 3, DEPTH_2 // 3

    def nrm(k, shape, scale):
        return jax.random.normal(k, shape, jnp.float32) * scale

    return {
        "x": nrm(ks[0], (BATCH, SEQ, d), 1.0),
        "c": nrm(ks[1], (BATCH, d), 1.0),
        "ada_w": nrm(ks[2], (DEPTH_2, d, 6 * d), 0.5 * d ** -0.5),
        "ada_b": nrm(ks[3], (DEPTH_2, 6 * d), 0.02),
        "norm_gain": 1.0 + nrm(ks[4], (DEPTH_2, 2, d), 0.02),
        "ffn_w_gate": nrm(ks[5], (DEPTH_2, d, D_FF), d ** -0.5),
        "ffn_w_up": nrm(ks[6], (DEPTH_2, d, D_FF), d ** -0.5),
        "ffn_w_down": nrm(ks[7], (DEPTH_2, D_FF, d), D_FF ** -0.5),
        "sb_w_in": nrm(ks[8], (n_sb, d, 3 * hd), d ** -0.5),
        "sb_w_out": nrm(ks[9], (n_sb, hd, d), hd ** -0.5),
        "moba_w_in": nrm(ks[10], (n_moba, d, 3 * hd), d ** -0.5),
        "moba_qk_gain": 1.0 + nrm(ks[11], (n_moba, 2, HEAD_DIM), 0.02),
        "moba_w_out": nrm(ks[12], (n_moba, hd, d), hd ** -0.5),
        "swa_w_in": nrm(ks[13], (n_swa, d, (N_HEADS + 2 * SWA_KV_HEADS) * HEAD_DIM), d ** -0.5),
        "swa_qk_gain": 1.0 + nrm(ks[14], (n_swa, 2, HEAD_DIM), 0.02),
        "swa_sinks": nrm(ks[15], (n_swa, N_HEADS), 0.5),
        "swa_w_out": nrm(ks[16], (n_swa, hd, d), hd ** -0.5),
    }

def second_block(x, c, ada_w, ada_b, norm_gain, ffn_w_gate, ffn_w_up, ffn_w_down,
              sb_w_in, sb_w_out, moba_w_in, moba_qk_gain, moba_w_out,
              swa_w_in, swa_qk_gain, swa_sinks, swa_w_out):
    s_len = x.shape[1]
    cos, sin = rope_tables(s_len)
    c_act = jax.nn.silu(c)
    for i in range(DEPTH_2):
        mod = c_act @ ada_w[i] + ada_b[i]
        sh1, sc1, g1, sh2, sc2, g2 = [m[:, None, :] for m in jnp.split(mod, 6, axis=-1)]
        h = modulate(rms_norm_2(x, norm_gain[i, 0]), sh1, sc1)
        kind, j = i % N_MIXERS, i // N_MIXERS
        if kind == 0:
            y = stick_breaking_attention(h, sb_w_in[j], sb_w_out[j])
        elif kind == 1:
            y = moba_attention(h, moba_w_in[j], moba_qk_gain[j], moba_w_out[j], cos, sin)
        else:
            y = swa_sink_attention(h, swa_w_in[j], swa_qk_gain[j], swa_sinks[j], swa_w_out[j], cos, sin)
        x = x + g1 * y
        h = modulate(rms_norm_2(x, norm_gain[i, 1]), sh2, sc2)
        x = x + g2 * swiglu(h, ffn_w_gate[i], ffn_w_up[i], ffn_w_down[i])
    return x


def setup_inputs(seed=0):
    out = dict(first_inputs(seed))
    for name, value in second_inputs(seed + 1).items():
        if name != "x":
            out[name + "_2"] = value
    return out


def reference(
    x, c, ctx, c_ctx, w_ada, b_ada, norm1, norm2, w_in, w_fourier, w_conv, rpb, w_out, w_rg,
    b_rg, w_re, b_re, w_gate, w_up, w_down, norm_final, c_2, ada_w_2, ada_b_2, norm_gain_2,
    ffn_w_gate_2, ffn_w_up_2, ffn_w_down_2, sb_w_in_2, sb_w_out_2, moba_w_in_2, moba_qk_gain_2,
    moba_w_out_2, swa_w_in_2, swa_qk_gain_2, swa_sinks_2, swa_w_out_2,
):
    x = first_block(
        x, c, ctx, c_ctx, w_ada, b_ada, norm1, norm2, w_in, w_fourier, w_conv, rpb, w_out, w_rg,
        b_rg, w_re, b_re, w_gate, w_up, w_down, norm_final,
    )
    return second_block(
        x, c_2, ada_w_2, ada_b_2, norm_gain_2, ffn_w_gate_2, ffn_w_up_2, ffn_w_down_2,
        sb_w_in_2, sb_w_out_2, moba_w_in_2, moba_qk_gain_2, moba_w_out_2, swa_w_in_2,
        swa_qk_gain_2, swa_sinks_2, swa_w_out_2,
    )


_drawn_inputs = setup_inputs


def setup_inputs(seed=0):
    import zlib

    import numpy as np

    out = dict(_drawn_inputs(seed))
    spreads = {}
    factors = {'norm2': 2.68,
     'rpb': 8.0,
     'b_rg': 8.0,
     'b_re': 5.396,
     'norm_gain_2': 4.065,
     'moba_qk_gain_2': 8.0,
     'swa_qk_gain_2': 8.0,
     'swa_sinks_2': 200.0}
    for name, (base, spread) in spreads.items():
        noise = np.random.default_rng([zlib.crc32(name.encode()), seed]).standard_normal(out[name].shape)
        drawn = base * np.exp(spread * noise) if base else spread * noise
        out[name] = __import__('jax').numpy.asarray(drawn.astype(out[name].dtype))
    for name, factor in factors.items():
        out[name] = (out[name] * factor).astype(out[name].dtype)
    return out
```

```python
from contextlib import ExitStack

import numpy as np
import concourse.bass as bass
from concourse import mybir

F32 = mybir.dt.float32
ALU = mybir.AluOpType
ACT = mybir.ActivationFunctionType
AX = mybir.AxisListType

P = 128
D = 1024
KT = D // P
T = 256
TT = T // P
HD = 64
SCALE = HD ** -0.5
EPS = 1e-6
NEG = -1e30
GRID_W, NA_KW, NA_KH = 64, 16, 8
NA_HEADS = 8
NA_PAIRS = NA_HEADS // 2
PAIRS = D // (2 * HD)
G, EG = 4, 8
E = G * EG
FE = 512
FT_E = FE // P
DFF = 2816
FT = DFF // P
GU = FT // 2
MODS = 6 * KT
RING = 3
SLOT = 4096
TRI = 3 * P
LAYERS = 4
R_EXP1, R_EXP2 = 8, 25
KINDS = ("sb", "moba", "swa", "sb")

CONST = {}
_at = 0
for _name, _n in (("ident", P), ("ones", P), ("headones", P), ("rot", P), ("suffix", P), ("cos", T), ("sin", T),
                  ("mask_sb", TRI), ("mask_moba", TRI), ("mask_swa", TRI), ("mask_na", T),
                  ("dft", TT * 2 * T), ("cd", P), ("sd", P), ("iota", E), ("eps", 1), ("zero", 1)):
    CONST[_name] = (_at, _at + _n)
    _at += _n
N_CONST = _at

VEC = {}
_at = 0
for _name, _n in (("c", KT * 2), ("c2", KT), ("norm1", KT), ("norm2", KT), ("normf", KT), ("w_conv", 2 * 3),
                  ("b_ada", MODS), ("gains2", LAYERS * 2 * KT), ("b_ada2", LAYERS * MODS), ("qk_moba", 2),
                  ("qk_swa", 2), ("sinks", 8 * PAIRS), ("b_route", G + E)):
    VEC[_name] = (_at, _at + _n)
    _at += _n
N_VEC = _at

N_HEAD = 4
PHASES = (
    [("ada_head", N_HEAD, SLOT), ("mix", 2, SLOT), ("na", 3 * NA_PAIRS, SLOT), ("out_0", 2, SLOT), ("moe", 3 * E, SLOT)]
    + [ph for i in range(LAYERS) for ph in
       ((f"pair_{i}", PAIRS, 3 * KT * P), (f"out_{i + 1}", 2, SLOT), (f"gu_{i}", GU, SLOT), (f"down_{i}", KT, FT * P))]
)
FIRST = {}
_at = 0
for _name, _n, _ in PHASES:
    FIRST[_name] = _at
    _at += _n


def build(nc, ins, out, subs=2 + 2 * LAYERS):
    layers = [i for i in range(LAYERS) if 2 + 2 * i < subs]
    phases = PHASES[:[4, 5][min(subs, 2) - 1]] + PHASES[5:5 + 2 * max(0, subs - 2)]
    ctx = ExitStack()
    with ctx:
        def sb(name, shape):
            return ctx.enter_context(nc.sbuf_tensor(name, shape, F32))

        def sem(name):
            return ctx.enter_context(nc.semaphore(name))

        const = sb("const_sb", [P, N_CONST])
        vec = sb("vec_sb", [P, N_VEC])
        ring = [sb(f"ring{s}", [P, SLOT]) for s in range(RING)]
        ada_ring = [sb(f"ada_ring{s}", [P, SLOT]) for s in range(2)]
        ada_sum = sb("ada_sum", [P, MODS * P])
        xT = sb("xT", [P, KT, T])
        xsq = sb("xsq", [P, KT, T])
        xn = sb("xn", [P, KT, T])
        hT = sb("hT", [P, KT, T])
        rinv = sb("rinv", [P, T])
        mixT = sb("mixT", [P, KT, T])
        work = sb("work", [P, 3, 4 * 2 * T])
        gact = [sb(f"gact{s}", [P, 2, T]) for s in range(RING)]
        mod = sb("mod", [P, MODS])
        modc = sb("modc", [P, 2 * KT])
        gain = sb("gain", [P, 3, KT])
        csilu = sb("csilu", [P, 2 * KT])
        c2silu = sb("c2silu", [P, KT])
        qk = sb("qk", [P, 2 * T])
        qn = sb("qn", [P, 2 * T])
        qr = sb("qr", [P, 2 * T])
        vv = sb("vv", [P, 4, P])
        stat = sb("stat", [P, 8, 4])
        wf = sb("wf", [P, 2, T])
        wr = sb("wr", [P, KT, G + E])
        logit = sb("logit", [P, TT, G + E])
        small = sb("small", [P, 16, TT])
        comb = sb("comb", [P, TT, E])
        combT = sb("combT", [E, T])
        comb_e = sb("comb_e", [E, T])
        bank = [ctx.enter_context(nc.psum_tensor(f"bank{i}", [P, 512], F32)) for i in range(8)]

        soft = work[:, 0, :].rearrange("p (c n) -> p c n", c=4)
        prob = work[:, 1, :].rearrange("p (c n) -> p c n", c=4)
        probT = work[:, 2, :].rearrange("p (h n) -> p h n", h=2)
        hid = work[:, :, :].rearrange("p a b -> p (a b)")[:, 0:FT * T].rearrange("p (f t) -> p f t", f=FT)
        rt = work[:, 0, 0:12 * TT * E].rearrange("p (i t e) -> p i t e", i=12, t=TT)
        lnms = xn[:, KT - 1, :]
        hcT = ada_sum[:, 0:KT * T].rearrange("p (k t) -> p k t", k=KT)
        ctxT = ada_sum[:, KT * T:2 * KT * T].rearrange("p (k t) -> p k t", k=KT)
        b16 = ada_ring[0][:, :].rearrange("p (c n) -> p c n", n=T)
        bias = b16.rearrange("p (q h) n -> p q h n", q=TT)

        def cst(name, lo=0, n=None):
            a, b = CONST[name]
            return const[:, a + lo:(a + lo + n) if n else b]

        def vc(name, lo=0, n=None):
            a, b = VEC[name]
            return vec[:, a + lo:(a + lo + n) if n else b]

        landed = [sem(f"landed{s}") for s in range(RING)]
        used = [sem(f"used{s}") for s in range(RING)]
        loaded, x_loaded, side_loaded = sem("loaded"), sem("x_loaded"), sem("side_loaded")
        ada_landed = [sem(f"ada_landed{s}") for s in range(2)]
        ada_prod, ada_half, ada_quarter, ada_summed = (sem(n) for n in ("ada_prod", "ada_half", "ada_quarter", "ada_summed"))
        silu_done, mods_done, mods_step, mods_ready = (sem(n) for n in ("silu_done", "mods_done", "mods_step", "mods_ready"))
        sq_ready, ssq_done, ln_ms, rinv_ready, xn_ready, h_ready = (
            sem(n) for n in ("sq_ready", "ssq_done", "ln_ms", "rinv_ready", "xn_ready", "h_ready"))
        y_done, x_done = sem("y_done"), sem("x_done")
        bias_masked = sem("bias_masked")
        mix_proj, mix_act, mix_dve, dft_pe, dft_act = (sem(n) for n in ("mix_proj", "mix_act", "mix_dve", "dft_pe", "dft_act"))
        na = {n: sem("na_" + n) for n in (
            "qk_proj", "qk_ready", "v_ready", "scores", "s_ready", "mx", "m_ready", "e_ready", "rs", "p_ready",
            "t_done", "pt_act", "pt_dve", "o_done", "o_ready", "ada_done", "ada_ready")}
        sk = {n: sem("sb_" + n) for n in (
            "qk_proj", "qk_ready", "v_ready", "scores", "zm_ready", "abs", "exp", "ln", "sp_ready", "suffix",
            "w_ready", "a_ready", "o_done", "o_ready")}
        sf = {n: sem("sf_" + n) for n in (
            "qk_proj", "raw", "ssum", "ln", "rinv", "qn_ready", "rope", "rot", "qr_ready", "v_ready", "scores",
            "s_ready", "mx", "m_ready", "sink_in", "sink_e", "e_ready", "den", "rs", "p_ready", "t_done", "pt_act", "pt_dve",
            "o_done", "o_ready")}
        route_done, route_act, route_step, comb_done, comb_ready = (
            sem(n) for n in ("route_done", "route_act", "route_step", "comb_done", "comb_ready"))
        comb_sel, comb_bc, moe_gu, moe_silu, moe_mul, moe_hid = (
            sem(n) for n in ("comb_sel", "comb_bc", "moe_gu", "moe_silu", "moe_mul", "moe_hid"))
        zeroed = sem("zeroed")
        ffn_silu, ffn_hid = sem("ffn_silu"), sem("ffn_hid")
        stored = sem("stored")

        block = ctx.enter_context(nc.Block())

        def slot(n):
            return ring[n % RING]

        def wait_chunk(eng, n, r=0):
            eng.wait_ge(landed[n % RING], 16 * (n // RING + 1) + 16 * r)

        def wait_used(eng, n, r=0):
            eng.wait_ge(used[n % RING], n // RING + 1 + r)

        def steps(eng, lo, hi, body):
            rounds = (hi - lo) // RING
            if rounds >= 2:
                with eng.Fori(0, rounds) as r:
                    for s in range(RING):
                        body(lo + s, r)
            else:
                rounds = 0
            for step in range(lo + RING * rounds, hi):
                body(step, 0)

        def norm_bank(e):
            return bank[4 if e == 2 or e > 4 and e % 2 else 3]

        def epoch(layer):
            kind = KINDS[layer] == "sb"
            return PAIRS * sum((KINDS[i] == "sb") == kind for i in range(layer))

        @block.sync
        def _(sp):
            sp.dma_start(vec[:, :], ins["vec"]).then_inc(loaded, 16)
            sp.dma_start(const[:, :], ins["const"]).then_inc(loaded, 16)
            sp.dma_start(ctxT, ins["ctxT"]).then_inc(x_loaded, 16)
            sp.dma_start(xT[:, :, :], ins["xT"]).then_inc(x_loaded, 16)
            for name, count, width in phases:
                n0 = FIRST[name]

                def load(step, r):
                    if n0 + step >= RING:
                        wait_used(sp, n0 + step - RING, r)
                    sp.dma_start(slot(n0 + step)[:, 0:width], ins[name][step + RING * r]).then_inc(landed[(n0 + step) % RING], 16)

                if n0 < RING:
                    for step in range(count):
                        load(step, 0)
                else:
                    steps(sp, 0, count, load)
            sp.wait_ge(x_done, KT * subs)
            if subs == 2:
                sp.wait_ge(h_ready, KT * 4)
            sp.dma_start(out, xT[:, :, :]).then_inc(stored, 16)
            sp.wait_ge(stored, 16)

        @block.gpsimd
        def _(pool):
            pool.dma_start(wf[:, :, :], ins["wf"]).then_inc(side_loaded, 16)
            pool.dma_start(wr[:, :, :], ins["wr"]).then_inc(side_loaded, 16)
            pool.dma_start(bias, ins["bias"]).then_inc(side_loaded, 16)
            pool.wait_ge(side_loaded, 48)
            pool.wait_ge(loaded, 32)
            nc.gpsimd.tensor_tensor(b16, b16, cst("mask_na").unsqueeze(1).broadcast_to([P, TT * NA_HEADS, T]),
                                    ALU.add).then_inc(bias_masked, 1)
            if not layers:
                return
            pool.wait_ge(silu_done, 2)
            chunks = MODS * P // 512
            wait_used(pool, FIRST["out_0"] - RING)
            pool.wait_ge(na["p_ready"], NA_PAIRS)
            for s in range(2):
                pool.dma_start(ada_ring[s][:, :], ins["ada2"][s]).then_inc(ada_landed[s], 16)

            def chunk(c, r, s, more):
                w3 = ada_ring[s][:, :].rearrange("p (k n) -> p k n", k=KT)
                pool.wait_ge(ada_landed[s], 16 * (c // 2 + 1) + 16 * r)
                nc.gpsimd.tensor_tensor(w3, w3, c2silu[:, :].unsqueeze(2).broadcast_to([P, KT, 512]),
                                        ALU.mult).then_inc(ada_prod, 1)
                pool.wait_ge(ada_prod, c + 1 + 2 * r)
                nc.gpsimd.tensor_tensor(w3[:, 0:4, :], w3[:, 0:4, :], w3[:, 4:8, :], ALU.add).then_inc(ada_half, 1)
                pool.wait_ge(ada_half, c + 1 + 2 * r)
                nc.gpsimd.tensor_tensor(w3[:, 0:2, :], w3[:, 0:2, :], w3[:, 2:4, :], ALU.add).then_inc(ada_quarter, 1)
                pool.wait_ge(ada_quarter, c + 1 + 2 * r)
                col = 512 * (c % chunks) + 1024 * r
                nc.gpsimd.tensor_tensor(ada_sum[:, bass.ds(col, 512)], w3[:, 0, :], w3[:, 1, :],
                                        ALU.add).then_inc(ada_summed, 1)
                if more:
                    pool.wait_ge(ada_summed, c + 1 + 2 * r)
                    pool.dma_start(ada_ring[s][:, :], ins["ada2"][c + 2 + 2 * r]).then_inc(ada_landed[s], 16)

            for i in layers:
                if i > 0:
                    pool.wait_ge(mods_done, i)
                with pool.Fori(0, chunks // 2 - 1) as r:
                    for s in range(2):
                        chunk(chunks * i + s, r, s, True)
                for s in range(2):
                    chunk(chunks * (i + 1) - 2 + s, 0, s, i != layers[-1])

        @block.tensor
        def _(pe):
            mm = nc.tensor.matmul

            def norm(e):
                b = norm_bank(e)
                for k in range(KT):
                    pe.wait_ge(sq_ready, KT * e + k + 1)
                    m = mm(b[:, 0:T], cst("ones"), xsq[:, k, :], start=k == 0, stop=k == KT - 1)
                m.then_inc(ssq_done, 1)

            def project(dst, w, lo, h):
                for k in range(KT):
                    m = mm(dst, w[:, k, lo:lo + P], h[:, k, :], start=k == 0, stop=k == KT - 1)
                return m

            def rows(dst, w, lo, n, h):
                for t in range(TT):
                    for k in range(KT):
                        m = mm(dst[:, t, :], h[:, k, t * P:(t + 1) * P], w[:, k, lo:lo + n], start=k == 0, stop=k == KT - 1)
                return m

            def chunk3(n, cols):
                return slot(n)[:, 0:KT * cols].rearrange("p (k n) -> p k n", k=KT)

            def out_proj(name):
                for c in range(2):
                    n = FIRST[name] + c
                    wait_chunk(pe, n)
                    w = chunk3(n, 512)
                    for f in range(4):
                        project(bank[(4 + 4 * c + f) % 8][:, 0:T], w, f * P, mixT).then_inc(y_done if f < 3 else used[n % RING], 1)

            def values(o, h, tiles, cols):
                for i, kt in enumerate(tiles):
                    (a, b), (c, d) = cols(kt)
                    m = mm(o[64 * h:64 * h + 64, a:b], vv[:, kt, 64 * h:64 * h + 64], probT[:, h, c:d],
                           start=i == 0, stop=i == len(tiles) - 1, skip_group_check=True)
                return m

            def tri(kt):
                return ((0, T), (0, T)) if kt == 0 else ((P, T), (T, TRI))

            pe.wait_ge(loaded, 32)
            pe.wait_ge(silu_done, 1)
            cc = csilu[:, :].rearrange("p (k c) -> p k c", c=2)

            def ada(n, dst, r=0):
                wait_chunk(pe, n, r)
                w = chunk3(n, 512)
                for f in range(4):
                    for k in range(KT):
                        m = mm(dst[:, 2 * f:2 * f + 2], w[:, k, f * P:(f + 1) * P], cc[:, k, :], start=k == 0, stop=k == KT - 1)
                return m

            for n in range(N_HEAD):
                m = ada(n, bank[2][:, 8 * n:8 * n + 8])
                m.then_inc(used[n % RING], 1)
            norm(0)
            pe.wait_ge(ln_ms, 1)
            norm(1)

            n = FIRST["mix"]
            pe.wait_ge(h_ready, 2 * KT)
            wait_chunk(pe, n)
            rows(bank[0][:, :].rearrange("p (t n) -> p t n", t=TT), chunk3(n, 512), 0, T, hT).then_inc(mix_proj, 1)
            project(bank[1][:, 0:T], chunk3(n, 512), 256, hT)
            project(bank[1][:, T:2 * T], chunk3(n, 512), 384, hT).then_inc(used[n % RING], 1)
            n += 1
            wait_chunk(pe, n)
            pe.wait_ge(mods_ready, 1)
            project(bank[2][:, 0:T], chunk3(n, 512), 0, hT)
            project(bank[2][:, T:2 * T], chunk3(n, 512), 128, hT).then_inc(mix_proj, 1)
            pe.wait_ge(rinv_ready, 2)
            project(bank[3][:, 0:T], chunk3(n, 512), 256, hT)
            project(bank[3][:, T:2 * T], chunk3(n, 512), 384, hT).then_inc(used[n % RING], 1)
            pe.wait_ge(dft_act, 1)
            f3 = qr[:, :].rearrange("p (t n) -> p t n", t=TT)
            for c in range(2):
                for t in range(TT):
                    m = mm(bank[4 + c][:, :], f3[:, t, c * P:(c + 1) * P], cst("dft", t * 2 * T, 2 * T), start=t == 0, stop=t == TT - 1)
            m.then_inc(dft_pe, 1)
            pe.wait_ge(dft_act, 2)
            for c in range(2):
                mm(bank[6 + c][:, 0:T], cst("cd"), soft[:, c, 0:T], start=True, stop=False)
                m = mm(bank[6 + c][:, 0:T], cst("sd"), soft[:, c, T:2 * T], start=False, stop=True)
            m.then_inc(dft_pe, 1)
            pe.wait_ge(dft_act, 3)
            pe.wait_ge(side_loaded, 48)
            for f in range(2):
                for k in range(2):
                    m = mm(bank[4 + f][:, 0:T], wf[:, k, f * P:(f + 1) * P], prob[:, k, 0:T], start=k == 0, stop=k == 1)
            m.then_inc(dft_pe, 1)

            pe.wait_ge(dft_act, 4)
            pe.wait_ge(mix_dve, 1)
            n0 = FIRST["na"]

            def na_pair(j, first, last):
                s = slot(n0)
                r = j
                if not last:
                    wait_chunk(pe, n0, r)
                    w = chunk3(n0, 3 * P)
                    project(bank[0][:, 0:T], w, 0, hT)
                    project(bank[0][:, T:2 * T], w, P, hT)
                    if not first:
                        pe.wait_ge(na["ada_ready"], j)
                    project(bank[2][:, 0:T], w, P, hcT).then_inc(na["qk_proj"], 1)
                    if not first:
                        pe.wait_ge(na["v_ready"], j)
                    v4 = bank[1][:, :].rearrange("p (t n) -> p t n", t=4)
                    rows(v4[:, 0:2, :], w, 2 * P, P, hT)
                    rows(v4[:, 2:4, :], w, 2 * P, P, hcT).then_inc(used[n0 % RING], 1)
                if not first:
                    pe.wait_ge(na["p_ready"], j)
                    for c in range(4):
                        for kt in range(4):
                            m = nc.tensor.transpose(bank[4 + c][:, kt * P:(kt + 1) * P], prob[:, c, kt * P:(kt + 1) * P], cst("ident"))
                    m.then_inc(na["t_done"], 1)
                if not last:
                    pe.wait_ge(na["qk_ready"], j + 1)
                    ada(n0 + 1, bank[2][:, 0:8], r).then_inc(used[(n0 + 1) % RING], 1)
                    ada(n0 + 2, bank[2][:, 8:16], r).then_inc(used[(n0 + 2) % RING], 1)
                if not first:
                    pe.wait_ge(na["pt_act"], j)
                    pe.wait_ge(na["pt_dve"], j)
                    pe.wait_ge(na["v_ready"], j)
                    for h in range(2):
                        m = values(bank[3], h, range(4), lambda kt: ((0, T), (kt * T, (kt + 1) * T)))
                    m.then_inc(na["o_done"], 1)
                if not last:
                    kc = qn[:, 0:T]
                    for h in range(2):
                        hp = slice(64 * h, 64 * h + 64)
                        for q in range(TT):
                            b = bank[4 + 2 * h + q]
                            mm(b[:, 0:T], qk[hp, q * P:(q + 1) * P], qk[hp, T:2 * T], start=True, stop=True)
                            m = mm(b[:, T:2 * T], qk[hp, q * P:(q + 1) * P], kc[hp, :], start=True, stop=True)
                    m.then_inc(na["scores"], 1)

            na_pair(0, True, False)
            with pe.Fori(1, NA_PAIRS) as j:
                na_pair(j, False, False)
            na_pair(NA_PAIRS, False, True)
            pe.wait_ge(na["o_ready"], NA_PAIRS)
            out_proj("out_0")

            if subs > 1:
                norm(2)
                pe.wait_ge(h_ready, KT * 3)
                rows(bank[0][:, 0:TT * (G + E)].rearrange("p (t n) -> p t n", t=TT), wr, 0, G + E, hT).then_inc(route_done, 1)
                pe.wait_ge(comb_done, 1)
                for t in range(TT):
                    m = nc.tensor.transpose(bank[1][0:E, t * P:(t + 1) * P], comb[:, t, :], cst("ident"))
                m.then_inc(route_done, 1)
                pe.wait_ge(zeroed, 1)
                pe.wait_ge(comb_ready, 1)
                for b in range(4, 8):
                    mm(bank[b][:, :], cst("ones"), qr[:, :], start=True, stop=False, skip_group_check=True)
                n0 = FIRST["moe"]
                with pe.Fori(0, E) as e:
                    pe.wait_ge(comb_sel, e + 1)
                    mm(bank[3][:, 0:T], cst("ones")[0:E, :], comb_e[:, :], start=True, stop=True).then_inc(comb_bc, 1)
                    wait_chunk(pe, n0, e)
                    wait_chunk(pe, n0 + 1, e)
                    for f in range(FT_E):
                        if f == 3:
                            pe.wait_ge(moe_hid, 4 * e + 1)
                        m = project(bank[f % 3][:, 0:T], chunk3(n0, 512), f * P, hT)
                        if f == 3:
                            m.then_inc(used[n0 % RING], 1)
                        m = project(bank[f % 3][:, T:2 * T], chunk3(n0 + 1, 512), f * P, hT)
                        m.then_inc(moe_gu if f < 3 else used[(n0 + 1) % RING], 1)
                    wait_chunk(pe, n0 + 2, e)
                    w = slot(n0 + 2)[:, :].rearrange("p (k n) -> p k n", k=FT_E)
                    for k in range(FT_E):
                        pe.wait_ge(moe_hid, 4 * e + k + 1)
                        for d in range(KT):
                            m = mm(bank[4 + d // 2][:, (d % 2) * T:(d % 2 + 1) * T], w[:, k, d * P:(d + 1) * P], hid[:, k, :],
                                   start=False, stop=False, skip_group_check=True)
                    m.then_inc(used[(n0 + 2) % RING], 1)
                norm(3)

            for i in layers:
                pe.wait_ge(ada_summed, 12 * (i + 1))
                if i == 0:
                    pe.wait_ge(h_ready, KT * 4)
                for m48 in range(MODS):
                    m = mm(bank[2][:, m48:m48 + 1], ada_sum[:, m48 * P:(m48 + 1) * P], cst("ones", 0, 1), start=True, stop=True)
                m.then_inc(mods_done, 1)
                norm(4 + 2 * i)
                pe.wait_ge(h_ready, KT * (5 + 2 * i))
                n0 = FIRST[f"pair_{i}"]
                base = epoch(i)

                def sb_pair(step, r, first=False, last=False):
                    j = step + RING * r + base
                    n = n0 + step
                    if not last:
                        wait_chunk(pe, n, r)
                        w = chunk3(n, 3 * P)
                        project(bank[0][:, 0:T], w, 0, hT)
                        project(bank[0][:, T:2 * T], w, P, hT).then_inc(sk["qk_proj"], 1)
                    if not first:
                        pe.wait_ge(sk["sp_ready"], j)
                        for h in range(2):
                            sp_ = soft[:, 2 + h, :]
                            mm(bank[6 + h][:, 0:T], cst("suffix"), sp_[:, 0:T], start=True, stop=False, skip_group_check=True)
                            mm(bank[6 + h][:, P:T], cst("ones"), sp_[:, T:TRI], start=False, stop=True, skip_group_check=True)
                            m = mm(bank[6 + h][:, T:TRI], cst("suffix"), sp_[:, T:TRI], start=True, stop=True, skip_group_check=True)
                        m.then_inc(sk["suffix"], 1)
                    if not last:
                        pe.wait_ge(sk["v_ready"], j)
                        rows(bank[1][:, 0:T].rearrange("p (t n) -> p t n", t=TT), w, 2 * P, P, hT).then_inc(used[n % RING], 1)
                    if not first:
                        pe.wait_ge(sk["v_ready"], j)
                        pe.wait_ge(sk["a_ready"], j)
                        for h in range(2):
                            m = values(bank[3], h, range(TT), tri)
                        m.then_inc(sk["o_done"], 1)
                    if not last:
                        pe.wait_ge(sk["qk_ready"], j + 1)
                        for h in range(2):
                            hp = slice(64 * h, 64 * h + 64)
                            mm(bank[4 + h][:, 0:T], qk[hp, T:T + P], qk[hp, 0:T], start=True, stop=True)
                            m = mm(bank[4 + h][:, T:TRI], qk[hp, T + P:2 * T], qk[hp, P:T], start=True, stop=True)
                        m.then_inc(sk["scores"], 1)

                def sf_pair(step, r, first=False, last=False):
                    j = step + RING * r + base
                    n = n0 + step
                    if not last:
                        wait_chunk(pe, n, r)
                        w = chunk3(n, 3 * P)
                        project(bank[0][:, 0:T], w, 0, hT)
                        project(bank[0][:, T:2 * T], w, P, hT).then_inc(sf["qk_proj"], 1)
                        pe.wait_ge(sf["v_ready"], j)
                        rows(bank[1][:, 0:T].rearrange("p (t n) -> p t n", t=TT), w, 2 * P, P, hT).then_inc(used[n % RING], 1)
                        pe.wait_ge(sf["raw"], 2 * j + 2)
                        mm(bank[2][:, :], cst("headones"), xsq[:, 0:2, :], start=True, stop=True).then_inc(sf["ssum"], 1)
                    if not first:
                        pe.wait_ge(sf["p_ready"], j)
                        for h in range(2):
                            for c in range(3):
                                m = nc.tensor.transpose(bank[6 + h][:, c * P:(c + 1) * P], prob[:, h, c * P:(c + 1) * P], cst("ident"))
                        m.then_inc(sf["t_done"], 1)
                    if not last:
                        pe.wait_ge(sf["qn_ready"], 2 * j + 2)
                        mm(bank[2][:, :], cst("rot"), qn[:, :], start=True, stop=True).then_inc(sf["rot"], 1)
                    if not first:
                        pe.wait_ge(sf["v_ready"], j)
                        pe.wait_ge(sf["pt_act"], j)
                        pe.wait_ge(sf["pt_dve"], j)
                        for h in range(2):
                            m = values(bank[3], h, range(TT), tri)
                        m.then_inc(sf["o_done"], 1)
                    if not last:
                        pe.wait_ge(sf["qr_ready"], j + 1)
                        for h in range(2):
                            hp = slice(64 * h, 64 * h + 64)
                            mm(bank[4 + h][:, 0:P], qr[hp, 0:P], qr[hp, T:T + P], start=True, stop=True)
                            m = mm(bank[4 + h][:, P:TRI], qr[hp, P:T], qr[hp, T:2 * T], start=True, stop=True)
                        m.then_inc(sf["scores"], 1)

                pair = sb_pair if KINDS[i] == "sb" else sf_pair
                pair(0, 0, first=True)
                steps(pe, 1, PAIRS, pair)
                pair(PAIRS, 0, last=True)
                pe.wait_ge((sk if KINDS[i] == "sb" else sf)["o_ready"], base + PAIRS)
                out_proj(f"out_{i + 1}")
                if 3 + 2 * i >= subs:
                    break

                norm(5 + 2 * i)
                pe.wait_ge(h_ready, KT * (6 + 2 * i))
                n0 = FIRST[f"gu_{i}"]

                def gate_up(step, r):
                    n = n0 + step
                    s = step % RING
                    wait_chunk(pe, n, r)
                    if step >= RING:
                        pe.wait_ge(ffn_hid, GU * i + step - (RING - 1) + RING * r)
                    w = chunk3(n, 512)
                    for half in range(2):
                        for f in range(2):
                            m = project(bank[2 * s + half][:, f * T:(f + 1) * T], w, half * 2 * P + f * P, hT)
                    m.then_inc(used[n % RING], 1)

                for step in range(RING):
                    gate_up(step, 0)
                steps(pe, RING, GU, gate_up)
                n1 = FIRST[f"down_{i}"]
                pe.wait_ge(ffn_hid, GU * (i + 1))

                def down(step, r):
                    n = n1 + step
                    wait_chunk(pe, n, r)
                    if step >= RING - 1:
                        pe.wait_ge(x_done, KT * (3 + 2 * i) + step - (RING - 1) + RING * r)
                    w = slot(n)[:, 0:FT * P].rearrange("p (k n) -> p k n", k=FT)
                    b = bank[5 + step % RING]
                    for k in range(FT):
                        m = mm(b[:, 0:T], w[:, k, :], hid[:, k, :], start=k == 0, stop=k == FT - 1)
                    m.then_inc(used[n % RING], 1)

                for step in range(2):
                    down(step, 0)
                steps(pe, 2, KT, down)

        @block.scalar
        def _(act):
            A = nc.scalar.activation

            def copy(o, i):
                return nc.scalar.copy(o, i)

            def norm(e, src, ready, out_t, g, shift):
                for k in range(KT):
                    if ready:
                        act.wait_ge(ready[0], ready[1] + (k + 1) * ready[2])
                    A(xsq[:, k, :], src[:, k, :], ACT.Square).then_inc(sq_ready, 1)
                act.wait_ge(ssq_done, e + 1)
                A(lnms, norm_bank(e)[:, 0:T], ACT.Ln, scale=1.0 / D, bias=cst("eps")).then_inc(ln_ms, 1)
                act.wait_ge(ln_ms, e + 1)
                A(rinv[:, :], lnms, ACT.Exp, scale=-0.5).then_inc(rinv_ready, 1)
                for k in range(KT):
                    act.wait_ge(xn_ready, KT * e + k + 1)
                    A(out_t[:, k, :], xn[:, k, :], ACT.Identity, scale=g(k), bias=shift(k)).then_inc(h_ready, 1)

            act.wait_ge(loaded, 32)
            A(csilu[:, :], vc("c"), ACT.Silu).then_inc(silu_done, 1)
            A(c2silu[:, :], vc("c2"), ACT.Silu).then_inc(silu_done, 1)
            act.wait_ge(x_loaded, 32)

            def gcol(i):
                return lambda k: gain[:, i, k:k + 1]

            def scol(t, lo):
                return lambda k: t[:, lo + k:lo + k + 1]

            act.wait_ge(mods_ready, 1)
            norm(0, ctxT, None, hcT, gcol(1), scol(modc, 0))
            norm(1, xT, None, hT, gcol(0), scol(mod, 0))

            act.wait_ge(mix_proj, 1)
            copy(qr[:, :], bank[0][:, :]).then_inc(dft_act, 1)
            act.wait_ge(mix_proj, 2)
            copy(gact[0][:, :, :], bank[2][:, :].rearrange("p (t n) -> p t n", t=2)).then_inc(mix_act, 1)
            act.wait_ge(dft_pe, 1)
            copy(soft[:, 0, :], bank[4][:, :])
            copy(soft[:, 1, :], bank[5][:, :]).then_inc(dft_act, 1)
            act.wait_ge(dft_pe, 2)
            copy(prob[:, 0, 0:T], bank[6][:, 0:T])
            copy(prob[:, 1, 0:T], bank[7][:, 0:T]).then_inc(dft_act, 1)
            act.wait_ge(dft_pe, 3)
            copy(mixT[:, 0, :], bank[4][:, 0:T])
            copy(mixT[:, 1, :], bank[5][:, 0:T]).then_inc(dft_act, 1)

            def na_pair(j, first, last):
                if not first:
                    act.wait_ge(na["m_ready"], j)
                    for c in range(4):
                        m = A(prob[:, c, :], soft[:, c, :], ACT.Exp, bias=stat[:, 1, c:c + 1], accum_out=stat[:, 2, c:c + 1])
                    m.then_inc(na["e_ready"], 1)
                if not last:
                    act.wait_ge(na["qk_proj"], j + 1)
                    copy(qk[:, :], bank[0][:, :])
                    copy(qn[:, 0:T], bank[2][:, 0:T]).then_inc(na["qk_ready"], 1)
                if not first:
                    act.wait_ge(na["t_done"], j)
                    for q in range(2):
                        m = copy(probT[:, 0, :].rearrange("p (k q n) -> p k q n", k=4, q=2)[:, :, q, :],
                                 bank[4 + q][:, :].rearrange("p (k n) -> p k n", k=4))
                    m.then_inc(na["pt_act"], 1)
                    act.wait_ge(na["o_done"], j)
                    copy(mixT[:, 1 + j, :], bank[3][:, 0:T]).then_inc(na["o_ready"], 1)

            na_pair(0, True, False)
            with act.Fori(1, NA_PAIRS) as j:
                na_pair(j, False, False)
            na_pair(NA_PAIRS, False, True)

            if subs > 1:
                act.wait_ge(mods_ready, 2)
                norm(2, xT, (x_done, 0, 1), hT, gcol(2), scol(mod, 3 * KT))
                act.wait_ge(route_step, R_EXP1)
                A(rt[:, 4, :, 0:G], rt[:, 0, :, 0:G], ACT.Exp).then_inc(route_act, 1)
                act.wait_ge(route_step, R_EXP2)
                A(small[:, 8, :], small[:, 7, :], ACT.Exp).then_inc(route_act, 1)
                with act.Fori(0, E) as e:
                    for f in range(FT_E):
                        if f < 3:
                            act.wait_ge(moe_gu, 3 * e + f + 1)
                        else:
                            wait_used(act, FIRST["moe"] + 1, e)
                        A(gact[f % 3][:, 0, :], bank[f % 3][:, 0:T], ACT.Silu).then_inc(moe_silu, 1)
                norm(3, xT, (x_done, KT, 1), xT, lambda k: vc("normf", k, 1), lambda k: cst("zero"))

            for i in layers:
                if i == 0:
                    ready = (h_ready, KT * 3, 1)
                else:
                    ready = (x_done, KT * (1 + 2 * i), 1)
                act.wait_ge(mods_ready, 3 + i)
                norm(4 + 2 * i, xT, ready, hT, gcol(0), scol(mod, 0))
                base = epoch(i)

                def sb_pair(step, r, first=False, last=False):
                    j = step + RING * r + base
                    lne = prob[:, 0:2, 0:TRI]
                    if not first:
                        act.wait_ge(sk["zm_ready"], j)
                        A(lne, soft[:, 0:2, 0:TRI], ACT.Abs).then_inc(sk["abs"], 1)
                        act.wait_ge(sk["abs"], j)
                        A(lne, lne, ACT.Exp, scale=-1.0).then_inc(sk["exp"], 1)
                        act.wait_ge(sk["exp"], j)
                        A(lne, lne, ACT.Ln, bias=1.0).then_inc(sk["ln"], 1)
                    if not last:
                        act.wait_ge(sk["qk_proj"], j + 1)
                        copy(qk[:, :], bank[0][:, :]).then_inc(sk["qk_ready"], 1)
                    if not first:
                        act.wait_ge(sk["w_ready"], j)
                        A(probT[:, :, 0:TRI], prob[:, 2:4, 0:TRI], ACT.Exp).then_inc(sk["a_ready"], 1)
                        act.wait_ge(sk["o_done"], j)
                        copy(mixT[:, j - 1 - base, :], bank[3][:, 0:T]).then_inc(sk["o_ready"], 1)

                def sf_pair(step, r, first=False, last=False):
                    j = step + RING * r + base
                    if not first:
                        act.wait_ge(sf["m_ready"], j)
                        for h in range(2):
                            for q in range(2):
                                cols = slice(0, P) if q == 0 else slice(P, TRI)
                                c = 2 * h + q
                                A(prob[:, h, cols], soft[:, h, cols], ACT.Exp, bias=stat[:, 1, c:c + 1],
                                  accum_out=stat[:, 2, c:c + 1])
                        act.wait_ge(sf["sink_in"], j)
                        A(stat[:, 5, :], stat[:, 4, :], ACT.Exp).then_inc(sf["e_ready"], 1)
                    if not last:
                        act.wait_ge(sf["qk_proj"], j + 1)
                        b2 = bank[0][:, :].rearrange("p (t n) -> p t n", t=2)
                        copy(qk[:, :], bank[0][:, :]).then_inc(sf["raw"], 1)
                        A(xsq[:, 0:2, :], b2, ACT.Square).then_inc(sf["raw"], 1)
                        act.wait_ge(sf["ssum"], j + 1)
                        A(xn[:, 0:2, :], bank[2][:, :].rearrange("p (t n) -> p t n", t=2), ACT.Ln, scale=1.0 / HD,
                          bias=cst("eps")).then_inc(sf["ln"], 1)
                        act.wait_ge(sf["ln"], j + 1)
                        A(xn[:, 2:4, :], xn[:, 0:2, :], ACT.Exp, scale=-0.5).then_inc(sf["rinv"], 1)
                    if not first:
                        act.wait_ge(sf["t_done"], j)
                        copy(probT[:, 0, 0:TRI], bank[6][:, 0:TRI]).then_inc(sf["pt_act"], 1)
                        act.wait_ge(sf["o_done"], j)
                        copy(mixT[:, j - 1 - base, :], bank[3][:, 0:T]).then_inc(sf["o_ready"], 1)

                pair = sb_pair if KINDS[i] == "sb" else sf_pair
                pair(0, 0, first=True)
                steps(act, 1, PAIRS, pair)
                pair(PAIRS, 0, last=True)
                if 3 + 2 * i >= subs:
                    break
                norm(5 + 2 * i, xT, (x_done, KT * (2 + 2 * i), 1), hT, gcol(2), scol(mod, 3 * KT))
                n0 = FIRST[f"gu_{i}"]

                def silu(step, r):
                    s = step % RING
                    wait_used(act, n0 + step, r)
                    A(gact[s][:, :, :], bank[2 * s][:, :].rearrange("p (t n) -> p t n", t=2), ACT.Silu).then_inc(ffn_silu, 1)

                for step in range(RING):
                    silu(step, 0)
                steps(act, RING, GU, silu)

        @block.vector
        def _(dve):
            V = nc.vector
            count = {}

            def then(ins, s):
                count[s] = count.get(s, 0) + 1
                ins.then_inc(CH[s], 1)
                dve.wait_ge(CH[s], count[s])

            CH = {"mods": mods_step, "route": route_step}

            def normalise(e):
                dve.wait_ge(rinv_ready, e + 1)
                for k in range(KT):
                    V.tensor_tensor(xn[:, k, :], (ctxT if e == 0 else xT)[:, k, :], rinv[:, :], ALU.mult).then_inc(xn_ready, 1)

            def update(c, f, n, a, g):
                if f < 3:
                    dve.wait_ge(y_done, 6 * a + 3 * c + f + 1)
                else:
                    wait_used(dve, n)
                d = 4 * c + f
                V.scalar_tensor_tensor(xT[:, d, :], bank[(4 + d) % 8][:, 0:T], mod[:, g * KT + d:g * KT + d + 1], xT[:, d, :],
                                       ALU.mult, ALU.add).then_inc(x_done, 1)

            for n in range(N_HEAD - RING, N_HEAD):
                wait_used(dve, n)
            m2 = bank[2][:, 0:4 * KT].rearrange("p (m c) -> p m c", c=2)
            then(V.tensor_tensor(mod[:, 0:2 * KT], m2[:, :, 0], vc("b_ada", 0, 2 * KT), ALU.add), "mods")
            then(V.tensor_tensor(modc[:, :], m2[:, :, 1], vc("b_ada", 0, 2 * KT), ALU.add), "mods")
            V.scalar_tensor_tensor(gain[:, 0, :], mod[:, KT:2 * KT], 1.0, vc("norm1"), ALU.add, ALU.mult)
            V.scalar_tensor_tensor(gain[:, 1, :], modc[:, KT:2 * KT], 1.0, vc("norm1"), ALU.add, ALU.mult).then_inc(mods_ready, 1)
            dve.wait_ge(x_loaded, 32)
            normalise(0)
            normalise(1)

            n = FIRST["mix"] + 1
            wait_used(dve, n)
            dve.wait_ge(mix_act, 1)
            ch, cv = gact[1], gact[2]
            then(V.tensor_tensor(ch[:, :, :], gact[0][:, :, :], bank[3][:, :].rearrange("p (t n) -> p t n", t=2), ALU.mult), "mods")
            for f in range(2):
                tap = [vc("w_conv", 3 * f + t, 1) for t in range(3)]
                then(V.tensor_scalar(cv[:, f, :], ch[:, f, :], tap[1], None, ALU.mult), "mods")
                then(V.scalar_tensor_tensor(cv[:, f, 1:T], ch[:, f, 0:T - 1], tap[0], cv[:, f, 1:T], ALU.mult, ALU.add), "mods")
                then(V.scalar_tensor_tensor(cv[:, f, 0:T - 1], ch[:, f, 1:T], tap[2], cv[:, f, 0:T - 1], ALU.mult, ALU.add), "mods")
            V.tensor_tensor(mixT[:, 6:8, :], cv[:, :, :], bank[1][:, :].rearrange("p (t n) -> p t n", t=2), ALU.mult).then_inc(mix_dve, 1)

            def row_softmax_in(k, j):
                dve.wait_ge(k["mx"], j)
                V.tensor_scalar(stat[:, 1, :], stat[:, 0, :], -1.0, None, ALU.mult).then_inc(k["m_ready"], 1)

            def na_pair(j, first, last):
                if not first:
                    dve.wait_ge(na["scores"], j)
                    for c in range(4):
                        V.scalar_tensor_tensor(soft[:, c, 0:T], bank[4 + c][:, 0:T], SCALE, bias[:, c % 2, 2 * (j - 1) + c // 2, :],
                                               ALU.mult, ALU.add)
                        m = V.tensor_scalar(soft[:, c, T:2 * T], bank[4 + c][:, T:2 * T], SCALE, None, ALU.mult)
                    m.then_inc(na["s_ready"], 1)
                    dve.wait_ge(na["s_ready"], j)
                    V.tensor_reduce(stat[:, 0, :], soft[:, :, :], AX.X, ALU.max).then_inc(na["mx"], 1)
                    row_softmax_in(na, j)
                    dve.wait_ge(na["e_ready"], j)
                    V.reciprocal(stat[:, 3, :], stat[:, 2, :]).then_inc(na["rs"], 1)
                    dve.wait_ge(na["rs"], j)
                    for c in range(4):
                        m = V.tensor_scalar(prob[:, c, :], prob[:, c, :], stat[:, 3, c:c + 1], None, ALU.mult)
                    m.then_inc(na["p_ready"], 1)
                    dve.wait_ge(na["t_done"], j)
                    for q in range(2):
                        m = V.tensor_copy(probT[:, 1, :].rearrange("p (k q n) -> p k q n", k=4, q=2)[:, :, q, :],
                                          bank[6 + q][:, :].rearrange("p (k n) -> p k n", k=4))
                    m.then_inc(na["pt_dve"], 1)
                if not last:
                    wait_used(dve, FIRST["na"] + 2, j)
                    V.tensor_tensor(mod[:, bass.ds(2 * KT + 8 * j, 8)], bank[2][:, 0:16].rearrange("p (m c) -> p m c", c=2)[:, :, 0],
                                    vec[:, bass.ds(VEC["b_ada"][0] + 2 * KT + 8 * j, 8)], ALU.add).then_inc(na["ada_ready"], 1)
                    if not first:
                        dve.wait_ge(na["o_done"], j)
                    wait_used(dve, FIRST["na"], j)
                    V.tensor_copy(vv[:, :, :], bank[1][:, :].rearrange("p (t n) -> p t n", t=4)).then_inc(na["v_ready"], 1)

            dve.wait_ge(bias_masked, 1)
            na_pair(0, True, False)
            with dve.Fori(1, NA_PAIRS) as j:
                na_pair(j, False, False)
            na_pair(NA_PAIRS, False, True)
            dve.wait_ge(na["ada_ready"], NA_PAIRS)
            V.scalar_tensor_tensor(gain[:, 2, :], mod[:, 4 * KT:5 * KT], 1.0, vc("norm2"), ALU.add, ALU.mult).then_inc(mods_ready, 1)
            for c in range(2):
                for f in range(4):
                    update(c, f, FIRST["out_0"] + c, 0, 2)

            if subs > 1:
                V.memset(qr[:, :], 0.0).then_inc(zeroed, 1)
                normalise(2)
                dve.wait_ge(route_done, 1)
                R = lambda i, n=E: rt[:, i, :, 0:n]
                S = lambda i: small[:, i, :]
                B = lambda a, n: a.unsqueeze(2).broadcast_to([P, TT, n])
                iota = lambda n: cst("iota", 0, n).unsqueeze(1).broadcast_to([P, TT, n])
                then(V.tensor_tensor(logit[:, :, :], bank[0][:, 0:TT * (G + E)].rearrange("p (t n) -> p t n", t=TT),
                                     vc("b_route").unsqueeze(1).broadcast_to([P, TT, G + E]), ALU.add), "route")

                def first_max(x, mx, eq, idx, hot, n):
                    then(V.tensor_reduce(mx, x, AX.X, ALU.max), "route")
                    then(V.tensor_tensor(eq, x, B(mx, n), ALU.is_equal), "route")
                    then(V.tensor_scalar(eq, eq, -64.0, None, ALU.mult), "route")
                    then(V.tensor_tensor(eq, eq, iota(n), ALU.add), "route")
                    then(V.tensor_reduce(idx, eq, AX.X, ALU.min), "route")
                    then(V.tensor_tensor(hot, eq, B(idx, n), ALU.is_equal), "route")

                lg = logit[:, :, 0:G]
                first_max(lg, S(0), R(1, G), S(1), R(3, G), G)
                then(V.tensor_tensor(R(0, G), lg, B(S(0), G), ALU.subtract), "route")
                then(V.tensor_scalar(R(5, G), R(3, G), -NEG, NEG, ALU.mult, ALU.add), "route")
                then(V.tensor_tensor(R(6).rearrange("p t (g e) -> p t g e", g=G),
                                     logit[:, :, G:G + E].rearrange("p t (g e) -> p t g e", g=G),
                                     R(5, G).unsqueeze(3).broadcast_to([P, TT, G, EG]), ALU.add), "route")
                first_max(R(6), S(4), R(1), S(5), R(7), E)
                then(V.tensor_scalar(R(8), R(7), 2 * NEG, None, ALU.mult), "route")
                then(V.tensor_tensor(R(8), R(8), R(6), ALU.add), "route")
                first_max(R(8), S(6), R(1), S(5), R(9), E)
                then(V.tensor_tensor(S(7), S(6), S(4), ALU.subtract), "route")
                dve.wait_ge(route_act, 1)
                then(V.tensor_reduce(S(2), R(4, G), AX.X, ALU.add), "route")
                then(V.reciprocal(S(3), S(2)), "route")
                dve.wait_ge(route_act, 2)
                then(V.tensor_scalar(S(9), S(8), 1.0, None, ALU.add), "route")
                then(V.reciprocal(S(10), S(9)), "route")
                then(V.tensor_tensor(S(11), S(10), S(3), ALU.mult), "route")
                then(V.tensor_tensor(S(12), S(11), S(8), ALU.mult), "route")
                then(V.tensor_tensor(R(10), R(7), B(S(11), E), ALU.mult), "route")
                then(V.tensor_tensor(R(11), R(9), B(S(12), E), ALU.mult), "route")
                V.tensor_tensor(comb[:, :, :], R(10), R(11), ALU.add).then_inc(comb_done, 1)
                dve.wait_ge(route_done, 2)
                V.tensor_copy(combT[:, :], bank[1][0:E, 0:T]).then_inc(comb_ready, 1)
                dve.wait_ge(comb_ready, 1)
                with dve.Fori(0, E) as e:
                    V.tensor_scalar(comb_e[:, :], combT[:, :], const[0:E, bass.ds(CONST["ident"][0] + e, 1)], None,
                                    ALU.mult).then_inc(comb_sel, 1)
                    for f in range(FT_E):
                        dve.wait_ge(moe_silu, 4 * e + f + 1)
                        V.tensor_tensor(gact[f % 3][:, 1, :], gact[f % 3][:, 0, :], bank[f % 3][:, T:2 * T], ALU.mult).then_inc(moe_mul, 1)
                        dve.wait_ge(moe_mul, 4 * e + f + 1)
                        if f == 0:
                            dve.wait_ge(comb_bc, e + 1)
                            wait_used(dve, FIRST["moe"] + 2 - RING, e)
                        V.tensor_tensor(hid[:, f, :], gact[f % 3][:, 1, :], bank[3][:, 0:T], ALU.mult).then_inc(moe_hid, 1)
                wait_used(dve, FIRST["moe"] + 3 * E - 1)
                for d in range(KT):
                    V.scalar_tensor_tensor(xT[:, d, :], bank[4 + d // 2][:, (d % 2) * T:(d % 2 + 1) * T],
                                           mod[:, 5 * KT + d:5 * KT + d + 1], xT[:, d, :], ALU.mult, ALU.add).then_inc(x_done, 1)
                normalise(3)

            for i in layers:
                dve.wait_ge(mods_done, 1 + i)
                dve.wait_ge(x_done, KT * (2 + 2 * i))
                then(V.tensor_tensor(mod[:, :], bank[2][:, 0:MODS], vc("b_ada2", MODS * i, MODS), ALU.add), "mods")
                V.scalar_tensor_tensor(gain[:, 0, :], mod[:, KT:2 * KT], 1.0, vc("gains2", 2 * KT * i, KT), ALU.add, ALU.mult)
                V.scalar_tensor_tensor(gain[:, 2, :], mod[:, 4 * KT:5 * KT], 1.0, vc("gains2", 2 * KT * i + KT, KT),
                                       ALU.add, ALU.mult).then_inc(mods_ready, 1)
                normalise(4 + 2 * i)
                n0 = FIRST[f"pair_{i}"]
                base = epoch(i)

                def values(k, step, r, j, first):
                    if not first:
                        dve.wait_ge(k["o_done"], j)
                    wait_used(dve, n0 + step, r)
                    V.tensor_copy(vv[:, 0:2, :], bank[1][:, 0:T].rearrange("p (t n) -> p t n", t=TT)).then_inc(k["v_ready"], 1)

                def sb_pair(step, r, first=False, last=False):
                    j = step + RING * r + base
                    mask = cst("mask_sb")
                    if not first:
                        dve.wait_ge(sk["scores"], j)
                        for h in range(2):
                            m = V.scalar_tensor_tensor(soft[:, h, 0:TRI], bank[4 + h][:, 0:TRI], SCALE, mask, ALU.mult, ALU.add)
                        m.then_inc(sk["zm_ready"], 1)
                        dve.wait_ge(sk["ln"], j)
                        V.scalar_tensor_tensor(soft[:, 2:4, 0:TRI], soft[:, 0:2, 0:TRI], 0.0, prob[:, 0:2, 0:TRI],
                                               ALU.max, ALU.add).then_inc(sk["sp_ready"], 1)
                        dve.wait_ge(sk["suffix"], j)
                        for h in range(2):
                            m = V.tensor_tensor(prob[:, 2 + h, 0:TRI], soft[:, h, 0:TRI], bank[6 + h][:, 0:TRI], ALU.subtract)
                        m.then_inc(sk["w_ready"], 1)
                    if not last:
                        values(sk, step, r, j, first)

                def sf_pair(step, r, first=False, last=False):
                    j = step + RING * r + base
                    kind = KINDS[i]
                    mask = cst("mask_" + kind)
                    if not first:
                        dve.wait_ge(sf["scores"], j)
                        for h in range(2):
                            m = V.scalar_tensor_tensor(soft[:, h, 0:TRI], bank[4 + h][:, 0:TRI], SCALE, mask, ALU.mult, ALU.add)
                        m.then_inc(sf["s_ready"], 1)
                        dve.wait_ge(sf["s_ready"], j)
                        V.tensor_reduce(stat[:, 6, 0:4:2], soft[:, 0:2, 0:P], AX.X, ALU.max)
                        V.tensor_reduce(stat[:, 6, 1:4:2], soft[:, 0:2, P:TRI], AX.X, ALU.max).then_inc(sf["mx"], 1)
                        dve.wait_ge(sf["mx"], j)
                        sink = (j - 1 - base) * 4
                        snk = vec[:, bass.ds(VEC["sinks"][0] + 4 * PAIRS * (kind == "moba") + sink, 4)]
                        V.tensor_tensor(stat[:, 0, :], stat[:, 6, :], snk, ALU.max).then_inc(sf["rs"], 1)
                        dve.wait_ge(sf["rs"], 3 * j - 2)
                        V.tensor_scalar(stat[:, 1, :], stat[:, 0, :], -1.0, None, ALU.mult).then_inc(sf["m_ready"], 1)
                        V.tensor_tensor(stat[:, 4, :], snk, stat[:, 0, :], ALU.subtract).then_inc(sf["sink_in"], 1)
                        dve.wait_ge(sf["e_ready"], j)
                        V.tensor_tensor(stat[:, 7, :], stat[:, 2, :], stat[:, 5, :], ALU.add).then_inc(sf["rs"], 1)
                        dve.wait_ge(sf["rs"], 3 * j - 1)
                        V.reciprocal(stat[:, 3, :], stat[:, 7, :]).then_inc(sf["rs"], 1)
                        dve.wait_ge(sf["rs"], 3 * j)
                        for h in range(2):
                            V.tensor_scalar(prob[:, h, 0:P], prob[:, h, 0:P], stat[:, 3, 2 * h:2 * h + 1], None, ALU.mult)
                            m = V.tensor_scalar(prob[:, h, P:TRI], prob[:, h, P:TRI], stat[:, 3, 2 * h + 1:2 * h + 2], None, ALU.mult)
                        m.then_inc(sf["p_ready"], 1)
                    if not last:
                        dve.wait_ge(sf["rinv"], j + 1)
                        for c in range(2):
                            V.scalar_tensor_tensor(qn[:, c * T:(c + 1) * T], qk[:, c * T:(c + 1) * T], vc("qk_" + kind, c, 1),
                                                   xn[:, 2 + c, :], ALU.mult, ALU.mult).then_inc(sf["qn_ready"], 1)
                        dve.wait_ge(sf["qn_ready"], 2 * j + 2)
                        V.tensor_tensor(xn[:, 4:6, :], qn[:, :].rearrange("p (c n) -> p c n", c=2),
                                        cst("cos").unsqueeze(1).broadcast_to([P, 2, T]), ALU.mult).then_inc(sf["rope"], 1)
                    if not first:
                        dve.wait_ge(sf["t_done"], j)
                        V.tensor_copy(probT[:, 1, 0:TRI], bank[7][:, 0:TRI]).then_inc(sf["pt_dve"], 1)
                    if not last:
                        dve.wait_ge(sf["rot"], j + 1)
                        V.tensor_tensor(xn[:, 6:8, :], bank[2][:, :].rearrange("p (c n) -> p c n", c=2),
                                        cst("sin").unsqueeze(1).broadcast_to([P, 2, T]), ALU.mult).then_inc(sf["rope"], 1)
                        dve.wait_ge(sf["rope"], 2 * j + 2)
                        V.tensor_tensor(qr[:, :].rearrange("p (c n) -> p c n", c=2), xn[:, 4:6, :], xn[:, 6:8, :],
                                        ALU.add).then_inc(sf["qr_ready"], 1)
                        values(sf, step, r, j, first)

                pair = sb_pair if KINDS[i] == "sb" else sf_pair
                pair(0, 0, first=True)
                steps(dve, 1, PAIRS, pair)
                pair(PAIRS, 0, last=True)
                for c in range(2):
                    for f in range(4):
                        update(c, f, FIRST[f"out_{i + 1}"] + c, 1 + i, 2)
                if 3 + 2 * i >= subs:
                    break
                normalise(5 + 2 * i)

                def gate_up(step, r):
                    s = step % RING
                    dve.wait_ge(ffn_silu, GU * i + step + 1 + RING * r)
                    V.tensor_tensor(hid[:, bass.ds(2 * step + 2 * RING * r, 2), :], gact[s][:, :, :],
                                    bank[2 * s + 1][:, :].rearrange("p (t n) -> p t n", t=2), ALU.mult).then_inc(ffn_hid, 1)

                for step in range(RING):
                    gate_up(step, 0)
                steps(dve, RING, GU, gate_up)

                def down(step, r):
                    wait_used(dve, FIRST[f"down_{i}"] + step, r)
                    d = step + RING * r
                    x = xT[:, bass.ds(d, 1), :]
                    V.scalar_tensor_tensor(x, bank[5 + step % RING][:, 0:T].unsqueeze(1), mod[:, bass.ds(5 * KT + d, 1)], x,
                                           ALU.mult, ALU.add).then_inc(x_done, 1)

                for step in range(2):
                    down(step, 0)
                steps(dve, 2, KT, down)


def constants():
    i, t = np.arange(P), np.arange(T)
    col = {}
    col["ident"] = np.eye(P)
    col["ones"] = np.ones((P, P))
    col["headones"] = i[:, None] // HD == i[None, :] // HD
    half, d = HD // 2, i % HD
    rot = np.zeros((P, P))
    lo = i[d < half]
    rot[lo + half, lo] = -1.0
    rot[lo, lo + half] = 1.0
    col["rot"] = rot
    col["suffix"] = i[:, None] >= i[None, :]
    f = np.float32
    inv = f(1.0) / (f(10000.0) ** (np.arange(0, HD, 2, dtype=f) / f(HD)))
    ang = (t.astype(f)[:, None] * inv[None, :]).astype(f)
    col["cos"] = np.cos(ang)[:, d % half].T
    col["sin"] = np.sin(ang)[:, d % half].T
    k, q = i[:, None], t[None, :]
    sb = [k < q, k + P < q[:, P:]]
    col["mask_sb"] = np.where(np.concatenate(sb, 1), 0.0, NEG)
    rows = [(i[:, None] + a, np.arange(n)[None, :]) for a, n in ((0, P), (P, T))]
    col["mask_moba"] = np.where(np.concatenate([kk <= qq for qq, kk in rows], 1), 0.0, NEG)
    col["mask_swa"] = np.where(np.concatenate([(kk <= qq) & (qq - kk < P) for qq, kk in rows], 1), 0.0, NEG)
    qc, kc = i[:, None] % GRID_W, t[None, :] % GRID_W
    start = np.clip(qc - NA_KW // 2, 0, GRID_W - NA_KW)
    col["mask_na"] = np.where((kc >= start) & (kc < start + NA_KW), 0.0, NEG)
    w = 2 * np.pi * ((t[:, None] * t[None, :]) % T) / T
    dft = np.stack([np.cos(w), np.sin(w)], 1).reshape(TT, P, 2, T)
    col["dft"] = dft.transpose(1, 0, 2, 3).reshape(P, -1)
    same = i[:, None] // HD == i[None, :] // HD
    w = 2 * np.pi * ((d[:, None] * d[None, :]) % HD) / HD
    norm = 1.0 / np.sqrt(T * HD)
    col["cd"] = np.where(same, np.cos(w) * norm, 0.0)
    col["sd"] = np.where(same, -np.sin(w) * norm, 0.0)
    col["iota"] = np.broadcast_to(np.arange(E), (P, E))
    col["eps"] = np.full((P, 1), EPS)
    col["zero"] = np.zeros((P, 1))
    out = np.zeros((P, N_CONST), np.float32)
    for name, (a, b) in CONST.items():
        out[:, a:b] = col[name]
    return out


def cols(v):
    v = np.asarray(v)
    return np.ascontiguousarray(np.moveaxis(v.reshape(*v.shape[:-1], -1, P), -1, 0)).reshape(P, -1)


def by_row(w, lo, n):
    return w[:, lo:lo + n].reshape(-1, P, n).transpose(1, 0, 2)


def lay_out(a):
    f = {k: np.asarray(v) for k, v in a.items()}
    o = {"const": constants()}
    rep = lambda v: np.broadcast_to(v, (P,) + v.shape)
    sinks = np.repeat(f["swa_sinks_2"][0], 2)
    o["vec"] = np.concatenate([
        np.stack([cols(f["c"][0]), cols(f["c_ctx"])], 2).reshape(P, -1), cols(f["c_2"][0]),
        cols(f["norm1"][0]), cols(f["norm2"][0]), cols(f["norm_final"]),
        f["w_conv"][0].reshape(3, 2, P).transpose(2, 1, 0).reshape(P, -1), cols(f["b_ada"][0]),
        cols(f["norm_gain_2"]), cols(f["ada_b_2"]),
        np.tile(f["moba_qk_gain_2"][0].T, (2, 1)), np.tile(f["swa_qk_gain_2"][0].T, (2, 1)),
        rep(sinks), np.full((P, 4 * PAIRS), NEG, np.float32),
        rep(np.concatenate([f["b_rg"][0], f["b_re"][0]]))], 1)
    o["xT"] = f["x"][0].T.reshape(KT, P, T).transpose(1, 0, 2)
    o["ctxT"] = f["ctx"][0].T.reshape(KT, P, T).transpose(1, 0, 2)
    ada = [by_row(f["w_ada"][0], 512 * n, 512) for n in range(MODS // 4)]
    o["ada_head"] = np.stack(ada[:N_HEAD])
    w = f["w_in"][0]
    q, k, v, gb, gc, h = (256, 768, 1280, 1792, 2048, 2304)
    o["mix"] = np.stack([np.concatenate([by_row(w, a_, 256), by_row(w, b_, 256)], 2) for a_, b_ in ((0, gb), (gc, h))])
    na = []
    for j in range(NA_PAIRS):
        pair = np.concatenate([by_row(w, at + P * j, P) for at in (q, k, v)], 2).reshape(P, -1)
        na += [np.concatenate([pair, np.zeros((P, SLOT - pair.shape[1]), np.float32)], 1)]
        na += [x.reshape(P, -1) for x in ada[N_HEAD + 2 * j:N_HEAD + 2 * j + 2]]
    o["na"] = np.stack(na)
    outs = [f["w_out"][0], f["sb_w_out_2"][0], f["moba_w_out_2"][0], f["swa_w_out_2"][0], f["sb_w_out_2"][1]]
    for n, w in enumerate(outs):
        o[f"out_{n}"] = np.stack([by_row(w, 512 * c, 512) for c in range(2)])
    o["wf"] = by_row(f["w_fourier"][0], 0, 256)
    o["wr"] = np.concatenate([by_row(f["w_rg"][0], 0, G), by_row(f["w_re"][0], 0, E)], 2)
    t = np.arange(T)
    row = t[None, :] // GRID_W - t[:, None] // GRID_W + NA_KH - 1
    coff = np.clip(t[None, :] % GRID_W - t[:, None] % GRID_W + NA_KW - 1, 0, 2 * NA_KW - 2)
    o["bias"] = f["rpb"][0][:, row, coff].reshape(NA_HEADS, TT, P, T).transpose(2, 1, 0, 3)
    o["moe"] = np.stack([x for e in range(E) for x in (
        by_row(f["w_gate"][0, e], 0, 512).reshape(P, -1), by_row(f["w_up"][0, e], 0, 512).reshape(P, -1),
        by_row(f["w_down"][0, e], 0, D).reshape(P, -1))])
    o["ada2"] = np.stack([by_row(f["ada_w_2"][i], 512 * n, 512) for i in range(LAYERS) for n in range(12)])
    swa = f["swa_w_in_2"][0]
    for i, kind in enumerate(KINDS):
        ch = []
        for j in range(PAIRS):
            if kind == "swa":
                g = j * 2 // PAIRS
                kk, vv_ = by_row(swa, D + HD * g, HD), by_row(swa, D + P + HD * g, HD)
                parts = [by_row(swa, P * j, P), kk, kk, vv_, vv_]
            else:
                w = f["moba_w_in_2"][0] if kind == "moba" else f["sb_w_in_2"][i // 3]
                parts = [by_row(w, at + P * j, P) for at in (0, D, 2 * D)]
            ch.append(np.concatenate(parts, 2))
        o[f"pair_{i}"] = np.stack(ch)
        g_, u_, d_ = f["ffn_w_gate_2"][i], f["ffn_w_up_2"][i], f["ffn_w_down_2"][i]
        o[f"gu_{i}"] = np.stack([np.concatenate([by_row(g_, 256 * n, 256), by_row(u_, 256 * n, 256)], 2) for n in range(GU)])
        o[f"down_{i}"] = np.stack([by_row(d_, P * n, P) for n in range(KT)])
    shape = {name: (n, P, width) for name, n, width in PHASES}
    shape["ada2"] = (LAYERS * 12, P, SLOT)
    return {k: np.ascontiguousarray(v.reshape(shape.get(k, v.shape))) for k, v in o.items()}


def kernel(**inputs):
    import concourse.bacc as bacc
    from concourse.bass_utils import run_bass_kernel_spmd

    nc = bacc.Bacc("TRN2", target_bir_lowering=False, num_devices=1)
    arrays = {f"in_{k}": v for k, v in lay_out(inputs).items()}
    ins = {k: nc.dram_tensor("in_" + k, arrays["in_" + k].shape, F32, kind="ExternalInput").ap() for k in
           [n[3:] for n in arrays]}
    out = nc.dram_tensor("out_xT", (P, KT, T), F32, kind="ExternalOutput").ap()
    build(nc, ins, out)
    r = run_bass_kernel_spmd(nc, [arrays], core_ids=[0])
    y = np.asarray(r.results[0]["out_xT"])
    return np.ascontiguousarray(y.transpose(2, 1, 0)).reshape(1, T, D)
```

```python
from contextlib import ExitStack

import numpy as np
import concourse.bass as bass
from concourse import mybir

F32 = mybir.dt.float32
ALU = mybir.AluOpType
ACT = mybir.ActivationFunctionType
AX = mybir.AxisListType

P = 128
D = 1024
KT = D // P
T = 256
TT = T // P
HD = 64
SCALE = HD ** -0.5
EPS = 1e-6
NEG = -1e30
GRID_W, NA_KW, NA_KH = 64, 16, 8
NA_HEADS = 8
NA_PAIRS = NA_HEADS // 2
PAIRS = D // (2 * HD)
G, EG = 4, 8
E = G * EG
FE = 512
FT_E = FE // P
DFF = 2816
FT = DFF // P
GU = FT // 2
MODS = 6 * KT
RING = 3
SLOT = 4096
TRI = 3 * P
LAYERS = 4
WIN = 96
KINDS = ("sb", "moba", "swa", "sb")

CONST = {}
_at = 0
for _name, _n in (("ident", P), ("ones", P), ("headones", P), ("rot", P), ("suffix", P), ("cos", T), ("sin", T),
                  ("mask_sb", TRI), ("mask_moba", TRI), ("mask_swa", TRI), ("mask_na", T),
                  ("dft", TT * 2 * T), ("cd", P), ("sd", P), ("iota", T), ("before", P), ("eps", 1), ("zero", 1)):
    CONST[_name] = (_at, _at + _n)
    _at += _n
N_CONST = _at

VEC = {}
_at = 0
for _name, _n in (("c", KT * 2), ("c2", KT), ("norm1", KT), ("norm2", KT), ("normf", KT), ("w_conv", 2 * 3),
                  ("b_ada", MODS), ("gains2", LAYERS * 2 * KT), ("b_ada2", LAYERS * MODS), ("qk_moba", 2),
                  ("qk_swa", 2), ("sinks", 8 * PAIRS), ("b_route", G + E)):
    VEC[_name] = (_at, _at + _n)
    _at += _n
N_VEC = _at

N_HEAD = 4
PHASES = (
    [("ada_head", N_HEAD, SLOT), ("mix", 2, SLOT), ("na", 3 * NA_PAIRS, SLOT), ("out_0", 2, SLOT), ("moe", 3 * E, SLOT)]
    + [ph for i in range(LAYERS) for ph in
       ((f"pair_{i}", PAIRS, 3 * KT * P), (f"out_{i + 1}", 2, SLOT), (f"gu_{i}", GU, SLOT), (f"down_{i}", KT, FT * P))]
)
FIRST = {}
_at = 0
for _name, _n, _ in PHASES:
    FIRST[_name] = _at
    _at += _n


def build(nc, ins, out, subs=2 + 2 * LAYERS):
    layers = [i for i in range(LAYERS) if 2 + 2 * i < subs]
    phases = PHASES[:[4, 5][min(subs, 2) - 1]] + PHASES[5:5 + 2 * max(0, subs - 2)]
    ctx = ExitStack()
    with ctx:
        def sb(name, shape):
            return ctx.enter_context(nc.sbuf_tensor(name, shape, F32))

        def sem(name):
            return ctx.enter_context(nc.semaphore(name))

        const = sb("const_sb", [P, N_CONST])
        vec = sb("vec_sb", [P, N_VEC])
        ring = [sb(f"ring{s}", [P, SLOT]) for s in range(RING)]
        ada_ring = [sb(f"ada_ring{s}", [P, SLOT]) for s in range(2)]
        ada_sum = sb("ada_sum", [P, MODS * P])
        xT = sb("xT", [P, KT, T])
        xsq = sb("xsq", [P, KT, T])
        xn = sb("xn", [P, KT, T])
        hT = sb("hT", [P, KT, T])
        rinv = sb("rinv", [P, T])
        mixT = sb("mixT", [P, KT, T])
        work = sb("work", [P, 3, 4 * 2 * T])
        gact = [sb(f"gact{s}", [P, 2, T]) for s in range(RING)]
        mod = sb("mod", [P, MODS])
        modc = sb("modc", [P, 2 * KT])
        gain = sb("gain", [P, 3, KT])
        csilu = sb("csilu", [P, 2 * KT])
        c2silu = sb("c2silu", [P, KT])
        qk = sb("qk", [P, 2 * T])
        qn = sb("qn", [P, 2 * T])
        qr = sb("qr", [P, 2 * T])
        vv = sb("vv", [P, 4, P])
        stat = sb("stat", [P, 8, 4])
        wf = sb("wf", [P, 2, T])
        wr = sb("wr", [P, KT, G + E])
        logit = sb("logit", [P, TT, G + E])
        small = sb("small", [P, 16, TT])
        comb = sb("comb", [P, TT, E])
        combT = sb("combT", [E, T])
        comb_e = sb("comb_e", [E, T])
        gcount = sb("gcount", [P, 3, G])
        win = ctx.enter_context(nc.sbuf_tensor("win", [P, G + 1], mybir.dt.int32))
        bank = [ctx.enter_context(nc.psum_tensor(f"bank{i}", [P, 512], F32)) for i in range(8)]

        soft = work[:, 0, :].rearrange("p (c n) -> p c n", c=4)
        prob = work[:, 1, :].rearrange("p (c n) -> p c n", c=4)
        probT = work[:, 2, :].rearrange("p (h n) -> p h n", h=2)
        hid = work[:, :, :].rearrange("p a b -> p (a b)")[:, 0:FT * T].rearrange("p (f t) -> p f t", f=FT)
        rt = work[:, 0, 0:12 * TT * E].rearrange("p (i t e) -> p i t e", i=12, t=TT)
        lnms = xn[:, KT - 1, :]
        rinv2 = [qn[:, 0:T], rinv[:, :]]
        hS = mixT
        htok = xn[:, :, :].rearrange("p k t -> p (k t)").rearrange("p (t d) -> p t d", t=TT)
        hW = [xn[:, :, :].rearrange("p k t -> p (k t)")[:, b * KT * WIN:(b + 1) * KT * WIN].rearrange("p (k n) -> p k n", k=KT)
              for b in range(2)]
        ysum = xsq
        place = qk[:, :].rearrange("p (t n) -> p t n", t=TT)
        placeT = qn[:, :].rearrange("p (t n) -> p t n", t=TT)
        hcT = ada_sum[:, 0:KT * T].rearrange("p (k t) -> p k t", k=KT)
        ctxT = ada_sum[:, KT * T:2 * KT * T].rearrange("p (k t) -> p k t", k=KT)
        b16 = ada_ring[0][:, :].rearrange("p (c n) -> p c n", n=T)
        bias = b16.rearrange("p (q h) n -> p q h n", q=TT)

        def cst(name, lo=0, n=None):
            a, b = CONST[name]
            return const[:, a + lo:(a + lo + n) if n else b]

        def vc(name, lo=0, n=None):
            a, b = VEC[name]
            return vec[:, a + lo:(a + lo + n) if n else b]

        landed = [sem(f"landed{s}") for s in range(RING)]
        used = [sem(f"used{s}") for s in range(RING)]
        loaded, const_loaded, ctx_loaded, x_loaded, side_loaded = (
            sem(n) for n in ("loaded", "const_loaded", "ctx_loaded", "x_loaded", "side_loaded"))
        ada_landed = [sem(f"ada_landed{s}") for s in range(2)]
        ada_prod, ada_half, ada_quarter, ada_summed = (sem(n) for n in ("ada_prod", "ada_half", "ada_quarter", "ada_summed"))
        ada_rows, ada_cols = sem("ada_rows"), sem("ada_cols")
        silu_done, mods_done, mods_step, mods_ready = (sem(n) for n in ("silu_done", "mods_done", "mods_step", "mods_ready"))
        sq_ready, ssq_done, ln_ms, rinv_ready, xn_ready, h_ready = (
            sem(n) for n in ("sq_ready", "ssq_done", "ln_ms", "rinv_ready", "xn_ready", "h_ready"))
        y_done, x_done = sem("y_done"), sem("x_done")
        bias_masked = sem("bias_masked")
        mix_proj, mix_act, mix_dve, dft_pe, dft_act = (sem(n) for n in ("mix_proj", "mix_act", "mix_dve", "dft_pe", "dft_act"))
        na = {n: sem("na_" + n) for n in (
            "qk_proj", "qk_ready", "v_ready", "scores", "s_ready", "mx", "m_ready", "e_ready", "rs", "p_ready",
            "t_done", "pt_act", "pt_dve", "o_done", "o_ready", "ada_row", "ada_done", "ada_ready")}
        sk = {n: sem("sb_" + n) for n in (
            "qk_proj", "qk_ready", "v_ready", "scores", "zm_ready", "abs", "exp", "ln", "sp_ready", "suffix",
            "w_ready", "a_ready", "o_done", "o_ready")}
        sf = {n: sem("sf_" + n) for n in (
            "qk_proj", "raw", "ssum", "ln", "rinv", "qn_ready", "rope", "rot", "qr_ready", "v_ready", "scores",
            "s_ready", "mx", "m_ready", "sink_in", "sink_e", "e_ready", "den", "rs", "p_ready", "t_done", "pt_act", "pt_dve",
            "o_done", "o_ready")}
        route_done, route_act, route_step, hot_ready, top_ready, win_ready, place_ready, comb_ready = (
            sem(n) for n in ("route_done", "route_act", "route_step", "hot_ready", "top_ready", "win_ready", "place_ready", "comb_ready"))
        perm_pe, perm_act, perm_dve, unperm = (sem(n) for n in ("perm_pe", "perm_act", "perm_dve", "unperm"))
        comb_sel, comb_bc, moe_gu, moe_silu, moe_mul, moe_hid = (
            sem(n) for n in ("comb_sel", "comb_bc", "moe_gu", "moe_silu", "moe_mul", "moe_hid"))
        zeroed, win_in, win_out, win_zero = sem("zeroed"), sem("win_in"), sem("win_out"), sem("win_zero")
        ffn_silu, ffn_hid = sem("ffn_silu"), sem("ffn_hid")
        stored = sem("stored")

        block = ctx.enter_context(nc.Block())

        def slot(n):
            return ring[n % RING]

        def wait_chunk(eng, n, r=0):
            eng.wait_ge(landed[n % RING], 16 * (n // RING + 1) + 16 * r)

        def wait_used(eng, n, r=0):
            eng.wait_ge(used[n % RING], n // RING + 1 + r)

        def steps(eng, lo, hi, body):
            rounds = (hi - lo) // RING
            if rounds >= 2:
                with eng.Fori(0, rounds) as r:
                    for s in range(RING):
                        body(lo + s, r)
            else:
                rounds = 0
            for step in range(lo + RING * rounds, hi):
                body(step, 0)

        def pair_of(b):
            return b[:, :].rearrange("p (t n) -> p t n", t=2)

        def moe_branches(eng, expert, window=None, gather=None, scatter=None, collect=None):
            eng.wait_ge(win_ready, 1)
            fits = eng.value_load(win[0:1, G:G + 1], min_val=0, max_val=1)
            with eng.If(fits == 1):
                for g in range(G):
                    at = window(g) if window else 0
                    if gather:
                        gather(g, at)
                    with eng.Fori(0, EG) as i:
                        expert(EG * g + i, g, at, WIN)
                    if scatter:
                        scatter(g, at)
            with eng.Else():
                if collect:
                    collect(False)
                with eng.Fori(0, E) as e:
                    expert(e, None, 0, T)
                if collect:
                    collect(True)

        def ada_row(n):
            return gact[n][:, :, :].rearrange("p a n -> p (a n)") if n < RING else qr[:, :]

        def norm_bank(e):
            return bank[4 if e == 2 or e > 4 and e % 2 else 3]

        def epoch(layer):
            kind = KINDS[layer] == "sb"
            return PAIRS * sum((KINDS[i] == "sb") == kind for i in range(layer))

        @block.sync
        def _(sp):
            sp.dma_start(vec[:, :], ins["vec"]).then_inc(loaded, 16)
            between = [(ctxT, ins["ctxT"], ctx_loaded), (const[:, :], ins["const"], const_loaded), (xT[:, :, :], ins["xT"], x_loaded)]
            for name, count, width in phases:
                n0 = FIRST[name]

                def load(step, r):
                    if n0 + step >= RING:
                        wait_used(sp, n0 + step - RING, r)
                    sp.dma_start(slot(n0 + step)[:, 0:width], ins[name][step + RING * r]).then_inc(landed[(n0 + step) % RING], 16)

                if name == "ada_head":
                    for step in range(count):
                        load(step, 0)
                        for dst, src, landed_in in between[step:step + 1]:
                            sp.dma_start(dst, src).then_inc(landed_in, 16)
                else:
                    steps(sp, 0, count, load)
            sp.wait_ge(x_done, KT * subs)
            if subs == 2:
                sp.wait_ge(h_ready, KT * 4)
            sp.dma_start(out, xT[:, :, :]).then_inc(stored, 16)
            sp.wait_ge(stored, 16)

        @block.gpsimd
        def _(pool):
            pool.dma_start(wf[:, :, :], ins["wf"]).then_inc(side_loaded, 16)
            pool.dma_start(wr[:, :, :], ins["wr"]).then_inc(side_loaded, 16)
            pool.dma_start(bias, ins["bias"]).then_inc(side_loaded, 16)
            pool.wait_ge(side_loaded, 48)
            pool.wait_ge(const_loaded, 16)
            nc.gpsimd.tensor_tensor(b16, b16, cst("mask_na").unsqueeze(1).broadcast_to([P, TT * NA_HEADS, T]),
                                    ALU.add).then_inc(bias_masked, 1)
            if not layers:
                return
            pool.wait_ge(silu_done, 2)
            chunks = MODS * P // 512
            wait_used(pool, FIRST["out_0"] - RING)
            pool.wait_ge(na["p_ready"], NA_PAIRS)
            for s in range(2):
                pool.dma_start(ada_ring[s][:, :], ins["ada2"][s]).then_inc(ada_landed[s], 16)

            def chunk(c, r, s, more):
                w3 = ada_ring[s][:, :].rearrange("p (k n) -> p k n", k=KT)
                pool.wait_ge(ada_landed[s], 16 * (c // 2 + 1) + 16 * r)
                nc.gpsimd.tensor_tensor(w3, w3, c2silu[:, :].unsqueeze(2).broadcast_to([P, KT, 512]),
                                        ALU.mult).then_inc(ada_prod, 1)
                pool.wait_ge(ada_prod, c + 1 + 2 * r)
                nc.gpsimd.tensor_tensor(w3[:, 0:4, :], w3[:, 0:4, :], w3[:, 4:8, :], ALU.add).then_inc(ada_half, 1)
                pool.wait_ge(ada_half, c + 1 + 2 * r)
                nc.gpsimd.tensor_tensor(w3[:, 0:2, :], w3[:, 0:2, :], w3[:, 2:4, :], ALU.add).then_inc(ada_quarter, 1)
                pool.wait_ge(ada_quarter, c + 1 + 2 * r)
                col = 512 * (c % chunks) + 1024 * r
                nc.gpsimd.tensor_tensor(ada_sum[:, bass.ds(col, 512)], w3[:, 0, :], w3[:, 1, :],
                                        ALU.add).then_inc(ada_summed, 1)
                if more:
                    pool.wait_ge(ada_summed, c + 1 + 2 * r)
                    if c < chunks:
                        wait_used(pool, FIRST["moe"] + 2, 2 * c + 4 * r)
                    pool.dma_start(ada_ring[s][:, :], ins["ada2"][c + 2 + 2 * r]).then_inc(ada_landed[s], 16)

            for i in layers:
                for half in range(2):
                    if i > 0:
                        pool.wait_ge(mods_done, 2 * i - 1 + half)
                    c0 = chunks * i + chunks // 2 * half
                    with pool.Fori(0, chunks // 4 - 1) as r:
                        for s in range(2):
                            chunk(c0 + s, r, s, True)
                    for s in range(2):
                        chunk(c0 + chunks // 2 - 2 + s, 0, s, (i, half) != (layers[-1], 1))

        @block.tensor
        def _(pe):
            mm = nc.tensor.matmul

            def norm(e):
                b = norm_bank(e)
                for k in range(KT):
                    pe.wait_ge(sq_ready, KT * e + k + 1)
                    m = mm(b[:, 0:T], cst("ones"), xsq[:, k, :], start=k == 0, stop=k == KT - 1)
                m.then_inc(ssq_done, 1)

            def project(dst, w, lo, h, ready=None):
                for k in range(KT):
                    if ready is not None:
                        pe.wait_ge(h_ready, ready + k + 1)
                    m = mm(dst, w[:, k, lo:lo + P], h[:, k, :], start=k == 0, stop=k == KT - 1)
                return m

            def rows(dst, w, lo, n, h, t0=0, t1=TT):
                for t in range(t0, t1):
                    for k in range(KT):
                        m = mm(dst[:, t, :], h[:, k, t * P:(t + 1) * P], w[:, k, lo:lo + n], start=k == 0, stop=k == KT - 1)
                return m

            def chunk3(n, cols):
                return slot(n)[:, 0:KT * cols].rearrange("p (k n) -> p k n", k=KT)

            def out_proj(name):
                for c in range(2):
                    n = FIRST[name] + c
                    wait_chunk(pe, n)
                    w = chunk3(n, 512)
                    for f in range(4):
                        project(bank[(4 + 4 * c + f) % 8][:, 0:T], w, f * P, mixT).then_inc(y_done if f < 3 else used[n % RING], 1)

            def values(o, h, tiles, cols):
                for i, kt in enumerate(tiles):
                    (a, b), (c, d) = cols(kt)
                    m = mm(o[64 * h:64 * h + 64, a:b], vv[:, kt, 64 * h:64 * h + 64], probT[:, h, c:d],
                           start=i == 0, stop=i == len(tiles) - 1, skip_group_check=True)
                return m

            def tri(kt):
                return ((0, T), (0, T)) if kt == 0 else ((P, T), (T, TRI))

            pe.wait_ge(silu_done, 1)
            cc = csilu[:, :].rearrange("p (k c) -> p k c", c=2)

            def ada(n, dst, r=0):
                wait_chunk(pe, n, r)
                w = chunk3(n, 512)
                for k in range(KT):
                    m = mm(dst, cc[:, k, 0:dst.shape[0]], w[:, k, :], start=k == 0, stop=k == KT - 1)
                m.then_inc(used[n % RING], 1)

            def ada_columns(dst, row, c):
                for f in range(4):
                    m = mm(dst[:, c * f:c * (f + 1)], row[:, f * P:(f + 1) * P], cst("ident")[0:c, 0:c], start=True, stop=True)
                return m

            for n in range(2):
                ada(n, bank[4 + n][0:2, :])
            pe.wait_ge(const_loaded, 16)
            norm(0)
            for n in range(2, N_HEAD):
                ada(n, bank[4 + n][0:2, :])
            pe.wait_ge(ln_ms, 1)
            norm(1)
            for n in range(N_HEAD):
                pe.wait_ge(ada_rows, n + 1)
                m = ada_columns(bank[2][:, 8 * n:8 * n + 8], ada_row(n)[0:2, :], 2)
            m.then_inc(ada_cols, 1)

            n = FIRST["mix"]
            pe.wait_ge(h_ready, 2 * KT)
            wait_chunk(pe, n)
            rows(bank[0][:, :].rearrange("p (t n) -> p t n", t=TT), chunk3(n, 512), 0, T, hT).then_inc(mix_proj, 1)
            project(bank[1][:, 0:T], chunk3(n, 512), 256, hT)
            project(bank[1][:, T:2 * T], chunk3(n, 512), 384, hT).then_inc(used[n % RING], 1)
            n += 1
            wait_chunk(pe, n)
            pe.wait_ge(mods_ready, 1)
            project(bank[2][:, 0:T], chunk3(n, 512), 0, hT)
            project(bank[2][:, T:2 * T], chunk3(n, 512), 128, hT).then_inc(mix_proj, 1)
            pe.wait_ge(rinv_ready, 2)
            project(bank[3][:, 0:T], chunk3(n, 512), 256, hT)
            project(bank[3][:, T:2 * T], chunk3(n, 512), 384, hT).then_inc(used[n % RING], 1)
            pe.wait_ge(dft_act, 1)
            f3 = qr[:, :].rearrange("p (t n) -> p t n", t=TT)
            for c in range(2):
                for t in range(TT):
                    m = mm(bank[4 + c][:, :], f3[:, t, c * P:(c + 1) * P], cst("dft", t * 2 * T, 2 * T), start=t == 0, stop=t == TT - 1)
            m.then_inc(dft_pe, 1)
            pe.wait_ge(dft_act, 2)
            for c in range(2):
                mm(bank[6 + c][:, 0:T], cst("cd"), soft[:, c, 0:T], start=True, stop=False)
                m = mm(bank[6 + c][:, 0:T], cst("sd"), soft[:, c, T:2 * T], start=False, stop=True)
            m.then_inc(dft_pe, 1)
            pe.wait_ge(dft_act, 3)
            pe.wait_ge(side_loaded, 48)
            for f in range(2):
                for k in range(2):
                    m = mm(bank[4 + f][:, 0:T], wf[:, k, f * P:(f + 1) * P], prob[:, k, 0:T], start=k == 0, stop=k == 1)
            m.then_inc(dft_pe, 1)

            pe.wait_ge(dft_act, 4)
            pe.wait_ge(mix_dve, 1)
            n0 = FIRST["na"]

            def na_pair(j, first, last):
                s = slot(n0)
                r = j
                if not last:
                    wait_chunk(pe, n0, r)
                    w = chunk3(n0, 3 * P)
                    project(bank[0][:, 0:T], w, 0, hT)
                    project(bank[0][:, T:2 * T], w, P, hT)
                    if not first:
                        pe.wait_ge(na["ada_ready"], j)
                    project(bank[2][:, 0:T], w, P, hcT).then_inc(na["qk_proj"], 1)
                    if not first:
                        pe.wait_ge(na["v_ready"], j)
                    v4 = bank[1][:, :].rearrange("p (t n) -> p t n", t=4)
                    rows(v4[:, 0:2, :], w, 2 * P, P, hT)
                    rows(v4[:, 2:4, :], w, 2 * P, P, hcT).then_inc(used[n0 % RING], 1)
                if not first:
                    pe.wait_ge(na["p_ready"], j)
                    for c in range(4):
                        for kt in range(4):
                            m = nc.tensor.transpose(bank[4 + c][:, kt * P:(kt + 1) * P], prob[:, c, kt * P:(kt + 1) * P], cst("ident"))
                    m.then_inc(na["t_done"], 1)
                if not last:
                    pe.wait_ge(na["qk_ready"], j + 1)
                    ada(n0 + 1, bank[2][0:1, :], r)
                    ada(n0 + 2, bank[0][0:1, :], r)
                if not first:
                    pe.wait_ge(na["pt_act"], j)
                    pe.wait_ge(na["pt_dve"], j)
                    pe.wait_ge(na["v_ready"], j)
                    for h in range(2):
                        m = values(bank[3], h, range(4), lambda kt: ((0, T), (kt * T, (kt + 1) * T)))
                    m.then_inc(na["o_done"], 1)
                if not last:
                    pe.wait_ge(na["ada_row"], j + 1)
                    ada_columns(bank[2][:, 0:4], ada_row(0)[0:1, :], 1)
                    ada_columns(bank[2][:, 4:8], ada_row(1)[0:1, :], 1).then_inc(na["ada_done"], 1)
                    kc = qn[:, 0:T]
                    for h in range(2):
                        hp = slice(64 * h, 64 * h + 64)
                        for q in range(TT):
                            b = bank[4 + 2 * h + q]
                            mm(b[:, 0:T], qk[hp, q * P:(q + 1) * P], qk[hp, T:2 * T], start=True, stop=True)
                            m = mm(b[:, T:2 * T], qk[hp, q * P:(q + 1) * P], kc[hp, :], start=True, stop=True)
                    m.then_inc(na["scores"], 1)

            na_pair(0, True, False)
            with pe.Fori(1, NA_PAIRS) as j:
                na_pair(j, False, False)
            na_pair(NA_PAIRS, False, True)
            pe.wait_ge(na["o_ready"], NA_PAIRS)
            out_proj("out_0")

            if subs > 1:
                norm(2)
                pe.wait_ge(h_ready, KT * 3)
                rows(bank[0][:, 0:TT * (G + E)].rearrange("p (t n) -> p t n", t=TT), wr, 0, G + E, hT).then_inc(route_done, 1)
                for t in range(TT):
                    for k in range(KT):
                        m = nc.tensor.transpose(bank[4 + 2 * t + k // 4][:, k % 4 * P:(k % 4 + 1) * P], hT[:, k, t * P:(t + 1) * P], cst("ident"))
                m.then_inc(perm_pe, 1)
                pe.wait_ge(hot_ready, 1)
                hot = [rt[:, 3, t, 0:G] for t in range(TT)]
                mm(bank[1][:, 0:G], cst("before"), hot[0], start=True, stop=True)
                mm(bank[1][:, G:2 * G], cst("before"), hot[1], start=True, stop=False)
                mm(bank[1][:, G:2 * G], cst("ones"), hot[0], start=False, stop=True)
                mm(bank[1][:, 2 * G:3 * G], cst("ones"), hot[0], start=True, stop=False)
                mm(bank[1][:, 2 * G:3 * G], cst("ones"), hot[1], start=False, stop=True).then_inc(perm_pe, 1)
                pe.wait_ge(place_ready, 1)
                for t in range(TT):
                    mm(bank[0][0:E, 0:T], comb[:, t, :], place[:, t, :], start=t == 0, stop=t == TT - 1)
                for t in range(TT):
                    for q in range(TT):
                        m = nc.tensor.transpose(bank[1][:, q * T + t * P:q * T + (t + 1) * P], place[:, t, q * P:(q + 1) * P], cst("ident"))
                m.then_inc(perm_pe, 1)
                pe.wait_ge(perm_act, 1)
                for k in range(KT):
                    for t in range(TT):
                        m = mm(bank[4 + k // 2][:, k % 2 * T:(k % 2 + 1) * T], htok[:, t, k * P:(k + 1) * P], place[:, t, :],
                               start=t == 0, stop=t == TT - 1)
                m.then_inc(perm_pe, 1)
                pe.wait_ge(zeroed, 1)
                pe.wait_ge(perm_act, 3)
                pe.wait_ge(perm_dve, 1)
                n0 = FIRST["moe"]

                def zero(banks, n):
                    for b in banks:
                        mm(bank[b][:, 0:n], cst("ones"), qr[:, 0:n], start=True, stop=False, skip_group_check=True)

                def gather(g, at):
                    pe.wait_ge(win_in, g + 1)
                    if g >= 2:
                        pe.wait_ge(win_out, g - 1)
                    zero((4 + g % 2 * 2, 5 + g % 2 * 2), 4 * WIN)

                def expert(e, g, at, n):
                    x = hS if g is None else hW[g % 2]
                    pe.wait_ge(comb_sel, e + 1)
                    mm(bank[3][:, 0:n], cst("ones")[0:E, :], comb_e[:, 0:n], start=True, stop=True).then_inc(comb_bc, 1)
                    for f in range(FT_E):
                        c = n0 + f // 2
                        if f % 2 == 0:
                            wait_chunk(pe, c, e)
                        if f == 3:
                            pe.wait_ge(moe_hid, 4 * e + 1)
                        w = chunk3(c, 512)
                        for half in range(2):
                            for k in range(KT):
                                at_w = (2 * half + f % 2) * P
                                m = mm(bank[f % 3][:, half * T:half * T + n], w[:, k, at_w:at_w + P], x[:, k, 0:n],
                                       start=k == 0, stop=k == KT - 1)
                        m.then_inc(moe_gu if f % 2 == 0 else used[c % RING], 1)
                    wait_chunk(pe, n0 + 2, e)
                    w = slot(n0 + 2)[:, :].rearrange("p (k n) -> p k n", k=FT_E)
                    for k in range(FT_E):
                        pe.wait_ge(moe_hid, 4 * e + k + 1)
                        for d in range(KT):
                            if g is None:
                                dst = bank[4 + d // 2][:, d % 2 * T:(d % 2 + 1) * T]
                            else:
                                dst = bank[4 + g % 2 * 2 + d // 4][:, d % 4 * WIN:(d % 4 + 1) * WIN]
                            m = mm(dst, w[:, k, d * P:(d + 1) * P], hid[:, k, 0:n], start=False, stop=False, skip_group_check=True)
                    m.then_inc(used[(n0 + 2) % RING], 1)

                moe_branches(pe, expert, gather=gather, collect=lambda end: None if end else zero(range(4, 8), 512))
                pe.wait_ge(perm_dve, 2)
                for q in range(TT):
                    for d in range(KT):
                        m = nc.tensor.transpose(bank[2 * q + d // 4][:, d % 4 * P:(d % 4 + 1) * P], ysum[:, d, q * P:(q + 1) * P], cst("ident"))
                m.then_inc(perm_pe, 1)
                pe.wait_ge(perm_act, 4)
                pe.wait_ge(perm_dve, 3)
                for d in range(KT):
                    for q in range(TT):
                        m = mm(bank[4 + d // 2][:, d % 2 * T:(d % 2 + 1) * T], htok[:, q, d * P:(d + 1) * P], placeT[:, q, :],
                               start=q == 0, stop=q == TT - 1)
                    if d % 2:
                        m.then_inc(unperm, 1)
                norm(3)

            def sum_mods(i, half):
                if i not in layers:
                    return
                pe.wait_ge(ada_summed, 12 * i + 6 * (half + 1))
                for c in range(3 * KT):
                    at = (3 * KT * half + c) * P
                    m = mm(bank[6][:, c:c + 1], ada_sum[:, at:at + P], cst("ones", 0, 1), start=True, stop=True)
                m.then_inc(mods_done, 1)

            if subs > 1:
                sum_mods(0, 0)
            for i in layers:
                norm(4 + 2 * i)
                pe.wait_ge(mods_ready, 3 + 2 * i)
                sum_mods(i, 1)
                x0 = KT * (4 + 2 * i)
                n0 = FIRST[f"pair_{i}"]
                base = epoch(i)

                def sb_pair(step, r, first=False, last=False):
                    j = step + RING * r + base
                    n = n0 + step
                    if not last:
                        wait_chunk(pe, n, r)
                        w = chunk3(n, 3 * P)
                        project(bank[0][:, 0:T], w, 0, hT, x0 if first else None)
                        project(bank[0][:, T:2 * T], w, P, hT).then_inc(sk["qk_proj"], 1)
                    if not first:
                        pe.wait_ge(sk["sp_ready"], j)
                        for h in range(2):
                            sp_ = soft[:, 2 + h, :]
                            mm(bank[6 + h][:, 0:T], cst("suffix"), sp_[:, 0:T], start=True, stop=False, skip_group_check=True)
                            mm(bank[6 + h][:, P:T], cst("ones"), sp_[:, T:TRI], start=False, stop=True, skip_group_check=True)
                            m = mm(bank[6 + h][:, T:TRI], cst("suffix"), sp_[:, T:TRI], start=True, stop=True, skip_group_check=True)
                        m.then_inc(sk["suffix"], 1)
                    if not last:
                        pe.wait_ge(sk["v_ready"], j)
                        rows(bank[1][:, 0:T].rearrange("p (t n) -> p t n", t=TT), w, 2 * P, P, hT).then_inc(used[n % RING], 1)
                    if not first:
                        pe.wait_ge(sk["v_ready"], j)
                        pe.wait_ge(sk["a_ready"], j)
                        for h in range(2):
                            m = values(bank[3], h, range(TT), tri)
                        m.then_inc(sk["o_done"], 1)
                    if not last:
                        pe.wait_ge(sk["qk_ready"], j + 1)
                        for h in range(2):
                            hp = slice(64 * h, 64 * h + 64)
                            mm(bank[4 + h][:, 0:T], qk[hp, T:T + P], qk[hp, 0:T], start=True, stop=True)
                            m = mm(bank[4 + h][:, T:TRI], qk[hp, T + P:2 * T], qk[hp, P:T], start=True, stop=True)
                        m.then_inc(sk["scores"], 1)

                def sf_pair(step, r, first=False, last=False):
                    j = step + RING * r + base
                    n = n0 + step
                    if not last:
                        wait_chunk(pe, n, r)
                        w = chunk3(n, 3 * P)
                        project(bank[0][:, 0:T], w, 0, hT, x0 if first else None)
                    if not first:
                        pe.wait_ge(sf["qr_ready"], j)
                        for h in range(2):
                            hp = slice(64 * h, 64 * h + 64)
                            mm(bank[4 + h][:, 0:P], qr[hp, 0:P], qr[hp, T:T + P], start=True, stop=True)
                            m = mm(bank[4 + h][:, P:TRI], qr[hp, P:T], qr[hp, T:2 * T], start=True, stop=True)
                        m.then_inc(sf["scores"], 1)
                    if not last:
                        project(bank[0][:, T:2 * T], w, P, hT).then_inc(sf["qk_proj"], 1)
                        pe.wait_ge(sf["v_ready"], j)
                        v2 = bank[1][:, 0:T].rearrange("p (t n) -> p t n", t=TT)
                        rows(v2, w, 2 * P, P, hT, 0, 1)
                        pe.wait_ge(sf["raw"], 2 * j + 2)
                        mm(bank[2][:, :], cst("headones"), xsq[:, 0:2, :], start=True, stop=True).then_inc(sf["ssum"], 1)
                        rows(v2, w, 2 * P, P, hT, 1, 2).then_inc(used[n % RING], 1)
                    if not first:
                        pe.wait_ge(sf["p_ready"], j)
                        for h in range(2):
                            for c in range(3):
                                m = nc.tensor.transpose(bank[6 + h][:, c * P:(c + 1) * P], prob[:, h, c * P:(c + 1) * P], cst("ident"))
                        m.then_inc(sf["t_done"], 1)
                    if not last:
                        pe.wait_ge(sf["qn_ready"], 2 * j + 2)
                        mm(bank[2][:, :], cst("rot"), qn[:, :], start=True, stop=True).then_inc(sf["rot"], 1)
                    if not first:
                        pe.wait_ge(sf["v_ready"], j)
                        pe.wait_ge(sf["pt_act"], j)
                        pe.wait_ge(sf["pt_dve"], j)
                        for h in range(2):
                            m = values(bank[3], h, range(TT), tri)
                        m.then_inc(sf["o_done"], 1)

                pair = sb_pair if KINDS[i] == "sb" else sf_pair
                pair(0, 0, first=True)
                steps(pe, 1, PAIRS, pair)
                pair(PAIRS, 0, last=True)
                pe.wait_ge((sk if KINDS[i] == "sb" else sf)["o_ready"], base + PAIRS)
                out_proj(f"out_{i + 1}")
                if 3 + 2 * i >= subs:
                    break

                norm(5 + 2 * i)
                sum_mods(i + 1, 0)
                x1 = KT * (5 + 2 * i)
                n0 = FIRST[f"gu_{i}"]

                def gate_up(step, r):
                    n = n0 + step
                    s = step % RING
                    wait_chunk(pe, n, r)
                    if step >= RING:
                        pe.wait_ge(ffn_hid, GU * i + step - (RING - 1) + RING * r)
                    w = chunk3(n, 512)
                    for half in range(2):
                        for f in range(2):
                            m = project(bank[2 * s + half][:, f * T:(f + 1) * T], w, half * 2 * P + f * P, hT,
                                        x1 if (step, half, f) == (0, 0, 0) else None)
                    m.then_inc(used[n % RING], 1)

                for step in range(RING):
                    gate_up(step, 0)
                steps(pe, RING, GU, gate_up)
                n1 = FIRST[f"down_{i}"]
                pe.wait_ge(ffn_hid, GU * (i + 1))

                def down(step, r):
                    n = n1 + step
                    wait_chunk(pe, n, r)
                    if step >= RING - 1:
                        pe.wait_ge(x_done, KT * (3 + 2 * i) + step - (RING - 1) + RING * r)
                    w = slot(n)[:, 0:FT * P].rearrange("p (k n) -> p k n", k=FT)
                    b = bank[5 + step % RING]
                    for k in range(FT):
                        m = mm(b[:, 0:T], w[:, k, :], hid[:, k, :], start=k == 0, stop=k == FT - 1)
                    m.then_inc(used[n % RING], 1)

                for step in range(2):
                    down(step, 0)
                steps(pe, 2, KT, down)

        @block.scalar
        def _(act):
            A = nc.scalar.activation

            def copy(o, i):
                return nc.scalar.copy(o, i)

            def norm(e, src, ready, out_t, g, shift):
                for k in range(KT):
                    if ready:
                        act.wait_ge(ready[0], ready[1] + (k + 1) * ready[2])
                    A(xsq[:, k, :], src[:, k, :], ACT.Square).then_inc(sq_ready, 1)
                act.wait_ge(ssq_done, e + 1)
                A(lnms, norm_bank(e)[:, 0:T], ACT.Ln, scale=1.0 / D, bias=cst("eps")).then_inc(ln_ms, 1)
                act.wait_ge(ln_ms, e + 1)
                A(rinv[:, :], lnms, ACT.Exp, scale=-0.5).then_inc(rinv_ready, 1)
                for k in range(KT):
                    act.wait_ge(xn_ready, KT * e + k + 1)
                    A(out_t[:, k, :], xn[:, k, :], ACT.Identity, scale=g(k), bias=shift(k)).then_inc(h_ready, 1)

            act.wait_ge(loaded, 16)
            A(csilu[:, :], vc("c"), ACT.Silu).then_inc(silu_done, 1)
            A(c2silu[:, :], vc("c2"), ACT.Silu).then_inc(silu_done, 1)

            def gcol(i):
                return lambda k: gain[:, i, k:k + 1]

            def scol(t, lo):
                return lambda k: t[:, lo + k:lo + k + 1]

            for e, src, src_loaded in ((0, ctxT, ctx_loaded), (1, xT, x_loaded)):
                act.wait_ge(src_loaded, 16)
                if e == 0:
                    act.wait_ge(const_loaded, 16)
                else:
                    act.wait_ge(ssq_done, 1)
                for k in range(KT):
                    A(xsq[:, k, :], src[:, k, :], ACT.Square).then_inc(sq_ready, 1)
                act.wait_ge(ssq_done, e + 1)
                A(qn[:, T:2 * T], bank[3][:, 0:T], ACT.Ln, scale=1.0 / D, bias=cst("eps")).then_inc(ln_ms, 1)
                act.wait_ge(ln_ms, e + 1)
                A(rinv2[e], qn[:, T:2 * T], ACT.Exp, scale=-0.5).then_inc(rinv_ready, 1)
            act.wait_ge(mods_ready, 1)
            for e, dst, g, shift in ((0, hcT, gcol(1), scol(modc, 0)), (1, hT, gcol(0), scol(mod, 0))):
                for k in range(KT):
                    act.wait_ge(xn_ready, KT * e + k + 1)
                    A(dst[:, k, :], xn[:, k, :], ACT.Identity, scale=g(k), bias=shift(k)).then_inc(h_ready, 1)

            act.wait_ge(mix_proj, 1)
            copy(qr[:, :], bank[0][:, :]).then_inc(dft_act, 1)
            act.wait_ge(mix_proj, 2)
            copy(gact[0][:, :, :], bank[2][:, :].rearrange("p (t n) -> p t n", t=2)).then_inc(mix_act, 1)
            act.wait_ge(dft_pe, 1)
            copy(soft[:, 0, :], bank[4][:, :])
            copy(soft[:, 1, :], bank[5][:, :]).then_inc(dft_act, 1)
            act.wait_ge(dft_pe, 2)
            copy(prob[:, 0, 0:T], bank[6][:, 0:T])
            copy(prob[:, 1, 0:T], bank[7][:, 0:T]).then_inc(dft_act, 1)
            act.wait_ge(dft_pe, 3)
            copy(mixT[:, 0, :], bank[4][:, 0:T])
            copy(mixT[:, 1, :], bank[5][:, 0:T]).then_inc(dft_act, 1)

            def na_pair(j, first, last):
                if not first:
                    act.wait_ge(na["m_ready"], j)
                    for c in range(4):
                        m = A(prob[:, c, :], soft[:, c, :], ACT.Exp, bias=stat[:, 1, c:c + 1], accum_out=stat[:, 2, c:c + 1])
                    m.then_inc(na["e_ready"], 1)
                if not last:
                    act.wait_ge(na["qk_proj"], j + 1)
                    copy(qk[:, :], bank[0][:, :])
                    copy(qn[:, 0:T], bank[2][:, 0:T]).then_inc(na["qk_ready"], 1)
                if not first:
                    act.wait_ge(na["t_done"], j)
                    for q in range(2):
                        m = copy(probT[:, 0, :].rearrange("p (k q n) -> p k q n", k=4, q=2)[:, :, q, :],
                                 bank[4 + q][:, :].rearrange("p (k n) -> p k n", k=4))
                    m.then_inc(na["pt_act"], 1)
                    act.wait_ge(na["o_done"], j)
                    copy(mixT[:, 1 + j, :], bank[3][:, 0:T]).then_inc(na["o_ready"], 1)

            na_pair(0, True, False)
            with act.Fori(1, NA_PAIRS) as j:
                na_pair(j, False, False)
            na_pair(NA_PAIRS, False, True)

            if subs > 1:
                act.wait_ge(mods_ready, 2)
                norm(2, xT, (x_done, 0, 1), hT, gcol(2), scol(mod, 3 * KT))
                act.wait_ge(hot_ready, 1)
                A(rt[:, 4, :, 0:G], rt[:, 0, :, 0:G], ACT.Exp).then_inc(route_act, 1)
                act.wait_ge(top_ready, 1)
                A(small[:, 8, :], small[:, 7, :], ACT.Exp).then_inc(route_act, 1)
                act.wait_ge(perm_pe, 1)
                for b in range(4):
                    m = copy(htok[:, b // 2, b % 2 * 512:(b % 2 + 1) * 512], bank[4 + b][:, :])
                m.then_inc(perm_act, 1)
                act.wait_ge(perm_pe, 3)
                copy(placeT, bank[1][:, :].rearrange("p (q t) -> p q t", q=TT)).then_inc(perm_act, 1)
                act.wait_ge(perm_pe, 4)
                for b in range(2):
                    m = copy(hS[:, 2 * b:2 * b + 2, :], pair_of(bank[4 + b]))
                m.then_inc(perm_act, 1)

                def expert(e, g, at, n):
                    for f in range(FT_E):
                        if f % 2 == 0:
                            act.wait_ge(moe_gu, 2 * e + f // 2 + 1)
                        else:
                            wait_used(act, FIRST["moe"] + f // 2, e)
                        A(gact[f % 3][:, 0, 0:n], bank[f % 3][:, 0:n], ACT.Silu).then_inc(moe_silu, 1)

                moe_branches(act, expert)
                act.wait_ge(perm_pe, 5)
                for b in range(2):
                    m = copy(htok[:, b // 2, b % 2 * 512:(b % 2 + 1) * 512], bank[b][:, :])
                m.then_inc(perm_act, 1)
                norm(3, xT, (x_done, KT, 1), xT, lambda k: vc("normf", k, 1), lambda k: cst("zero"))

            for i in layers:
                if i == 0:
                    ready = (h_ready, KT * 3, 1)
                else:
                    ready = (x_done, KT * (1 + 2 * i), 1)
                act.wait_ge(mods_ready, 3 + 2 * i)
                norm(4 + 2 * i, xT, ready, hT, gcol(0), scol(mod, 0))
                base = epoch(i)

                def sb_pair(step, r, first=False, last=False):
                    j = step + RING * r + base
                    lne = prob[:, 0:2, 0:TRI]
                    if not first:
                        act.wait_ge(sk["zm_ready"], j)
                        A(lne, soft[:, 0:2, 0:TRI], ACT.Abs).then_inc(sk["abs"], 1)
                        act.wait_ge(sk["abs"], j)
                        A(lne, lne, ACT.Exp, scale=-1.0).then_inc(sk["exp"], 1)
                        act.wait_ge(sk["exp"], j)
                        A(lne, lne, ACT.Ln, bias=1.0).then_inc(sk["ln"], 1)
                    if not last:
                        act.wait_ge(sk["qk_proj"], j + 1)
                        copy(qk[:, :], bank[0][:, :]).then_inc(sk["qk_ready"], 1)
                    if not first:
                        act.wait_ge(sk["w_ready"], j)
                        A(probT[:, :, 0:TRI], prob[:, 2:4, 0:TRI], ACT.Exp).then_inc(sk["a_ready"], 1)
                        act.wait_ge(sk["o_done"], j)
                        copy(mixT[:, j - 1 - base, :], bank[3][:, 0:T]).then_inc(sk["o_ready"], 1)

                def sf_pair(step, r, first=False, last=False):
                    j = step + RING * r + base
                    if not first:
                        act.wait_ge(sf["m_ready"], j)
                        for h in range(2):
                            for q in range(2):
                                cols = slice(0, P) if q == 0 else slice(P, TRI)
                                c = 2 * h + q
                                A(prob[:, h, cols], soft[:, h, cols], ACT.Exp, bias=stat[:, 1, c:c + 1],
                                  accum_out=stat[:, 2, c:c + 1])
                        act.wait_ge(sf["sink_in"], j)
                        A(stat[:, 5, :], stat[:, 4, :], ACT.Exp).then_inc(sf["e_ready"], 1)
                    if not last:
                        act.wait_ge(sf["qk_proj"], j + 1)
                        b2 = bank[0][:, :].rearrange("p (t n) -> p t n", t=2)
                        copy(qk[:, :], bank[0][:, :]).then_inc(sf["raw"], 1)
                        A(xsq[:, 0:2, :], b2, ACT.Square).then_inc(sf["raw"], 1)
                        act.wait_ge(sf["ssum"], j + 1)
                        A(xn[:, 0:2, :], bank[2][:, :].rearrange("p (t n) -> p t n", t=2), ACT.Ln, scale=1.0 / HD,
                          bias=cst("eps")).then_inc(sf["ln"], 1)
                        act.wait_ge(sf["ln"], j + 1)
                        A(xn[:, 2:4, :], xn[:, 0:2, :], ACT.Exp, scale=-0.5).then_inc(sf["rinv"], 1)
                    if not first:
                        act.wait_ge(sf["t_done"], j)
                        copy(probT[:, 0, 0:TRI], bank[6][:, 0:TRI]).then_inc(sf["pt_act"], 1)
                        act.wait_ge(sf["o_done"], j)
                        copy(mixT[:, j - 1 - base, :], bank[3][:, 0:T]).then_inc(sf["o_ready"], 1)

                pair = sb_pair if KINDS[i] == "sb" else sf_pair
                pair(0, 0, first=True)
                steps(act, 1, PAIRS, pair)
                pair(PAIRS, 0, last=True)
                if 3 + 2 * i >= subs:
                    break
                act.wait_ge(mods_ready, 4 + 2 * i)
                norm(5 + 2 * i, xT, (x_done, KT * (2 + 2 * i), 1), hT, gcol(2), scol(mod, 3 * KT))
                n0 = FIRST[f"gu_{i}"]

                def silu(step, r):
                    s = step % RING
                    wait_used(act, n0 + step, r)
                    A(gact[s][:, :, :], bank[2 * s][:, :].rearrange("p (t n) -> p t n", t=2), ACT.Silu).then_inc(ffn_silu, 1)

                for step in range(RING):
                    silu(step, 0)
                steps(act, RING, GU, silu)

        @block.vector
        def _(dve):
            V = nc.vector
            count = {}

            def then(ins, s):
                count[s] = count.get(s, 0) + 1
                ins.then_inc(CH[s], 1)
                dve.wait_ge(CH[s], count[s])

            CH = {"mods": mods_step, "route": route_step}

            def normalise(e):
                dve.wait_ge(rinv_ready, e + 1)
                for k in range(KT):
                    V.tensor_tensor(xn[:, k, :], xT[:, k, :], rinv[:, :], ALU.mult).then_inc(xn_ready, 1)

            def update(c, f, n, a, g):
                if f < 3:
                    dve.wait_ge(y_done, 6 * a + 3 * c + f + 1)
                else:
                    wait_used(dve, n)
                d = 4 * c + f
                V.scalar_tensor_tensor(xT[:, d, :], bank[(4 + d) % 8][:, 0:T], mod[:, g * KT + d:g * KT + d + 1], xT[:, d, :],
                                       ALU.mult, ALU.add).then_inc(x_done, 1)

            def normalise_in(e, src):
                dve.wait_ge(rinv_ready, e + 1)
                for k in range(KT):
                    if e == 1:
                        dve.wait_ge(h_ready, k + 1)
                    V.tensor_tensor(xn[:, k, :], src[:, k, :], rinv2[e], ALU.mult).then_inc(xn_ready, 1)

            for n in range(N_HEAD):
                if n == 2:
                    normalise_in(0, ctxT)
                wait_used(dve, n)
                V.tensor_copy(ada_row(n)[0:2, :], bank[4 + n][0:2, :]).then_inc(ada_rows, 1)
            dve.wait_ge(ada_cols, 1)
            m2 = bank[2][:, 0:4 * KT].rearrange("p (m c) -> p m c", c=2)
            then(V.tensor_tensor(mod[:, 0:2 * KT], m2[:, :, 0], vc("b_ada", 0, 2 * KT), ALU.add), "mods")
            then(V.tensor_tensor(modc[:, :], m2[:, :, 1], vc("b_ada", 0, 2 * KT), ALU.add), "mods")
            V.scalar_tensor_tensor(gain[:, 0, :], mod[:, KT:2 * KT], 1.0, vc("norm1"), ALU.add, ALU.mult)
            V.scalar_tensor_tensor(gain[:, 1, :], modc[:, KT:2 * KT], 1.0, vc("norm1"), ALU.add, ALU.mult).then_inc(mods_ready, 1)
            normalise_in(1, xT)

            n = FIRST["mix"] + 1
            wait_used(dve, n)
            dve.wait_ge(mix_act, 1)
            ch, cv = gact[1], gact[2]
            then(V.tensor_tensor(ch[:, :, :], gact[0][:, :, :], bank[3][:, :].rearrange("p (t n) -> p t n", t=2), ALU.mult), "mods")
            for f in range(2):
                tap = [vc("w_conv", 3 * f + t, 1) for t in range(3)]
                then(V.tensor_scalar(cv[:, f, :], ch[:, f, :], tap[1], None, ALU.mult), "mods")
                then(V.scalar_tensor_tensor(cv[:, f, 1:T], ch[:, f, 0:T - 1], tap[0], cv[:, f, 1:T], ALU.mult, ALU.add), "mods")
                then(V.scalar_tensor_tensor(cv[:, f, 0:T - 1], ch[:, f, 1:T], tap[2], cv[:, f, 0:T - 1], ALU.mult, ALU.add), "mods")
            V.tensor_tensor(mixT[:, 6:8, :], cv[:, :, :], bank[1][:, :].rearrange("p (t n) -> p t n", t=2), ALU.mult).then_inc(mix_dve, 1)

            def row_softmax_in(k, j):
                dve.wait_ge(k["mx"], j)
                V.tensor_scalar(stat[:, 1, :], stat[:, 0, :], -1.0, None, ALU.mult).then_inc(k["m_ready"], 1)

            def na_pair(j, first, last):
                if not first:
                    dve.wait_ge(na["scores"], j)
                    for c in range(4):
                        V.scalar_tensor_tensor(soft[:, c, 0:T], bank[4 + c][:, 0:T], SCALE, bias[:, c % 2, 2 * (j - 1) + c // 2, :],
                                               ALU.mult, ALU.add)
                        m = V.tensor_scalar(soft[:, c, T:2 * T], bank[4 + c][:, T:2 * T], SCALE, None, ALU.mult)
                    m.then_inc(na["s_ready"], 1)
                    dve.wait_ge(na["s_ready"], j)
                    V.tensor_reduce(stat[:, 0, :], soft[:, :, :], AX.X, ALU.max).then_inc(na["mx"], 1)
                    row_softmax_in(na, j)
                    dve.wait_ge(na["e_ready"], j)
                    V.reciprocal(stat[:, 3, :], stat[:, 2, :]).then_inc(na["rs"], 1)
                    dve.wait_ge(na["rs"], j)
                    for c in range(4):
                        m = V.tensor_scalar(prob[:, c, :], prob[:, c, :], stat[:, 3, c:c + 1], None, ALU.mult)
                    m.then_inc(na["p_ready"], 1)
                    dve.wait_ge(na["t_done"], j)
                    for q in range(2):
                        m = V.tensor_copy(probT[:, 1, :].rearrange("p (k q n) -> p k q n", k=4, q=2)[:, :, q, :],
                                          bank[6 + q][:, :].rearrange("p (k n) -> p k n", k=4))
                    m.then_inc(na["pt_dve"], 1)
                if not last:
                    wait_used(dve, FIRST["na"] + 1, j)
                    V.tensor_copy(ada_row(0)[0:1, :], bank[2][0:1, :])
                    wait_used(dve, FIRST["na"] + 2, j)
                    V.tensor_copy(ada_row(1)[0:1, :], bank[0][0:1, :]).then_inc(na["ada_row"], 1)
                    if not first:
                        dve.wait_ge(na["o_done"], j)
                    wait_used(dve, FIRST["na"], j)
                    V.tensor_copy(vv[:, :, :], bank[1][:, :].rearrange("p (t n) -> p t n", t=4)).then_inc(na["v_ready"], 1)
                    dve.wait_ge(na["ada_done"], j + 1)
                    V.tensor_tensor(mod[:, bass.ds(2 * KT + 8 * j, 8)], bank[2][:, 0:8],
                                    vec[:, bass.ds(VEC["b_ada"][0] + 2 * KT + 8 * j, 8)], ALU.add).then_inc(na["ada_ready"], 1)

            dve.wait_ge(bias_masked, 1)
            na_pair(0, True, False)
            with dve.Fori(1, NA_PAIRS) as j:
                na_pair(j, False, False)
            na_pair(NA_PAIRS, False, True)
            dve.wait_ge(na["ada_ready"], NA_PAIRS)
            V.scalar_tensor_tensor(gain[:, 2, :], mod[:, 4 * KT:5 * KT], 1.0, vc("norm2"), ALU.add, ALU.mult).then_inc(mods_ready, 1)
            for c in range(2):
                for f in range(4):
                    update(c, f, FIRST["out_0"] + c, 0, 2)

            if subs > 1:
                V.memset(qr[:, :], 0.0).then_inc(zeroed, 1)
                normalise(2)
                dve.wait_ge(route_done, 1)
                R = lambda i, n=E: rt[:, i, :, 0:n]
                S = lambda i: small[:, i, :]
                B = lambda a, n: a.unsqueeze(2).broadcast_to([P, TT, n])
                iota = lambda n: cst("iota", 0, n).unsqueeze(1).broadcast_to([P, TT, n])
                then(V.tensor_tensor(logit[:, :, :], bank[0][:, 0:TT * (G + E)].rearrange("p (t n) -> p t n", t=TT),
                                     vc("b_route").unsqueeze(1).broadcast_to([P, TT, G + E]), ALU.add), "route")

                def first_max(x, mx, eq, idx, hot, n):
                    then(V.tensor_reduce(mx, x, AX.X, ALU.max), "route")
                    then(V.tensor_tensor(eq, x, B(mx, n), ALU.is_equal), "route")
                    then(V.tensor_scalar(eq, eq, -64.0, None, ALU.mult), "route")
                    then(V.tensor_tensor(eq, eq, iota(n), ALU.add), "route")
                    then(V.tensor_reduce(idx, eq, AX.X, ALU.min), "route")
                    then(V.tensor_tensor(hot, eq, B(idx, n), ALU.is_equal), "route")

                lg = logit[:, :, 0:G]
                first_max(lg, S(0), R(1, G), S(1), R(3, G), G)
                V.tensor_tensor(R(0, G), lg, B(S(0), G), ALU.subtract).then_inc(hot_ready, 1)
                then(V.tensor_scalar(R(5, G), R(3, G), -NEG, NEG, ALU.mult, ALU.add), "route")
                then(V.tensor_tensor(R(6).rearrange("p t (g e) -> p t g e", g=G),
                                     logit[:, :, G:G + E].rearrange("p t (g e) -> p t g e", g=G),
                                     R(5, G).unsqueeze(3).broadcast_to([P, TT, G, EG]), ALU.add), "route")
                first_max(R(6), S(4), R(1), S(5), R(7), E)
                then(V.tensor_scalar(R(8), R(7), 2 * NEG, None, ALU.mult), "route")
                then(V.tensor_tensor(R(8), R(8), R(6), ALU.add), "route")
                first_max(R(8), S(6), R(1), S(5), R(9), E)
                V.tensor_tensor(S(7), S(6), S(4), ALU.subtract).then_inc(top_ready, 1)
                dve.wait_ge(route_act, 1)
                then(V.tensor_reduce(S(2), R(4, G), AX.X, ALU.add), "route")
                then(V.reciprocal(S(3), S(2)), "route")
                dve.wait_ge(route_act, 2)
                then(V.tensor_scalar(S(9), S(8), 1.0, None, ALU.add), "route")
                then(V.reciprocal(S(10), S(9)), "route")
                then(V.tensor_tensor(S(11), S(10), S(3), ALU.mult), "route")
                then(V.tensor_tensor(S(12), S(11), S(8), ALU.mult), "route")
                then(V.tensor_tensor(R(10), R(7), B(S(11), E), ALU.mult), "route")
                then(V.tensor_tensor(R(11), R(9), B(S(12), E), ALU.mult), "route")
                then(V.tensor_tensor(comb[:, :, :], R(10), R(11), ALU.add), "route")
                dve.wait_ge(perm_pe, 2)
                then(V.tensor_copy(gcount[:, 0, :], bank[1][:, 2 * G:3 * G]), "route")
                then(V.memset(gcount[:, 1, :], 0.0), "route")
                for g in range(1, G):
                    then(V.tensor_tensor(gcount[:, 1, g:g + 1], gcount[:, 1, g - 1:g], gcount[:, 0, g - 1:g], ALU.add), "route")
                then(V.tensor_reduce(gcount[:, 2, 0:1], gcount[:, 0, :], AX.X, ALU.max), "route")
                then(V.tensor_scalar(win[:, 0:G], gcount[:, 1, :], float(T - WIN), None, ALU.min), "route")
                V.tensor_scalar(win[:, G:G + 1], gcount[:, 2, 0:1], float(WIN), None, ALU.is_le).then_inc(win_ready, 1)
                for t in range(TT):
                    then(V.tensor_tensor(rt[:, 4, t, 0:G], bank[1][:, t * G:(t + 1) * G], gcount[:, 1, :], ALU.add), "route")
                then(V.tensor_tensor(R(4, G), R(4, G), R(3, G), ALU.mult), "route")
                then(V.tensor_reduce(S(13), R(4, G), AX.X, ALU.add), "route")
                for t in range(TT):
                    m = V.tensor_scalar(place[:, t, :], cst("iota"), small[:, 13, t:t + 1], None, ALU.is_equal)
                m.then_inc(place_ready, 1)
                dve.wait_ge(perm_pe, 3)
                V.tensor_copy(combT[:, :], bank[0][0:E, 0:T]).then_inc(comb_ready, 1)
                dve.wait_ge(perm_pe, 4)
                for b in range(2, 4):
                    m = V.tensor_copy(hS[:, 2 * b:2 * b + 2, :], pair_of(bank[4 + b]))
                m.then_inc(perm_dve, 1)
                dve.wait_ge(comb_ready, 1)

                V.memset(ysum[:, :, :], 0.0).then_inc(win_zero, 1)

                def window(g):
                    return dve.value_load(win[0:1, g:g + 1], min_val=0, max_val=T - WIN)

                def gather(g, at):
                    if g == 0:
                        dve.wait_ge(perm_act, 3)
                        dve.wait_ge(perm_dve, 1)
                    V.tensor_copy(hW[g % 2], hS[:, :, bass.ds(at, WIN)]).then_inc(win_in, 1)

                def scatter(g, at):
                    wait_used(dve, FIRST["moe"] + 2, EG * (g + 1) - 1)
                    if g == 0:
                        dve.wait_ge(win_zero, 1)
                    else:
                        dve.wait_ge(win_out, g)
                    for b in range(2):
                        yb = ysum[:, 4 * b:4 * b + 4, bass.ds(at, WIN)]
                        m = V.tensor_tensor(yb, yb, bank[4 + g % 2 * 2 + b][:, 0:4 * WIN].rearrange("p (d n) -> p d n", d=4), ALU.add)
                    m.then_inc(win_out if g < G - 1 else perm_dve, 1)

                def collect(end):
                    if end:
                        wait_used(dve, FIRST["moe"] + 3 * E - 1)
                        for b in range(4):
                            m = V.tensor_copy(ysum[:, 2 * b:2 * b + 2, :], pair_of(bank[4 + b]))
                        m.then_inc(perm_dve, 1)

                def expert(e, g, at, n):
                    src = combT[:, :] if g is None else combT[:, bass.ds(at, n)]
                    V.tensor_scalar(comb_e[:, 0:n], src, const[0:E, bass.ds(CONST["ident"][0] + e, 1)], None,
                                    ALU.mult).then_inc(comb_sel, 1)
                    for f in range(FT_E):
                        dve.wait_ge(moe_silu, 4 * e + f + 1)
                        V.tensor_tensor(gact[f % 3][:, 1, 0:n], gact[f % 3][:, 0, 0:n], bank[f % 3][:, T:T + n], ALU.mult).then_inc(moe_mul, 1)
                        dve.wait_ge(moe_mul, 4 * e + f + 1)
                        if f == 0:
                            dve.wait_ge(comb_bc, e + 1)
                            wait_used(dve, FIRST["moe"] + 2 - RING, e)
                        V.tensor_tensor(hid[:, f, 0:n], gact[f % 3][:, 1, 0:n], bank[3][:, 0:n], ALU.mult).then_inc(moe_hid, 1)

                moe_branches(dve, expert, window, gather, scatter, collect)
                dve.wait_ge(perm_pe, 5)
                for b in range(2, 4):
                    m = V.tensor_copy(htok[:, b // 2, b % 2 * 512:(b % 2 + 1) * 512], bank[b][:, :])
                m.then_inc(perm_dve, 1)
                for d in range(KT):
                    dve.wait_ge(unperm, d // 2 + 1)
                    V.scalar_tensor_tensor(xT[:, d, :], bank[4 + d // 2][:, (d % 2) * T:(d % 2 + 1) * T],
                                           mod[:, 5 * KT + d:5 * KT + d + 1], xT[:, d, :], ALU.mult, ALU.add).then_inc(x_done, 1)
                normalise(3)

            def take_mods(i, half):
                if i not in layers:
                    return
                dve.wait_ge(mods_done, 2 * i + half + 1)
                lo = 3 * KT * half
                then(V.tensor_tensor(mod[:, lo:lo + 3 * KT], bank[6][:, 0:3 * KT], vc("b_ada2", MODS * i + lo, 3 * KT), ALU.add), "mods")
                V.scalar_tensor_tensor(gain[:, 2 * half, :], mod[:, lo + KT:lo + 2 * KT], 1.0, vc("gains2", (2 * i + half) * KT, KT),
                                       ALU.add, ALU.mult).then_inc(mods_ready, 1)

            take_mods(0, 0)
            for i in layers:
                normalise(4 + 2 * i)
                take_mods(i, 1)
                n0 = FIRST[f"pair_{i}"]
                base = epoch(i)

                def values(k, step, r, j, first):
                    if not first:
                        dve.wait_ge(k["o_done"], j)
                    wait_used(dve, n0 + step, r)
                    V.tensor_copy(vv[:, 0:2, :], bank[1][:, 0:T].rearrange("p (t n) -> p t n", t=TT)).then_inc(k["v_ready"], 1)

                def sb_pair(step, r, first=False, last=False):
                    j = step + RING * r + base
                    mask = cst("mask_sb")
                    if not first:
                        dve.wait_ge(sk["scores"], j)
                        for h in range(2):
                            m = V.scalar_tensor_tensor(soft[:, h, 0:TRI], bank[4 + h][:, 0:TRI], SCALE, mask, ALU.mult, ALU.add)
                        m.then_inc(sk["zm_ready"], 1)
                        dve.wait_ge(sk["ln"], j)
                        V.scalar_tensor_tensor(soft[:, 2:4, 0:TRI], soft[:, 0:2, 0:TRI], 0.0, prob[:, 0:2, 0:TRI],
                                               ALU.max, ALU.add).then_inc(sk["sp_ready"], 1)
                        dve.wait_ge(sk["suffix"], j)
                        for h in range(2):
                            m = V.tensor_tensor(prob[:, 2 + h, 0:TRI], soft[:, h, 0:TRI], bank[6 + h][:, 0:TRI], ALU.subtract)
                        m.then_inc(sk["w_ready"], 1)
                    if not last:
                        values(sk, step, r, j, first)

                def sf_pair(step, r, first=False, last=False):
                    j = step + RING * r + base
                    kind = KINDS[i]
                    mask = cst("mask_" + kind)
                    if not first:
                        dve.wait_ge(sf["scores"], j)
                        for h in range(2):
                            m = V.scalar_tensor_tensor(soft[:, h, 0:TRI], bank[4 + h][:, 0:TRI], SCALE, mask, ALU.mult, ALU.add)
                        m.then_inc(sf["s_ready"], 1)
                        dve.wait_ge(sf["s_ready"], j)
                        V.tensor_reduce(stat[:, 6, 0:4:2], soft[:, 0:2, 0:P], AX.X, ALU.max)
                        V.tensor_reduce(stat[:, 6, 1:4:2], soft[:, 0:2, P:TRI], AX.X, ALU.max).then_inc(sf["mx"], 1)
                        dve.wait_ge(sf["mx"], j)
                        sink = (j - 1 - base) * 4
                        snk = vec[:, bass.ds(VEC["sinks"][0] + 4 * PAIRS * (kind == "moba") + sink, 4)]
                        V.tensor_tensor(stat[:, 0, :], stat[:, 6, :], snk, ALU.max).then_inc(sf["rs"], 1)
                        dve.wait_ge(sf["rs"], 3 * j - 2)
                        V.tensor_scalar(stat[:, 1, :], stat[:, 0, :], -1.0, None, ALU.mult).then_inc(sf["m_ready"], 1)
                        V.tensor_tensor(stat[:, 4, :], snk, stat[:, 0, :], ALU.subtract).then_inc(sf["sink_in"], 1)
                        dve.wait_ge(sf["e_ready"], j)
                        V.tensor_tensor(stat[:, 7, :], stat[:, 2, :], stat[:, 5, :], ALU.add).then_inc(sf["rs"], 1)
                        dve.wait_ge(sf["rs"], 3 * j - 1)
                        V.reciprocal(stat[:, 3, :], stat[:, 7, :]).then_inc(sf["rs"], 1)
                        dve.wait_ge(sf["rs"], 3 * j)
                        for h in range(2):
                            V.tensor_scalar(prob[:, h, 0:P], prob[:, h, 0:P], stat[:, 3, 2 * h:2 * h + 1], None, ALU.mult)
                            m = V.tensor_scalar(prob[:, h, P:TRI], prob[:, h, P:TRI], stat[:, 3, 2 * h + 1:2 * h + 2], None, ALU.mult)
                        m.then_inc(sf["p_ready"], 1)
                    if not last:
                        dve.wait_ge(sf["rinv"], j + 1)
                        for c in range(2):
                            V.scalar_tensor_tensor(qn[:, c * T:(c + 1) * T], qk[:, c * T:(c + 1) * T], vc("qk_" + kind, c, 1),
                                                   xn[:, 2 + c, :], ALU.mult, ALU.mult).then_inc(sf["qn_ready"], 1)
                        dve.wait_ge(sf["qn_ready"], 2 * j + 2)
                        V.tensor_tensor(xn[:, 4:6, :], qn[:, :].rearrange("p (c n) -> p c n", c=2),
                                        cst("cos").unsqueeze(1).broadcast_to([P, 2, T]), ALU.mult).then_inc(sf["rope"], 1)
                    if not first:
                        dve.wait_ge(sf["t_done"], j)
                        V.tensor_copy(probT[:, 1, 0:TRI], bank[7][:, 0:TRI]).then_inc(sf["pt_dve"], 1)
                    if not last:
                        dve.wait_ge(sf["rot"], j + 1)
                        V.tensor_tensor(xn[:, 6:8, :], bank[2][:, :].rearrange("p (c n) -> p c n", c=2),
                                        cst("sin").unsqueeze(1).broadcast_to([P, 2, T]), ALU.mult).then_inc(sf["rope"], 1)
                        dve.wait_ge(sf["rope"], 2 * j + 2)
                        V.tensor_tensor(qr[:, :].rearrange("p (c n) -> p c n", c=2), xn[:, 4:6, :], xn[:, 6:8, :],
                                        ALU.add).then_inc(sf["qr_ready"], 1)
                        values(sf, step, r, j, first)

                pair = sb_pair if KINDS[i] == "sb" else sf_pair
                pair(0, 0, first=True)
                steps(dve, 1, PAIRS, pair)
                pair(PAIRS, 0, last=True)
                for c in range(2):
                    for f in range(4):
                        update(c, f, FIRST[f"out_{i + 1}"] + c, 1 + i, 2)
                if 3 + 2 * i >= subs:
                    break
                normalise(5 + 2 * i)
                take_mods(i + 1, 0)

                def gate_up(step, r):
                    s = step % RING
                    dve.wait_ge(ffn_silu, GU * i + step + 1 + RING * r)
                    V.tensor_tensor(hid[:, bass.ds(2 * step + 2 * RING * r, 2), :], gact[s][:, :, :],
                                    bank[2 * s + 1][:, :].rearrange("p (t n) -> p t n", t=2), ALU.mult).then_inc(ffn_hid, 1)

                for step in range(RING):
                    gate_up(step, 0)
                steps(dve, RING, GU, gate_up)

                def down(step, r):
                    wait_used(dve, FIRST[f"down_{i}"] + step, r)
                    d = step + RING * r
                    x = xT[:, bass.ds(d, 1), :]
                    V.scalar_tensor_tensor(x, bank[5 + step % RING][:, 0:T].unsqueeze(1), mod[:, bass.ds(5 * KT + d, 1)], x,
                                           ALU.mult, ALU.add).then_inc(x_done, 1)

                for step in range(2):
                    down(step, 0)
                steps(dve, 2, KT, down)


def constants():
    i, t = np.arange(P), np.arange(T)
    col = {}
    col["ident"] = np.eye(P)
    col["ones"] = np.ones((P, P))
    col["headones"] = i[:, None] // HD == i[None, :] // HD
    half, d = HD // 2, i % HD
    rot = np.zeros((P, P))
    lo = i[d < half]
    rot[lo + half, lo] = -1.0
    rot[lo, lo + half] = 1.0
    col["rot"] = rot
    col["suffix"] = i[:, None] >= i[None, :]
    f = np.float32
    inv = f(1.0) / (f(10000.0) ** (np.arange(0, HD, 2, dtype=f) / f(HD)))
    ang = (t.astype(f)[:, None] * inv[None, :]).astype(f)
    col["cos"] = np.cos(ang)[:, d % half].T
    col["sin"] = np.sin(ang)[:, d % half].T
    k, q = i[:, None], t[None, :]
    sb = [k < q, k + P < q[:, P:]]
    col["mask_sb"] = np.where(np.concatenate(sb, 1), 0.0, NEG)
    rows = [(i[:, None] + a, np.arange(n)[None, :]) for a, n in ((0, P), (P, T))]
    col["mask_moba"] = np.where(np.concatenate([kk <= qq for qq, kk in rows], 1), 0.0, NEG)
    col["mask_swa"] = np.where(np.concatenate([(kk <= qq) & (qq - kk < P) for qq, kk in rows], 1), 0.0, NEG)
    qc, kc = i[:, None] % GRID_W, t[None, :] % GRID_W
    start = np.clip(qc - NA_KW // 2, 0, GRID_W - NA_KW)
    col["mask_na"] = np.where((kc >= start) & (kc < start + NA_KW), 0.0, NEG)
    w = 2 * np.pi * ((t[:, None] * t[None, :]) % T) / T
    dft = np.stack([np.cos(w), np.sin(w)], 1).reshape(TT, P, 2, T)
    col["dft"] = dft.transpose(1, 0, 2, 3).reshape(P, -1)
    same = i[:, None] // HD == i[None, :] // HD
    w = 2 * np.pi * ((d[:, None] * d[None, :]) % HD) / HD
    norm = 1.0 / np.sqrt(T * HD)
    col["cd"] = np.where(same, np.cos(w) * norm, 0.0)
    col["sd"] = np.where(same, -np.sin(w) * norm, 0.0)
    col["iota"] = np.broadcast_to(np.arange(T), (P, T))
    col["before"] = i[:, None] < i[None, :]
    col["eps"] = np.full((P, 1), EPS)
    col["zero"] = np.zeros((P, 1))
    out = np.zeros((P, N_CONST), np.float32)
    for name, (a, b) in CONST.items():
        out[:, a:b] = col[name]
    return out


def cols(v):
    v = np.asarray(v)
    return np.ascontiguousarray(np.moveaxis(v.reshape(*v.shape[:-1], -1, P), -1, 0)).reshape(P, -1)


def by_row(w, lo, n):
    return w[:, lo:lo + n].reshape(-1, P, n).transpose(1, 0, 2)


def lay_out(a):
    f = {k: np.asarray(v) for k, v in a.items()}
    o = {"const": constants()}
    rep = lambda v: np.broadcast_to(v, (P,) + v.shape)
    sinks = np.repeat(f["swa_sinks_2"][0], 2)
    o["vec"] = np.concatenate([
        np.stack([cols(f["c"][0]), cols(f["c_ctx"])], 2).reshape(P, -1), cols(f["c_2"][0]),
        cols(f["norm1"][0]), cols(f["norm2"][0]), cols(f["norm_final"]),
        f["w_conv"][0].reshape(3, 2, P).transpose(2, 1, 0).reshape(P, -1), cols(f["b_ada"][0]),
        cols(f["norm_gain_2"]), cols(f["ada_b_2"]),
        np.tile(f["moba_qk_gain_2"][0].T, (2, 1)), np.tile(f["swa_qk_gain_2"][0].T, (2, 1)),
        rep(sinks), np.full((P, 4 * PAIRS), NEG, np.float32),
        rep(np.concatenate([f["b_rg"][0], f["b_re"][0]]))], 1)
    o["xT"] = f["x"][0].T.reshape(KT, P, T).transpose(1, 0, 2)
    o["ctxT"] = f["ctx"][0].T.reshape(KT, P, T).transpose(1, 0, 2)
    ada = [by_row(f["w_ada"][0], 512 * n, 512) for n in range(MODS // 4)]
    o["ada_head"] = np.stack(ada[:N_HEAD])
    w = f["w_in"][0]
    q, k, v, gb, gc, h = (256, 768, 1280, 1792, 2048, 2304)
    o["mix"] = np.stack([np.concatenate([by_row(w, a_, 256), by_row(w, b_, 256)], 2) for a_, b_ in ((0, gb), (gc, h))])
    na = []
    for j in range(NA_PAIRS):
        pair = np.concatenate([by_row(w, at + P * j, P) for at in (q, k, v)], 2).reshape(P, -1)
        na += [np.concatenate([pair, np.zeros((P, SLOT - pair.shape[1]), np.float32)], 1)]
        na += [x.reshape(P, -1) for x in ada[N_HEAD + 2 * j:N_HEAD + 2 * j + 2]]
    o["na"] = np.stack(na)
    outs = [f["w_out"][0], f["sb_w_out_2"][0], f["moba_w_out_2"][0], f["swa_w_out_2"][0], f["sb_w_out_2"][1]]
    for n, w in enumerate(outs):
        o[f"out_{n}"] = np.stack([by_row(w, 512 * c, 512) for c in range(2)])
    o["wf"] = by_row(f["w_fourier"][0], 0, 256)
    o["wr"] = np.concatenate([by_row(f["w_rg"][0], 0, G), by_row(f["w_re"][0], 0, E)], 2)
    t = np.arange(T)
    row = t[None, :] // GRID_W - t[:, None] // GRID_W + NA_KH - 1
    coff = np.clip(t[None, :] % GRID_W - t[:, None] % GRID_W + NA_KW - 1, 0, 2 * NA_KW - 2)
    o["bias"] = f["rpb"][0][:, row, coff].reshape(NA_HEADS, TT, P, T).transpose(2, 1, 0, 3)
    o["moe"] = np.stack([x for e in range(E) for x in (
        *(np.concatenate([by_row(f[n][0, e], 2 * P * c, 2 * P) for n in ("w_gate", "w_up")], 2).reshape(P, -1) for c in range(2)),
        by_row(f["w_down"][0, e], 0, D).reshape(P, -1))])
    o["ada2"] = np.stack([by_row(f["ada_w_2"][i], 512 * n, 512) for i in range(LAYERS) for n in range(12)])
    swa = f["swa_w_in_2"][0]
    for i, kind in enumerate(KINDS):
        ch = []
        for j in range(PAIRS):
            if kind == "swa":
                g = j * 2 // PAIRS
                kk, vv_ = by_row(swa, D + HD * g, HD), by_row(swa, D + P + HD * g, HD)
                parts = [by_row(swa, P * j, P), kk, kk, vv_, vv_]
            else:
                w = f["moba_w_in_2"][0] if kind == "moba" else f["sb_w_in_2"][i // 3]
                parts = [by_row(w, at + P * j, P) for at in (0, D, 2 * D)]
            ch.append(np.concatenate(parts, 2))
        o[f"pair_{i}"] = np.stack(ch)
        g_, u_, d_ = f["ffn_w_gate_2"][i], f["ffn_w_up_2"][i], f["ffn_w_down_2"][i]
        o[f"gu_{i}"] = np.stack([np.concatenate([by_row(g_, 256 * n, 256), by_row(u_, 256 * n, 256)], 2) for n in range(GU)])
        o[f"down_{i}"] = np.stack([by_row(d_, P * n, P) for n in range(KT)])
    shape = {name: (n, P, width) for name, n, width in PHASES}
    shape["ada2"] = (LAYERS * 12, P, SLOT)
    return {k: np.ascontiguousarray(v.reshape(shape.get(k, v.shape))) for k, v in o.items()}


def kernel(**inputs):
    import concourse.bacc as bacc
    from concourse.bass_utils import run_bass_kernel_spmd

    nc = bacc.Bacc("TRN2", target_bir_lowering=False, num_devices=1)
    arrays = {f"in_{k}": v for k, v in lay_out(inputs).items()}
    ins = {k: nc.dram_tensor("in_" + k, arrays["in_" + k].shape, F32, kind="ExternalInput").ap() for k in
           [n[3:] for n in arrays]}
    out = nc.dram_tensor("out_xT", (P, KT, T), F32, kind="ExternalOutput").ap()
    build(nc, ins, out)
    r = run_bass_kernel_spmd(nc, [arrays], core_ids=[0])
    y = np.asarray(r.results[0]["out_xT"])
    return np.ascontiguousarray(y.transpose(2, 1, 0)).reshape(1, T, D)
```

```python
from contextlib import ExitStack

import numpy as np
import concourse.bass as bass
from concourse import mybir

F32 = mybir.dt.float32
F32R = mybir.dt.float32r
ALU = mybir.AluOpType
ACT = mybir.ActivationFunctionType
AX = mybir.AxisListType

P = 128
D = 1024
KT = D // P
T = 256
TT = T // P
HD = 64
SCALE = HD ** -0.5
EPS = 1e-6
NEG = -1e30
GRID_W, NA_KW, NA_KH = 64, 16, 8
NA_HEADS = 8
NA_PAIRS = NA_HEADS // 2
PAIRS = D // (2 * HD)
G, EG = 4, 8
E = G * EG
FE = 512
FT_E = FE // P
DFF = 2816
FT = DFF // P
GU = FT // 2
MODS = 6 * KT
RING = 3
SLOT = 4096
TRI = 3 * P
LAYERS = 4
WIN = 96
KINDS = ("sb", "moba", "swa", "sb")

CONST = {}
_at = 0
for _name, _n in (("ident", P), ("ones", P), ("headones", P), ("rot", P), ("suffix", P), ("cos", T), ("sin", T),
                  ("mask_sb", TRI), ("mask_moba", TRI), ("mask_swa", TRI), ("mask_na", T),
                  ("dft", TT * 2 * T), ("cd", P), ("sd", P), ("iota", T), ("before", P), ("eps", 1), ("zero", 1)):
    CONST[_name] = (_at, _at + _n)
    _at += _n
N_CONST = _at

VEC = {}
_at = 0
for _name, _n in (("c", KT * 2), ("c2", KT), ("norm1", KT), ("norm2", KT), ("normf", KT), ("w_conv", 2 * 3),
                  ("b_ada", MODS), ("gains2", LAYERS * 2 * KT), ("b_ada2", LAYERS * MODS), ("qk_moba", 2),
                  ("qk_swa", 2), ("sinks", 8 * PAIRS), ("b_route", G + E)):
    VEC[_name] = (_at, _at + _n)
    _at += _n
N_VEC = _at

N_HEAD = 4
PHASES = (
    [("ada_head", N_HEAD, SLOT), ("mix", 2, SLOT), ("na", 3 * NA_PAIRS, SLOT), ("out_0", 2, SLOT), ("moe", 3 * E, SLOT)]
    + [ph for i in range(LAYERS) for ph in
       ((f"pair_{i}", PAIRS, 3 * KT * P), (f"out_{i + 1}", 2, SLOT), (f"gu_{i}", GU, SLOT), (f"down_{i}", KT, FT * P))]
)
FIRST = {}
_at = 0
for _name, _n, _ in PHASES:
    FIRST[_name] = _at
    _at += _n


def build(nc, ins, out, subs=2 + 2 * LAYERS):
    layers = [i for i in range(LAYERS) if 2 + 2 * i < subs]
    phases = PHASES[:[4, 5][min(subs, 2) - 1]] + PHASES[5:5 + 2 * max(0, subs - 2)]
    ctx = ExitStack()
    with ctx:
        offset = {}

        def sb(name, shape):
            offset[name] = -(-nc.sbuf_base // 32) * 32
            return ctx.enter_context(nc.sbuf_tensor(name, shape, F32))

        def as_parts(name, shape):
            return nc.alloc_sbuf_tensor_at(name + "_parts", shape, F32R, offset=offset[name])

        def sem(name):
            return ctx.enter_context(nc.semaphore(name))

        const = sb("const_sb", [P, N_CONST])
        vec = sb("vec_sb", [P, N_VEC])
        ring = [sb(f"ring{s}", [P, SLOT]) for s in range(RING)]
        ada_ring = [sb(f"ada_ring{s}", [P, SLOT]) for s in range(2)]
        ada_sum = sb("ada_sum", [P, MODS * P])
        xT = sb("xT", [P, KT, T])
        xsq = sb("xsq", [P, KT, T])
        xn = sb("xn", [P, KT, T])
        hT = sb("hT", [P, KT, T])
        rinv = sb("rinv", [P, T])
        mixT = sb("mixT", [P, KT, T])
        work = sb("work", [P, 3, 4 * 2 * T])
        gact = [sb(f"gact{s}", [P, 2, T]) for s in range(RING)]
        mod = sb("mod", [P, MODS])
        modc = sb("modc", [P, 2 * KT])
        gain = sb("gain", [P, 3, KT])
        csilu = sb("csilu", [P, 2 * KT])
        c2silu = sb("c2silu", [P, KT])
        qk = sb("qk", [P, 2 * T])
        qn = sb("qn", [P, 2 * T])
        qr = sb("qr", [P, 2 * T])
        vv = sb("vv", [P, 4, P])
        stat = sb("stat", [P, 8, 4])
        wf = sb("wf", [P, 2, T])
        wr = sb("wr", [P, KT, G + E])
        logit = sb("logit", [P, TT, G + E])
        small = sb("small", [P, 16, TT])
        comb = sb("comb", [P, TT, E])
        combT = sb("combT", [E, T])
        comb_e = sb("comb_e", [E, T])
        gcount = sb("gcount", [P, 3, G])
        win = ctx.enter_context(nc.sbuf_tensor("win", [P, G + 1], mybir.dt.int32))
        bank = [ctx.enter_context(nc.psum_tensor(f"bank{i}", [P, 512], F32)) for i in range(8)]

        soft = work[:, 0, :].rearrange("p (c n) -> p c n", c=4)
        prob = work[:, 1, :].rearrange("p (c n) -> p c n", c=4)
        probT = work[:, 2, :].rearrange("p (h n) -> p h n", h=2)
        rt = work[:, 0, 0:12 * TT * E].rearrange("p (i t e) -> p i t e", i=12, t=TT)
        lnms = xn[:, KT - 1, :]
        rinv2 = [qn[:, 0:T], rinv[:, :]]
        flat = lambda t: t[:, :, :].rearrange("p k t -> p (k t)")
        parts = (0, 7, 14, 18, FT)
        QUARTER = SLOT // 4

        def split_views(ring, xsq, xn, hT, mixT, work, qk, qn, qr, vv):
            v = {"xsq": xsq, "hT": hT}
            v["whi"] = [(mixT if f < 2 else xn)[:, 4 * (f % 2):4 * (f % 2) + 4, :].rearrange("p a (b n) -> p (a b) n", n=P) for f in range(4)]
            v["whd"] = [b[:, 0:P * (hi - lo)] for b, lo, hi in zip(
                (flat(mixT)[:, 0:4 * T], flat(mixT)[:, 4 * T:], flat(vv), flat(work)[:, FT * T:]), parts, parts[1:])]
            v["hid_hi"] = [b[:, :].rearrange("p (t n) -> p t n", t=2) for b in (qk, qn, qr)] + [
                b[:, 2 * c:2 * c + 2, :] for b in (xn, hT) for c in range(4)]
            v["hid"] = flat(work)[:, 0:FT * T].rearrange("p (f t) -> p f t", f=FT)
            v["hW"] = [[flat(t)[:, h * KT * WIN:(h + 1) * KT * WIN].rearrange("p (k n) -> p k n", k=KT) for h in range(2)] for t in (xn, hT)]
            v["ehi"] = [flat(work)[:, (1 + f) * QUARTER:(2 + f) * QUARTER] for f in range(4)]
            v["hidT"] = [flat(work)[:, h * FT_E * WIN:(h + 1) * FT_E * WIN] for h in range(2)]
            v["w_gu"] = lambda n, f: ring[n % RING][:, :].rearrange("p (k n) -> p k n", k=KT)[:, :, f * P:(f + 1) * P]
            v["w_down"] = lambda n, f: ring[n % RING][:, parts[f] * P:parts[f + 1] * P]
            v["quarter"] = lambda n, f: ring[n % RING][:, f * QUARTER:(f + 1) * QUARTER]
            return v

        full = split_views(ring, xsq, xn, hT, mixT, work, qk, qn, qr, vv)
        part = split_views([as_parts(f"ring{s}", [P, SLOT]) for s in range(RING)],
                           *(as_parts(n, [P, KT, T]) for n in ("xsq", "xn", "hT", "mixT")), as_parts("work", [P, 3, 4 * 2 * T]),
                           *(as_parts(n, [P, 2 * T]) for n in ("qk", "qn", "qr")), as_parts("vv", [P, 4, P]))
        hid = full["hid"]

        hS = mixT
        htok = xn[:, :, :].rearrange("p k t -> p (k t)").rearrange("p (t d) -> p t d", t=TT)
        ywin = flat(work)[0:WIN, 5 * QUARTER:6 * QUARTER]
        wcomb = comb
        ysum = xsq
        place = qk[:, :].rearrange("p (t n) -> p t n", t=TT)
        placeT = qn[:, :].rearrange("p (t n) -> p t n", t=TT)
        hcT = ada_sum[:, 0:KT * T].rearrange("p (k t) -> p k t", k=KT)
        ctxT = ada_sum[:, KT * T:2 * KT * T].rearrange("p (k t) -> p k t", k=KT)
        b16 = ada_ring[0][:, :].rearrange("p (c n) -> p c n", n=T)
        bias = b16.rearrange("p (q h) n -> p q h n", q=TT)

        def cst(name, lo=0, n=None):
            a, b = CONST[name]
            return const[:, a + lo:(a + lo + n) if n else b]

        def vc(name, lo=0, n=None):
            a, b = VEC[name]
            return vec[:, a + lo:(a + lo + n) if n else b]

        landed = [sem(f"landed{s}") for s in range(RING)]
        used = [sem(f"used{s}") for s in range(RING)]
        loaded, const_loaded, ctx_loaded, x_loaded, side_loaded = (
            sem(n) for n in ("loaded", "const_loaded", "ctx_loaded", "x_loaded", "side_loaded"))
        ada_landed = [sem(f"ada_landed{s}") for s in range(2)]
        ada_prod, ada_half, ada_quarter, ada_summed = (sem(n) for n in ("ada_prod", "ada_half", "ada_quarter", "ada_summed"))
        ada_rows, ada_cols = sem("ada_rows"), sem("ada_cols")
        silu_done, mods_done, mods_step, mods_ready = (sem(n) for n in ("silu_done", "mods_done", "mods_step", "mods_ready"))
        sq_ready, ssq_done, ln_ms, rinv_ready, xn_ready, h_ready = (
            sem(n) for n in ("sq_ready", "ssq_done", "ln_ms", "rinv_ready", "xn_ready", "h_ready"))
        y_done, x_done = sem("y_done"), sem("x_done")
        bias_masked = sem("bias_masked")
        mix_proj, mix_act, mix_dve, dft_pe, dft_act = (sem(n) for n in ("mix_proj", "mix_act", "mix_dve", "dft_pe", "dft_act"))
        na = {n: sem("na_" + n) for n in (
            "qk_proj", "qk_ready", "v_ready", "scores", "s_ready", "mx", "m_ready", "e_ready", "rs", "p_ready",
            "t_done", "pt_act", "pt_dve", "o_done", "o_ready", "ada_row", "ada_done", "ada_ready")}
        sk = {n: sem("sb_" + n) for n in (
            "qk_proj", "qk_ready", "v_ready", "scores", "zm_ready", "abs", "exp", "ln", "sp_ready", "suffix",
            "w_ready", "a_ready", "o_done", "o_ready")}
        sf = {n: sem("sf_" + n) for n in (
            "qk_proj", "raw", "ssum", "ln", "rinv", "qn_ready", "rope", "rot", "qr_ready", "v_ready", "scores",
            "s_ready", "mx", "m_ready", "sink_in", "sink_e", "e_ready", "den", "rs", "p_ready", "t_done", "pt_act", "pt_dve",
            "o_done", "o_ready")}
        route_done, route_act, route_step, hot_ready, top_ready, win_ready, place_ready, comb_ready = (
            sem(n) for n in ("route_done", "route_act", "route_step", "hot_ready", "top_ready", "win_ready", "place_ready", "comb_ready"))
        perm_pe, perm_act, perm_dve, unperm = (sem(n) for n in ("perm_pe", "perm_act", "perm_dve", "unperm"))
        comb_sel, comb_bc, moe_gu, moe_silu, moe_mul, moe_hid = (
            sem(n) for n in ("comb_sel", "comb_bc", "moe_gu", "moe_silu", "moe_mul", "moe_hid"))
        win_hi, quarter_hi, quarter_lo, quarter_done, e_silu, e_hidden, e_turned, e_hi, e_lo, y_taken, y_turned, w_turned, w_taken = (
            sem(n) for n in ("win_hi", "quarter_hi", "quarter_lo", "quarter_done", "e_silu", "e_hidden", "e_turned", "e_hi", "e_lo",
                             "y_taken", "y_turned", "w_turned", "w_taken"))
        zeroed, win_in, win_out, win_zero = sem("zeroed"), sem("win_in"), sem("win_out"), sem("win_zero")
        w_hi, w_lo, h_hi, h_lo, f_hi, f_lo, tile_done = (
            sem(n) for n in ("w_hi", "w_lo", "h_hi", "h_lo", "f_hi", "f_lo", "tile_done"))
        ffn_silu, ffn_hid = sem("ffn_silu"), sem("ffn_hid")
        stored = sem("stored")

        block = ctx.enter_context(nc.Block())

        def slot(n):
            return ring[n % RING]

        def split_count(i, step, down=False):
            return (GU + KT) * i + (GU if down else 0) + step

        def wait_chunk(eng, n, r=0):
            eng.wait_ge(landed[n % RING], 16 * (n // RING + 1) + 16 * r)

        def wait_used(eng, n, r=0):
            eng.wait_ge(used[n % RING], n // RING + 1 + r)

        def steps(eng, lo, hi, body):
            rounds = (hi - lo) // RING
            if rounds >= 2:
                with eng.Fori(0, rounds) as r:
                    for s in range(RING):
                        body(lo + s, r)
            else:
                rounds = 0
            for step in range(lo + RING * rounds, hi):
                body(step, 0)

        def pair_of(b):
            return b[:, :].rearrange("p (t n) -> p t n", t=2)

        def moe_branches(eng, expert, win_expert, window=None, gather=None, scatter=None, collect=None):
            eng.wait_ge(win_ready, 1)
            fits = eng.value_load(win[0:1, G:G + 1], min_val=0, max_val=1)
            with eng.If(fits == 1):
                at = window(0) if window else 0
                if gather:
                    gather(0, at)
                for g in range(G):
                    with eng.Fori(0, EG) as i:
                        win_expert(EG * g + i, g)
                    at_before = at
                    if g < G - 1:
                        at = window(g + 1) if window else 0
                        if gather:
                            gather(g + 1, at)
                    if scatter:
                        scatter(g, at_before)
            with eng.Else():
                if collect:
                    collect(False)
                with eng.Fori(0, E) as e:
                    expert(e)
                if collect:
                    collect(True)

        def ada_row(n):
            return gact[n][:, :, :].rearrange("p a n -> p (a n)") if n < RING else qr[:, :]

        def norm_bank(e):
            return bank[4 if e == 2 or e > 4 and e % 2 else 3]

        def epoch(layer):
            kind = KINDS[layer] == "sb"
            return PAIRS * sum((KINDS[i] == "sb") == kind for i in range(layer))

        @block.sync
        def _(sp):
            sp.dma_start(vec[:, :], ins["vec"]).then_inc(loaded, 16)
            between = [(ctxT, ins["ctxT"], ctx_loaded), (const[:, :], ins["const"], const_loaded), (xT[:, :, :], ins["xT"], x_loaded)]
            for name, count, width in phases:
                n0 = FIRST[name]

                def load(step, r):
                    if n0 + step >= RING:
                        wait_used(sp, n0 + step - RING, r)
                    sp.dma_start(slot(n0 + step)[:, 0:width], ins[name][step + RING * r]).then_inc(landed[(n0 + step) % RING], 16)

                if name == "ada_head":
                    for step in range(count):
                        load(step, 0)
                        for dst, src, landed_in in between[step:step + 1]:
                            sp.dma_start(dst, src).then_inc(landed_in, 16)
                else:
                    steps(sp, 0, count, load)
            sp.wait_ge(x_done, KT * subs)
            if subs == 2:
                sp.wait_ge(h_ready, KT * 4)
            sp.dma_start(out, xT[:, :, :]).then_inc(stored, 16)
            sp.wait_ge(stored, 16)

        @block.gpsimd
        def _(pool):
            pool.dma_start(wf[:, :, :], ins["wf"]).then_inc(side_loaded, 16)
            pool.dma_start(wr[:, :, :], ins["wr"]).then_inc(side_loaded, 16)
            pool.dma_start(bias, ins["bias"]).then_inc(side_loaded, 16)
            pool.wait_ge(side_loaded, 48)
            pool.wait_ge(const_loaded, 16)
            nc.gpsimd.tensor_tensor(b16, b16, cst("mask_na").unsqueeze(1).broadcast_to([P, TT * NA_HEADS, T]),
                                    ALU.add).then_inc(bias_masked, 1)
            if not layers:
                return
            pool.wait_ge(silu_done, 2)
            chunks = MODS * P // 512
            def load(c, s):
                pool.dma_start(ada_ring[s][:, :], ins["ada2"][c]).then_inc(ada_landed[s], 16)

            def chunk(n, s, loads, col):
                w3 = ada_ring[s][:, :].rearrange("p (k n) -> p k n", k=KT)
                pool.wait_ge(ada_landed[s], 16 * loads)
                nc.gpsimd.tensor_tensor(w3, w3, c2silu[:, :].unsqueeze(2).broadcast_to([P, KT, 512]),
                                        ALU.mult).then_inc(ada_prod, 1)
                pool.wait_ge(ada_prod, n + 1)
                nc.gpsimd.tensor_tensor(w3[:, 0:4, :], w3[:, 0:4, :], w3[:, 4:8, :], ALU.add).then_inc(ada_half, 1)
                pool.wait_ge(ada_half, n + 1)
                nc.gpsimd.tensor_tensor(w3[:, 0:2, :], w3[:, 0:2, :], w3[:, 2:4, :], ALU.add).then_inc(ada_quarter, 1)
                pool.wait_ge(ada_quarter, n + 1)
                nc.gpsimd.tensor_tensor(ada_sum[:, bass.ds(col, 512)], w3[:, 0, :], w3[:, 1, :],
                                        ALU.add).then_inc(ada_summed, 1)
                pool.wait_ge(ada_summed, n + 1)

            early = chunks - 4
            load(4, 1)
            pool.wait_ge(h_ready, KT)
            with pool.Fori(0, early - 1) as r:
                chunk(r, 1, 1 + r, 4 * 512 + 512 * r)
                load(5 + r, 1)
            chunk(early - 1, 1, early, (chunks - 1) * 512)
            wait_used(pool, FIRST["out_0"] - RING)
            pool.wait_ge(na["p_ready"], NA_PAIRS)
            for c in range(2):
                load(c, c)
            for c in range(4):
                chunk(early + c, c % 2, c // 2 + 1 + (early if c % 2 else 0), 512 * c)
                if c < 2:
                    load(c + 2, c)
                else:
                    if layers[-1] > 0:
                        load(chunks + c - 2, c - 2)

            for i in layers[1:]:
                for half in range(2):
                    pool.wait_ge(mods_done, 2 * i - 1 + half)
                    c0 = chunks * i + chunks // 2 * half
                    with pool.Fori(0, chunks // 4 - 1) as r:
                        for s in range(2):
                            c = c0 + s
                            chunk(c + 2 * r, s, c // 2 + 1 + (4 if s else -4) + r, 512 * (c % chunks) + 1024 * r)
                            load(c + 2 + 2 * r, s)
                    for s in range(2):
                        c = c0 + chunks // 2 - 2 + s
                        chunk(c, s, c // 2 + 1 + (4 if s else -4), 512 * (c % chunks))
                        if (i, half) != (layers[-1], 1):
                            load(c + 2, s)

        @block.tensor
        def _(pe):
            mm = nc.tensor.matmul

            def norm(e):
                b = norm_bank(e)
                for k in range(KT):
                    pe.wait_ge(sq_ready, KT * e + k + 1)
                    m = mm(b[:, 0:T], cst("ones"), xsq[:, k, :], start=k == 0, stop=k == KT - 1)
                m.then_inc(ssq_done, 1)

            def project(dst, w, lo, h, ready=None):
                for k in range(KT):
                    if ready is not None:
                        pe.wait_ge(h_ready, ready + k + 1)
                    m = mm(dst, w[:, k, lo:lo + P], h[:, k, :], start=k == 0, stop=k == KT - 1)
                return m

            def rows(dst, w, lo, n, h, t0=0, t1=TT):
                for t in range(t0, t1):
                    for k in range(KT):
                        m = mm(dst[:, t, :], h[:, k, t * P:(t + 1) * P], w[:, k, lo:lo + n], start=k == 0, stop=k == KT - 1)
                return m

            def split_product(dst, w, x, start, stop):
                for a, b in ((0, 0), (0, 1), (1, 0)):
                    m = mm(dst, w[a], x[b], start=start and (a, b) == (0, 0), stop=stop and a == 1)
                return m

            def chunk3(n, cols):
                return slot(n)[:, 0:KT * cols].rearrange("p (k n) -> p k n", k=KT)

            def out_proj(name):
                for c in range(2):
                    n = FIRST[name] + c
                    wait_chunk(pe, n)
                    w = chunk3(n, 512)
                    for f in range(4):
                        project(bank[(4 + 4 * c + f) % 8][:, 0:T], w, f * P, mixT).then_inc(y_done if f < 3 else used[n % RING], 1)

            def values(o, h, tiles, cols):
                for i, kt in enumerate(tiles):
                    (a, b), (c, d) = cols(kt)
                    m = mm(o[64 * h:64 * h + 64, a:b], vv[:, kt, 64 * h:64 * h + 64], probT[:, h, c:d],
                           start=i == 0, stop=i == len(tiles) - 1, skip_group_check=True)
                return m

            def tri(kt):
                return ((0, T), (0, T)) if kt == 0 else ((P, T), (T, TRI))

            pe.wait_ge(silu_done, 1)
            cc = csilu[:, :].rearrange("p (k c) -> p k c", c=2)

            def ada(n, dst, r=0):
                wait_chunk(pe, n, r)
                w = chunk3(n, 512)
                for k in range(KT):
                    m = mm(dst, cc[:, k, 0:dst.shape[0]], w[:, k, :], start=k == 0, stop=k == KT - 1)
                m.then_inc(used[n % RING], 1)

            def ada_columns(dst, row, c):
                for f in range(4):
                    m = mm(dst[:, c * f:c * (f + 1)], row[:, f * P:(f + 1) * P], cst("ident")[0:c, 0:c], start=True, stop=True)
                return m

            for n in range(2):
                ada(n, bank[4 + n][0:2, :])
            pe.wait_ge(const_loaded, 16)
            norm(0)
            for n in range(2, N_HEAD):
                ada(n, bank[4 + n][0:2, :])
            pe.wait_ge(ln_ms, 1)
            norm(1)
            for n in range(N_HEAD):
                pe.wait_ge(ada_rows, n + 1)
                m = ada_columns(bank[2][:, 8 * n:8 * n + 8], ada_row(n)[0:2, :], 2)
            m.then_inc(ada_cols, 1)

            n = FIRST["mix"]
            pe.wait_ge(h_ready, 2 * KT)
            wait_chunk(pe, n)
            rows(bank[0][:, :].rearrange("p (t n) -> p t n", t=TT), chunk3(n, 512), 0, T, hT).then_inc(mix_proj, 1)
            project(bank[1][:, 0:T], chunk3(n, 512), 256, hT)
            project(bank[1][:, T:2 * T], chunk3(n, 512), 384, hT).then_inc(used[n % RING], 1)
            n += 1
            wait_chunk(pe, n)
            pe.wait_ge(mods_ready, 1)
            project(bank[2][:, 0:T], chunk3(n, 512), 0, hT)
            project(bank[2][:, T:2 * T], chunk3(n, 512), 128, hT).then_inc(mix_proj, 1)
            pe.wait_ge(rinv_ready, 2)
            project(bank[3][:, 0:T], chunk3(n, 512), 256, hT)
            project(bank[3][:, T:2 * T], chunk3(n, 512), 384, hT).then_inc(used[n % RING], 1)
            pe.wait_ge(dft_act, 1)
            f3 = qr[:, :].rearrange("p (t n) -> p t n", t=TT)
            for c in range(2):
                for t in range(TT):
                    m = mm(bank[4 + c][:, :], f3[:, t, c * P:(c + 1) * P], cst("dft", t * 2 * T, 2 * T), start=t == 0, stop=t == TT - 1)
            m.then_inc(dft_pe, 1)
            pe.wait_ge(dft_act, 2)
            for c in range(2):
                mm(bank[6 + c][:, 0:T], cst("cd"), soft[:, c, 0:T], start=True, stop=False)
                m = mm(bank[6 + c][:, 0:T], cst("sd"), soft[:, c, T:2 * T], start=False, stop=True)
            m.then_inc(dft_pe, 1)
            pe.wait_ge(dft_act, 3)
            pe.wait_ge(side_loaded, 48)
            for f in range(2):
                for k in range(2):
                    m = mm(bank[4 + f][:, 0:T], wf[:, k, f * P:(f + 1) * P], prob[:, k, 0:T], start=k == 0, stop=k == 1)
            m.then_inc(dft_pe, 1)

            pe.wait_ge(dft_act, 4)
            pe.wait_ge(mix_dve, 1)
            n0 = FIRST["na"]

            def na_pair(j, first, last):
                s = slot(n0)
                r = j
                if not last:
                    wait_chunk(pe, n0, r)
                    w = chunk3(n0, 3 * P)
                    project(bank[0][:, 0:T], w, 0, hT)
                    project(bank[0][:, T:2 * T], w, P, hT)
                    if not first:
                        pe.wait_ge(na["ada_ready"], j)
                    project(bank[2][:, 0:T], w, P, hcT).then_inc(na["qk_proj"], 1)
                    if not first:
                        pe.wait_ge(na["v_ready"], j)
                    v4 = bank[1][:, :].rearrange("p (t n) -> p t n", t=4)
                    rows(v4[:, 0:2, :], w, 2 * P, P, hT)
                    rows(v4[:, 2:4, :], w, 2 * P, P, hcT).then_inc(used[n0 % RING], 1)
                if not first:
                    pe.wait_ge(na["p_ready"], j)
                    for c in range(4):
                        for kt in range(4):
                            m = nc.tensor.transpose(bank[4 + c][:, kt * P:(kt + 1) * P], prob[:, c, kt * P:(kt + 1) * P], cst("ident"))
                    m.then_inc(na["t_done"], 1)
                if not last:
                    pe.wait_ge(na["qk_ready"], j + 1)
                    ada(n0 + 1, bank[2][0:1, :], r)
                    ada(n0 + 2, bank[0][0:1, :], r)
                if not first:
                    pe.wait_ge(na["pt_act"], j)
                    pe.wait_ge(na["pt_dve"], j)
                    pe.wait_ge(na["v_ready"], j)
                    for h in range(2):
                        m = values(bank[3], h, range(4), lambda kt: ((0, T), (kt * T, (kt + 1) * T)))
                    m.then_inc(na["o_done"], 1)
                if not last:
                    pe.wait_ge(na["ada_row"], j + 1)
                    ada_columns(bank[2][:, 0:4], ada_row(0)[0:1, :], 1)
                    ada_columns(bank[2][:, 4:8], ada_row(1)[0:1, :], 1).then_inc(na["ada_done"], 1)
                    kc = qn[:, 0:T]
                    for h in range(2):
                        hp = slice(64 * h, 64 * h + 64)
                        for q in range(TT):
                            b = bank[4 + 2 * h + q]
                            mm(b[:, 0:T], qk[hp, q * P:(q + 1) * P], qk[hp, T:2 * T], start=True, stop=True)
                            m = mm(b[:, T:2 * T], qk[hp, q * P:(q + 1) * P], kc[hp, :], start=True, stop=True)
                    m.then_inc(na["scores"], 1)

            na_pair(0, True, False)
            with pe.Fori(1, NA_PAIRS) as j:
                na_pair(j, False, False)
            na_pair(NA_PAIRS, False, True)
            pe.wait_ge(na["o_ready"], NA_PAIRS)
            out_proj("out_0")

            if subs > 1:
                norm(2)
                pe.wait_ge(h_ready, KT * 3)
                rows(bank[0][:, 0:TT * (G + E)].rearrange("p (t n) -> p t n", t=TT), wr, 0, G + E, hT).then_inc(route_done, 1)
                for t in range(TT):
                    for k in range(KT):
                        m = nc.tensor.transpose(bank[4 + 2 * t + k // 4][:, k % 4 * P:(k % 4 + 1) * P], hT[:, k, t * P:(t + 1) * P], cst("ident"))
                m.then_inc(perm_pe, 1)
                pe.wait_ge(hot_ready, 1)
                hot = [rt[:, 3, t, 0:G] for t in range(TT)]
                mm(bank[1][:, 0:G], cst("before"), hot[0], start=True, stop=True)
                mm(bank[1][:, G:2 * G], cst("before"), hot[1], start=True, stop=False)
                mm(bank[1][:, G:2 * G], cst("ones"), hot[0], start=False, stop=True)
                mm(bank[1][:, 2 * G:3 * G], cst("ones"), hot[0], start=True, stop=False)
                mm(bank[1][:, 2 * G:3 * G], cst("ones"), hot[1], start=False, stop=True).then_inc(perm_pe, 1)
                pe.wait_ge(place_ready, 1)
                for t in range(TT):
                    mm(bank[0][0:E, 0:T], comb[:, t, :], place[:, t, :], start=t == 0, stop=t == TT - 1)
                for t in range(TT):
                    for q in range(TT):
                        m = nc.tensor.transpose(bank[1][:, q * T + t * P:q * T + (t + 1) * P], place[:, t, q * P:(q + 1) * P], cst("ident"))
                m.then_inc(perm_pe, 1)
                pe.wait_ge(perm_act, 1)
                for k in range(KT):
                    for t in range(TT):
                        m = mm(bank[4 + k // 2][:, k % 2 * T:(k % 2 + 1) * T], htok[:, t, k * P:(k + 1) * P], place[:, t, :],
                               start=t == 0, stop=t == TT - 1)
                m.then_inc(perm_pe, 1)
                pe.wait_ge(zeroed, 1)
                pe.wait_ge(perm_act, 3)
                pe.wait_ge(perm_dve, 1)
                n0 = FIRST["moe"]

                def zero(banks, n):
                    for b in banks:
                        mm(bank[b][:, 0:n], cst("ones"), qr[:, 0:n], start=True, stop=False, skip_group_check=True)

                def gather(g, at):
                    pe.wait_ge(comb_sel, g + 1)
                    nc.tensor.transpose(bank[3][0:WIN, 0:E], comb_e[:, 0:WIN], cst("ident")[0:E, 0:E]).then_inc(w_turned, 1)
                    pe.wait_ge(win_in, g + 1)
                    if g >= 2:
                        pe.wait_ge(win_out, g - 1)
                    zero((4 + g % 2 * 2, 5 + g % 2 * 2), 512)

                def win_expert(e, g):
                    x = part["hW"][g % 2]

                    def products(c, f):
                        n = n0 + c
                        pe.wait_ge(quarter_lo, 12 * e + 4 * c + f + 1)
                        for k in range(2):
                            for a, b in ((0, 0), (0, 1), (1, 0)):
                                wq = (part["ehi"][f], part["quarter"](n, f))[a][:, k * 512:(k + 1) * 512]
                                if c < 2:
                                    m = mm(bank[c][0:WIN, :], x[b][:, 2 * f + k, :], wq,
                                           start=(f, k, a, b) == (0, 0, 0, 0), stop=(f, k, a) == (3, 1, 1))
                                else:
                                    m = mm(bank[4 + g % 2 * 2 + k][0:WIN, :], part["hidT"][b][:, f * WIN:(f + 1) * WIN], wq,
                                           start=False, stop=False, skip_group_check=True)
                        m.then_inc(quarter_done if f < 3 else used[n % RING], 1)

                    def turn(c):
                        pe.wait_ge(e_hidden, 2 * e + c + 1)
                        for f in range(2):
                            m = nc.tensor.transpose(bank[2][:, (2 * c + f) * WIN:(2 * c + f + 1) * WIN],
                                                    gact[c][0:WIN, 1, f * P:(f + 1) * P], cst("ident")[0:WIN, 0:WIN])
                        m.then_inc(e_turned, 1)

                    for f in range(4):
                        products(0, f)
                    for f in range(4):
                        if f == 2:
                            turn(0)
                        products(1, f)
                    pe.wait_ge(e_lo, 2 * e + 1)
                    for f in range(4):
                        if f == 2:
                            turn(1)
                            pe.wait_ge(e_lo, 2 * e + 2)
                        products(2, f)

                def scatter(g, at):
                    pe.wait_ge(y_taken, g + 1)
                    for d in range(KT):
                        m = nc.tensor.transpose(bank[4 + g % 2 * 2 + d // 4][:, d % 4 * WIN:(d % 4 + 1) * WIN],
                                                ywin[:, d * P:(d + 1) * P], cst("ident")[0:WIN, 0:WIN])
                    m.then_inc(y_turned, 1)

                def expert(e):
                    pe.wait_ge(comb_sel, e + 1)
                    mm(bank[3][:, 0:T], cst("ones")[0:E, :], comb_e[:, 0:T], start=True, stop=True).then_inc(comb_bc, 1)
                    for f in range(FT_E):
                        c = n0 + f // 2
                        if f % 2 == 0:
                            wait_chunk(pe, c, e)
                        if f == 3:
                            pe.wait_ge(moe_hid, 4 * e + 1)
                        w = chunk3(c, 512)
                        for half in range(2):
                            m = project(bank[f % 3][:, half * T:(half + 1) * T], w, (2 * half + f % 2) * P, hS)
                        m.then_inc(moe_gu if f % 2 == 0 else used[c % RING], 1)
                    wait_chunk(pe, n0 + 2, e)
                    w = slot(n0 + 2)[:, :].rearrange("p (k n) -> p k n", k=FT_E)
                    for k in range(FT_E):
                        pe.wait_ge(moe_hid, 4 * e + k + 1)
                        for d in range(KT):
                            m = mm(bank[4 + d // 2][:, d % 2 * T:(d % 2 + 1) * T], w[:, k, d * P:(d + 1) * P], hid[:, k, :],
                                   start=False, stop=False, skip_group_check=True)
                    m.then_inc(used[(n0 + 2) % RING], 1)

                mm(bank[4][:, 0:1], cst("ones"), qr[:, 0:1], start=True, stop=True, skip_group_check=True).then_inc(quarter_done, 3)
                moe_branches(pe, expert, win_expert, gather=gather, scatter=scatter, collect=lambda end: None if end else zero(range(4, 8), 512))
                pe.wait_ge(perm_dve, 2)
                for q in range(TT):
                    for d in range(KT):
                        m = nc.tensor.transpose(bank[2 * q + d // 4][:, d % 4 * P:(d % 4 + 1) * P], ysum[:, d, q * P:(q + 1) * P], cst("ident"))
                m.then_inc(perm_pe, 1)
                pe.wait_ge(perm_act, 4)
                pe.wait_ge(perm_dve, 3)
                for d in range(KT):
                    for q in range(TT):
                        m = mm(bank[4 + d // 2][:, d % 2 * T:(d % 2 + 1) * T], htok[:, q, d * P:(d + 1) * P], placeT[:, q, :],
                               start=q == 0, stop=q == TT - 1)
                    if d % 2:
                        m.then_inc(unperm, 1)
                norm(3)

            def sum_mods(i, half):
                if i not in layers:
                    return
                pe.wait_ge(ada_summed, 12 * i + 6 * (half + 1) if i else 12)
                for c in range(3 * KT):
                    at = (3 * KT * half + c) * P
                    m = mm(bank[6][:, c:c + 1], ada_sum[:, at:at + P], cst("ones", 0, 1), start=True, stop=True)
                m.then_inc(mods_done, 1)

            if subs > 1:
                sum_mods(0, 0)
            for i in layers:
                norm(4 + 2 * i)
                pe.wait_ge(mods_ready, 3 + 2 * i)
                sum_mods(i, 1)
                x0 = KT * (4 + 2 * i)
                n0 = FIRST[f"pair_{i}"]
                base = epoch(i)

                def sb_pair(step, r, first=False, last=False):
                    j = step + RING * r + base
                    n = n0 + step
                    if not last:
                        wait_chunk(pe, n, r)
                        w = chunk3(n, 3 * P)
                        project(bank[0][:, 0:T], w, 0, hT, x0 if first else None)
                        project(bank[0][:, T:2 * T], w, P, hT).then_inc(sk["qk_proj"], 1)
                    if not first:
                        pe.wait_ge(sk["sp_ready"], j)
                        for h in range(2):
                            sp_ = soft[:, 2 + h, :]
                            mm(bank[6 + h][:, 0:T], cst("suffix"), sp_[:, 0:T], start=True, stop=False, skip_group_check=True)
                            mm(bank[6 + h][:, P:T], cst("ones"), sp_[:, T:TRI], start=False, stop=True, skip_group_check=True)
                            m = mm(bank[6 + h][:, T:TRI], cst("suffix"), sp_[:, T:TRI], start=True, stop=True, skip_group_check=True)
                        m.then_inc(sk["suffix"], 1)
                    if not last:
                        pe.wait_ge(sk["v_ready"], j)
                        rows(bank[1][:, 0:T].rearrange("p (t n) -> p t n", t=TT), w, 2 * P, P, hT).then_inc(used[n % RING], 1)
                    if not first:
                        pe.wait_ge(sk["v_ready"], j)
                        pe.wait_ge(sk["a_ready"], j)
                        for h in range(2):
                            m = values(bank[3], h, range(TT), tri)
                        m.then_inc(sk["o_done"], 1)
                    if not last:
                        pe.wait_ge(sk["qk_ready"], j + 1)
                        for h in range(2):
                            hp = slice(64 * h, 64 * h + 64)
                            mm(bank[4 + h][:, 0:T], qk[hp, T:T + P], qk[hp, 0:T], start=True, stop=True)
                            m = mm(bank[4 + h][:, T:TRI], qk[hp, T + P:2 * T], qk[hp, P:T], start=True, stop=True)
                        m.then_inc(sk["scores"], 1)

                def sf_pair(step, r, first=False, last=False):
                    j = step + RING * r + base
                    n = n0 + step
                    if not last:
                        wait_chunk(pe, n, r)
                        w = chunk3(n, 3 * P)
                        project(bank[0][:, 0:T], w, 0, hT, x0 if first else None)
                    if not first:
                        pe.wait_ge(sf["qr_ready"], j)
                        for h in range(2):
                            hp = slice(64 * h, 64 * h + 64)
                            mm(bank[4 + h][:, 0:P], qr[hp, 0:P], qr[hp, T:T + P], start=True, stop=True)
                            m = mm(bank[4 + h][:, P:TRI], qr[hp, P:T], qr[hp, T:2 * T], start=True, stop=True)
                        m.then_inc(sf["scores"], 1)
                    if not last:
                        project(bank[0][:, T:2 * T], w, P, hT).then_inc(sf["qk_proj"], 1)
                        pe.wait_ge(sf["v_ready"], j)
                        v2 = bank[1][:, 0:T].rearrange("p (t n) -> p t n", t=TT)
                        rows(v2, w, 2 * P, P, hT, 0, 1)
                        pe.wait_ge(sf["raw"], 2 * j + 2)
                        mm(bank[2][:, :], cst("headones"), xsq[:, 0:2, :], start=True, stop=True).then_inc(sf["ssum"], 1)
                        rows(v2, w, 2 * P, P, hT, 1, 2).then_inc(used[n % RING], 1)
                    if not first:
                        pe.wait_ge(sf["p_ready"], j)
                        for h in range(2):
                            for c in range(3):
                                m = nc.tensor.transpose(bank[6 + h][:, c * P:(c + 1) * P], prob[:, h, c * P:(c + 1) * P], cst("ident"))
                        m.then_inc(sf["t_done"], 1)
                    if not last:
                        pe.wait_ge(sf["qn_ready"], 2 * j + 2)
                        mm(bank[2][:, :], cst("rot"), qn[:, :], start=True, stop=True).then_inc(sf["rot"], 1)
                    if not first:
                        pe.wait_ge(sf["v_ready"], j)
                        pe.wait_ge(sf["pt_act"], j)
                        pe.wait_ge(sf["pt_dve"], j)
                        for h in range(2):
                            m = values(bank[3], h, range(TT), tri)
                        m.then_inc(sf["o_done"], 1)

                pair = sb_pair if KINDS[i] == "sb" else sf_pair
                pair(0, 0, first=True)
                steps(pe, 1, PAIRS, pair)
                pair(PAIRS, 0, last=True)
                pe.wait_ge((sk if KINDS[i] == "sb" else sf)["o_ready"], base + PAIRS)
                out_proj(f"out_{i + 1}")
                if 3 + 2 * i >= subs:
                    break

                norm(5 + 2 * i)
                sum_mods(i + 1, 0)
                n0 = FIRST[f"gu_{i}"]

                def gate_up(step, r):
                    n = n0 + step
                    s = step % RING
                    if step >= RING:
                        pe.wait_ge(ffn_hid, GU * i + step - (RING - 1) + RING * r)
                    for f in range(4):
                        pe.wait_ge(w_lo, 4 * split_count(i, step) + f + 1 + 4 * RING * r)
                        for k in range(KT):
                            if (step, f) == (0, 0):
                                pe.wait_ge(h_lo, KT * i + k + 1)
                            dst = bank[2 * s + f // 2][:, f % 2 * T:(f % 2 + 1) * T]
                            m = split_product(dst, (part["whi"][f][:, k, :], part["w_gu"](n, f)[:, k, :]), (part["xsq"][:, k, :], part["hT"][:, k, :]),
                                              k == 0, k == KT - 1)
                        m.then_inc(tile_done if f < 3 else used[n % RING], 1)

                for step in range(RING):
                    gate_up(step, 0)
                steps(pe, RING, GU, gate_up)
                n1 = FIRST[f"down_{i}"]

                def down(step, r):
                    n = n1 + step
                    if step >= RING - 1:
                        pe.wait_ge(x_done, KT * (3 + 2 * i) + step - (RING - 1) + RING * r)
                    b = bank[5 + step % RING]
                    for f in range(4):
                        pe.wait_ge(w_lo, 4 * split_count(i, step, True) + f + 1 + 4 * RING * r)
                        for k in range(parts[f], parts[f + 1]):
                            if step == 0:
                                pe.wait_ge(f_lo, GU * i + k // 2 + 1)
                            at = (k - parts[f]) * P
                            m = split_product(b[:, 0:T], (part["whd"][f][:, at:at + P], part["w_down"](n, f)[:, at:at + P]),
                                              (part["hid_hi"][k // 2][:, k % 2, :], part["hid"][:, k, :]), k == 0, k == FT - 1)
                        m.then_inc(tile_done if f < 3 else used[n % RING], 1)

                for step in range(2):
                    down(step, 0)
                steps(pe, 2, KT, down)

        @block.scalar
        def _(act):
            A = nc.scalar.activation

            def copy(o, i):
                return nc.scalar.copy(o, i)

            def norm(e, src, ready, out_t, g, shift, between=None, high=None):
                for k in range(KT):
                    if ready:
                        act.wait_ge(ready[0], ready[1] + (k + 1) * ready[2])
                    A(xsq[:, k, :], src[:, k, :], ACT.Square).then_inc(sq_ready, 1)
                if between:
                    between()
                act.wait_ge(ssq_done, e + 1)
                A(lnms, norm_bank(e)[:, 0:T], ACT.Ln, scale=1.0 / D, bias=cst("eps")).then_inc(ln_ms, 1)
                act.wait_ge(ln_ms, e + 1)
                A(rinv[:, :], lnms, ACT.Exp, scale=-0.5).then_inc(rinv_ready, 1)
                for k in range(KT):
                    act.wait_ge(xn_ready, KT * e + k + 1)
                    A(out_t[:, k, :], xn[:, k, :], ACT.Identity, scale=g(k), bias=shift(k)).then_inc(h_ready, 1)
                    if high is not None:
                        A(part["xsq"][:, k, :], xn[:, k, :], ACT.Identity, scale=g(k), bias=shift(k)).then_inc(h_hi, 1)

            act.wait_ge(loaded, 16)
            A(csilu[:, :], vc("c"), ACT.Silu).then_inc(silu_done, 1)
            A(c2silu[:, :], vc("c2"), ACT.Silu).then_inc(silu_done, 1)

            def gcol(i):
                return lambda k: gain[:, i, k:k + 1]

            def scol(t, lo):
                return lambda k: t[:, lo + k:lo + k + 1]

            for e, src, src_loaded in ((0, ctxT, ctx_loaded), (1, xT, x_loaded)):
                act.wait_ge(src_loaded, 16)
                if e == 0:
                    act.wait_ge(const_loaded, 16)
                else:
                    act.wait_ge(ssq_done, 1)
                for k in range(KT):
                    A(xsq[:, k, :], src[:, k, :], ACT.Square).then_inc(sq_ready, 1)
                act.wait_ge(ssq_done, e + 1)
                A(qn[:, T:2 * T], bank[3][:, 0:T], ACT.Ln, scale=1.0 / D, bias=cst("eps")).then_inc(ln_ms, 1)
                act.wait_ge(ln_ms, e + 1)
                A(rinv2[e], qn[:, T:2 * T], ACT.Exp, scale=-0.5).then_inc(rinv_ready, 1)
            act.wait_ge(mods_ready, 1)
            for e, dst, g, shift in ((0, hcT, gcol(1), scol(modc, 0)), (1, hT, gcol(0), scol(mod, 0))):
                for k in range(KT):
                    act.wait_ge(xn_ready, KT * e + k + 1)
                    A(dst[:, k, :], xn[:, k, :], ACT.Identity, scale=g(k), bias=shift(k)).then_inc(h_ready, 1)

            act.wait_ge(mix_proj, 1)
            copy(qr[:, :], bank[0][:, :]).then_inc(dft_act, 1)
            act.wait_ge(mix_proj, 2)
            copy(gact[0][:, :, :], bank[2][:, :].rearrange("p (t n) -> p t n", t=2)).then_inc(mix_act, 1)
            act.wait_ge(dft_pe, 1)
            copy(soft[:, 0, :], bank[4][:, :])
            copy(soft[:, 1, :], bank[5][:, :]).then_inc(dft_act, 1)
            act.wait_ge(dft_pe, 2)
            copy(prob[:, 0, 0:T], bank[6][:, 0:T])
            copy(prob[:, 1, 0:T], bank[7][:, 0:T]).then_inc(dft_act, 1)
            act.wait_ge(dft_pe, 3)
            copy(mixT[:, 0, :], bank[4][:, 0:T])
            copy(mixT[:, 1, :], bank[5][:, 0:T]).then_inc(dft_act, 1)

            def na_pair(j, first, last):
                if not first:
                    act.wait_ge(na["m_ready"], j)
                    for c in range(4):
                        m = A(prob[:, c, :], soft[:, c, :], ACT.Exp, bias=stat[:, 1, c:c + 1], accum_out=stat[:, 2, c:c + 1])
                    m.then_inc(na["e_ready"], 1)
                if not last:
                    act.wait_ge(na["qk_proj"], j + 1)
                    copy(qk[:, :], bank[0][:, :])
                    copy(qn[:, 0:T], bank[2][:, 0:T]).then_inc(na["qk_ready"], 1)
                if not first:
                    act.wait_ge(na["t_done"], j)
                    for q in range(2):
                        m = copy(probT[:, 0, :].rearrange("p (k q n) -> p k q n", k=4, q=2)[:, :, q, :],
                                 bank[4 + q][:, :].rearrange("p (k n) -> p k n", k=4))
                    m.then_inc(na["pt_act"], 1)
                    act.wait_ge(na["o_done"], j)
                    copy(mixT[:, 1 + j, :], bank[3][:, 0:T]).then_inc(na["o_ready"], 1)

            na_pair(0, True, False)
            with act.Fori(1, NA_PAIRS) as j:
                na_pair(j, False, False)
            na_pair(NA_PAIRS, False, True)

            if subs > 1:
                act.wait_ge(mods_ready, 2)
                norm(2, xT, (x_done, 0, 1), hT, gcol(2), scol(mod, 3 * KT))
                act.wait_ge(hot_ready, 1)
                A(rt[:, 4, :, 0:G], rt[:, 0, :, 0:G], ACT.Exp).then_inc(route_act, 1)
                act.wait_ge(top_ready, 1)
                A(small[:, 8, :], small[:, 7, :], ACT.Exp).then_inc(route_act, 1)
                act.wait_ge(perm_pe, 1)
                for b in range(4):
                    m = copy(htok[:, b // 2, b % 2 * 512:(b % 2 + 1) * 512], bank[4 + b][:, :])
                m.then_inc(perm_act, 1)
                act.wait_ge(perm_pe, 3)
                copy(placeT, bank[1][:, :].rearrange("p (q t) -> p q t", q=TT)).then_inc(perm_act, 1)
                act.wait_ge(perm_pe, 4)
                for b in range(2):
                    m = copy(hS[:, 2 * b:2 * b + 2, :], pair_of(bank[4 + b]))
                m.then_inc(perm_act, 1)

                n0 = FIRST["moe"]

                def gather(g, at):
                    if g == 0:
                        act.wait_ge(perm_act, 3)
                        act.wait_ge(perm_dve, 1)
                    copy(part["hW"][g % 2][0], hS[:, :, bass.ds(at, WIN)]).then_inc(win_hi, 1)

                def win_expert(e, g):
                    def split(c, f):
                        if f == 0:
                            wait_chunk(act, n0 + c, e)
                        if f < 3:
                            act.wait_ge(quarter_done, 9 * e + 3 * c + f + 1)
                        else:
                            wait_used(act, n0 + c - 1, e)
                        copy(part["ehi"][f], full["quarter"](n0 + c, f)).then_inc(quarter_hi, 1)

                    def silu(c):
                        wait_used(act, n0 + c, e)
                        A(gact[c][0:WIN, 0, :], bank[c][0:WIN, 0:T], ACT.Silu).then_inc(e_silu, 1)

                    def high(c):
                        act.wait_ge(e_turned, 2 * e + c + 1)
                        copy(part["hidT"][0][:, 2 * c * WIN:2 * (c + 1) * WIN],
                             bank[2][:, 2 * c * WIN:2 * (c + 1) * WIN]).then_inc(e_hi, 1)

                    for f in range(4):
                        split(0, f)
                    for c in range(2):
                        for f in range(4):
                            if f == 2:
                                silu(c)
                            split(c + 1, f)
                        high(c)

                def expert(e):
                    for f in range(FT_E):
                        if f % 2 == 0:
                            act.wait_ge(moe_gu, 2 * e + f // 2 + 1)
                        else:
                            wait_used(act, FIRST["moe"] + f // 2, e)
                        A(gact[f % 3][:, 0, :], bank[f % 3][:, 0:T], ACT.Silu).then_inc(moe_silu, 1)

                moe_branches(act, expert, win_expert, lambda g: act.value_load(win[0:1, g:g + 1], min_val=0, max_val=T - WIN), gather)
                act.wait_ge(perm_pe, 5)
                for b in range(2):
                    m = copy(htok[:, b // 2, b % 2 * 512:(b % 2 + 1) * 512], bank[b][:, :])
                m.then_inc(perm_act, 1)
                norm(3, xT, (x_done, KT, 1), xT, lambda k: vc("normf", k, 1), lambda k: cst("zero"))

            for i in layers:
                if i == 0:
                    ready = (h_ready, KT * 3, 1)
                else:
                    ready = (x_done, KT * (1 + 2 * i), 1)
                act.wait_ge(mods_ready, 3 + 2 * i)
                norm(4 + 2 * i, xT, ready, hT, gcol(0), scol(mod, 0))
                base = epoch(i)

                def sb_pair(step, r, first=False, last=False):
                    j = step + RING * r + base
                    lne = prob[:, 0:2, 0:TRI]
                    if not first:
                        act.wait_ge(sk["zm_ready"], j)
                        A(lne, soft[:, 0:2, 0:TRI], ACT.Abs).then_inc(sk["abs"], 1)
                        act.wait_ge(sk["abs"], j)
                        A(lne, lne, ACT.Exp, scale=-1.0).then_inc(sk["exp"], 1)
                        act.wait_ge(sk["exp"], j)
                        A(lne, lne, ACT.Ln, bias=1.0).then_inc(sk["ln"], 1)
                    if not last:
                        act.wait_ge(sk["qk_proj"], j + 1)
                        copy(qk[:, :], bank[0][:, :]).then_inc(sk["qk_ready"], 1)
                    if not first:
                        act.wait_ge(sk["w_ready"], j)
                        A(probT[:, :, 0:TRI], prob[:, 2:4, 0:TRI], ACT.Exp).then_inc(sk["a_ready"], 1)
                        act.wait_ge(sk["o_done"], j)
                        copy(mixT[:, j - 1 - base, :], bank[3][:, 0:T]).then_inc(sk["o_ready"], 1)

                def sf_pair(step, r, first=False, last=False):
                    j = step + RING * r + base
                    if not first:
                        act.wait_ge(sf["m_ready"], j)
                        for h in range(2):
                            for q in range(2):
                                cols = slice(0, P) if q == 0 else slice(P, TRI)
                                c = 2 * h + q
                                A(prob[:, h, cols], soft[:, h, cols], ACT.Exp, bias=stat[:, 1, c:c + 1],
                                  accum_out=stat[:, 2, c:c + 1])
                        act.wait_ge(sf["sink_in"], j)
                        A(stat[:, 5, :], stat[:, 4, :], ACT.Exp).then_inc(sf["e_ready"], 1)
                    if not last:
                        act.wait_ge(sf["qk_proj"], j + 1)
                        b2 = bank[0][:, :].rearrange("p (t n) -> p t n", t=2)
                        copy(qk[:, :], bank[0][:, :]).then_inc(sf["raw"], 1)
                        A(xsq[:, 0:2, :], b2, ACT.Square).then_inc(sf["raw"], 1)
                        act.wait_ge(sf["ssum"], j + 1)
                        A(xn[:, 0:2, :], bank[2][:, :].rearrange("p (t n) -> p t n", t=2), ACT.Ln, scale=1.0 / HD,
                          bias=cst("eps")).then_inc(sf["ln"], 1)
                        act.wait_ge(sf["ln"], j + 1)
                        A(xn[:, 2:4, :], xn[:, 0:2, :], ACT.Exp, scale=-0.5).then_inc(sf["rinv"], 1)
                    if not first:
                        act.wait_ge(sf["t_done"], j)
                        copy(probT[:, 0, 0:TRI], bank[6][:, 0:TRI]).then_inc(sf["pt_act"], 1)
                        act.wait_ge(sf["o_done"], j)
                        copy(mixT[:, j - 1 - base, :], bank[3][:, 0:T]).then_inc(sf["o_ready"], 1)

                pair = sb_pair if KINDS[i] == "sb" else sf_pair
                pair(0, 0, first=True)
                steps(act, 1, PAIRS, pair)
                pair(PAIRS, 0, last=True)
                if 3 + 2 * i >= subs:
                    break
                act.wait_ge(mods_ready, 4 + 2 * i)
                n0 = FIRST[f"gu_{i}"]

                n1 = FIRST[f"down_{i}"]

                def split(step, r, f, down=False):
                    n = (n1 if down else n0) + step
                    if (down or step) and f < 3:
                        act.wait_ge(tile_done, 3 * split_count(i, step - 1, down) + f + 1 + 3 * RING * r)
                    elif down or step:
                        wait_used(act, n - 1, r)
                    copy((part["whd"] if down else part["whi"])[f], (full["w_down"] if down else full["w_gu"])(n, f)).then_inc(w_hi, 1)

                def silu(step, r):
                    s = step % RING
                    wait_used(act, n0 + step, r)
                    A(gact[s][:, :, :], bank[2 * s][:, :].rearrange("p (t n) -> p t n", t=2), ACT.Silu).then_inc(ffn_silu, 1)

                def gate_up(step, r):
                    wait_chunk(act, n0 + step, r)
                    for f in range(4):
                        if f == 2:
                            silu(step - 1, r)
                        split(step, r, f)

                def first_split():
                    wait_chunk(act, n0)
                    for f in range(2):
                        split(0, 0, f)

                norm(5 + 2 * i, xT, (x_done, KT * (2 + 2 * i), 1), hT, gcol(2), scol(mod, 3 * KT), first_split, True)
                act.wait_ge(h_hi, KT * (i + 1))
                for f in range(2, 4):
                    split(0, 0, f)
                for step in range(1, RING):
                    gate_up(step, 0)
                steps(act, RING, GU, gate_up)

                def hidden(p):
                    act.wait_ge(ffn_hid, GU * i + p + 1)
                    copy(part["hid_hi"][p], hid[:, 2 * p:2 * p + 2, :]).then_inc(f_hi, 1)

                for p in range(3):
                    hidden(p)
                wait_chunk(act, n1)
                for f in range(2):
                    split(0, 0, f, True)
                silu(GU - 1, 0)
                for p in range(3, GU):
                    hidden(p)
                    if p == 6:
                        for f in range(2, 4):
                            split(0, 0, f, True)

                def down(step, r):
                    wait_chunk(act, n1 + step, r)
                    for f in range(4):
                        split(step, r, f, True)

                for step in range(1, 2):
                    down(step, 0)
                steps(act, 2, KT, down)

        @block.vector
        def _(dve):
            V = nc.vector
            count = {}

            def then(ins, s):
                count[s] = count.get(s, 0) + 1
                ins.then_inc(CH[s], 1)
                dve.wait_ge(CH[s], count[s])

            CH = {"mods": mods_step, "route": route_step}

            def normalise(e):
                dve.wait_ge(rinv_ready, e + 1)
                for k in range(KT):
                    V.tensor_tensor(xn[:, k, :], xT[:, k, :], rinv[:, :], ALU.mult).then_inc(xn_ready, 1)

            def update(c, f, n, a, g):
                if f < 3:
                    dve.wait_ge(y_done, 6 * a + 3 * c + f + 1)
                else:
                    wait_used(dve, n)
                d = 4 * c + f
                V.scalar_tensor_tensor(xT[:, d, :], bank[(4 + d) % 8][:, 0:T], mod[:, g * KT + d:g * KT + d + 1], xT[:, d, :],
                                       ALU.mult, ALU.add).then_inc(x_done, 1)

            def normalise_in(e, src):
                dve.wait_ge(rinv_ready, e + 1)
                for k in range(KT):
                    if e == 1:
                        dve.wait_ge(h_ready, k + 1)
                    V.tensor_tensor(xn[:, k, :], src[:, k, :], rinv2[e], ALU.mult).then_inc(xn_ready, 1)

            for n in range(N_HEAD):
                if n == 2:
                    normalise_in(0, ctxT)
                wait_used(dve, n)
                V.tensor_copy(ada_row(n)[0:2, :], bank[4 + n][0:2, :]).then_inc(ada_rows, 1)
            dve.wait_ge(ada_cols, 1)
            m2 = bank[2][:, 0:4 * KT].rearrange("p (m c) -> p m c", c=2)
            then(V.tensor_tensor(mod[:, 0:2 * KT], m2[:, :, 0], vc("b_ada", 0, 2 * KT), ALU.add), "mods")
            then(V.tensor_tensor(modc[:, :], m2[:, :, 1], vc("b_ada", 0, 2 * KT), ALU.add), "mods")
            V.scalar_tensor_tensor(gain[:, 0, :], mod[:, KT:2 * KT], 1.0, vc("norm1"), ALU.add, ALU.mult)
            V.scalar_tensor_tensor(gain[:, 1, :], modc[:, KT:2 * KT], 1.0, vc("norm1"), ALU.add, ALU.mult).then_inc(mods_ready, 1)
            normalise_in(1, xT)

            n = FIRST["mix"] + 1
            wait_used(dve, n)
            dve.wait_ge(mix_act, 1)
            ch, cv = gact[1], gact[2]
            then(V.tensor_tensor(ch[:, :, :], gact[0][:, :, :], bank[3][:, :].rearrange("p (t n) -> p t n", t=2), ALU.mult), "mods")
            for f in range(2):
                tap = [vc("w_conv", 3 * f + t, 1) for t in range(3)]
                then(V.tensor_scalar(cv[:, f, :], ch[:, f, :], tap[1], None, ALU.mult), "mods")
                then(V.scalar_tensor_tensor(cv[:, f, 1:T], ch[:, f, 0:T - 1], tap[0], cv[:, f, 1:T], ALU.mult, ALU.add), "mods")
                then(V.scalar_tensor_tensor(cv[:, f, 0:T - 1], ch[:, f, 1:T], tap[2], cv[:, f, 0:T - 1], ALU.mult, ALU.add), "mods")
            V.tensor_tensor(mixT[:, 6:8, :], cv[:, :, :], bank[1][:, :].rearrange("p (t n) -> p t n", t=2), ALU.mult).then_inc(mix_dve, 1)

            def row_softmax_in(k, j):
                dve.wait_ge(k["mx"], j)
                V.tensor_scalar(stat[:, 1, :], stat[:, 0, :], -1.0, None, ALU.mult).then_inc(k["m_ready"], 1)

            def na_pair(j, first, last):
                if not first:
                    dve.wait_ge(na["scores"], j)
                    for c in range(4):
                        V.scalar_tensor_tensor(soft[:, c, 0:T], bank[4 + c][:, 0:T], SCALE, bias[:, c % 2, 2 * (j - 1) + c // 2, :],
                                               ALU.mult, ALU.add)
                        m = V.tensor_scalar(soft[:, c, T:2 * T], bank[4 + c][:, T:2 * T], SCALE, None, ALU.mult)
                    m.then_inc(na["s_ready"], 1)
                    dve.wait_ge(na["s_ready"], j)
                    V.tensor_reduce(stat[:, 0, :], soft[:, :, :], AX.X, ALU.max).then_inc(na["mx"], 1)
                    row_softmax_in(na, j)
                    dve.wait_ge(na["e_ready"], j)
                    V.reciprocal(stat[:, 3, :], stat[:, 2, :]).then_inc(na["rs"], 1)
                    dve.wait_ge(na["rs"], j)
                    for c in range(4):
                        m = V.tensor_scalar(prob[:, c, :], prob[:, c, :], stat[:, 3, c:c + 1], None, ALU.mult)
                    m.then_inc(na["p_ready"], 1)
                    dve.wait_ge(na["t_done"], j)
                    for q in range(2):
                        m = V.tensor_copy(probT[:, 1, :].rearrange("p (k q n) -> p k q n", k=4, q=2)[:, :, q, :],
                                          bank[6 + q][:, :].rearrange("p (k n) -> p k n", k=4))
                    m.then_inc(na["pt_dve"], 1)
                if not last:
                    wait_used(dve, FIRST["na"] + 1, j)
                    V.tensor_copy(ada_row(0)[0:1, :], bank[2][0:1, :])
                    wait_used(dve, FIRST["na"] + 2, j)
                    V.tensor_copy(ada_row(1)[0:1, :], bank[0][0:1, :]).then_inc(na["ada_row"], 1)
                    if not first:
                        dve.wait_ge(na["o_done"], j)
                    wait_used(dve, FIRST["na"], j)
                    V.tensor_copy(vv[:, :, :], bank[1][:, :].rearrange("p (t n) -> p t n", t=4)).then_inc(na["v_ready"], 1)
                    dve.wait_ge(na["ada_done"], j + 1)
                    V.tensor_tensor(mod[:, bass.ds(2 * KT + 8 * j, 8)], bank[2][:, 0:8],
                                    vec[:, bass.ds(VEC["b_ada"][0] + 2 * KT + 8 * j, 8)], ALU.add).then_inc(na["ada_ready"], 1)

            dve.wait_ge(bias_masked, 1)
            na_pair(0, True, False)
            with dve.Fori(1, NA_PAIRS) as j:
                na_pair(j, False, False)
            na_pair(NA_PAIRS, False, True)
            dve.wait_ge(na["ada_ready"], NA_PAIRS)
            V.scalar_tensor_tensor(gain[:, 2, :], mod[:, 4 * KT:5 * KT], 1.0, vc("norm2"), ALU.add, ALU.mult).then_inc(mods_ready, 1)
            for c in range(2):
                for f in range(4):
                    update(c, f, FIRST["out_0"] + c, 0, 2)

            if subs > 1:
                V.memset(qr[:, :], 0.0).then_inc(zeroed, 1)
                normalise(2)
                dve.wait_ge(route_done, 1)
                R = lambda i, n=E: rt[:, i, :, 0:n]
                S = lambda i: small[:, i, :]
                B = lambda a, n: a.unsqueeze(2).broadcast_to([P, TT, n])
                iota = lambda n: cst("iota", 0, n).unsqueeze(1).broadcast_to([P, TT, n])
                then(V.tensor_tensor(logit[:, :, :], bank[0][:, 0:TT * (G + E)].rearrange("p (t n) -> p t n", t=TT),
                                     vc("b_route").unsqueeze(1).broadcast_to([P, TT, G + E]), ALU.add), "route")

                def first_max(x, mx, eq, idx, hot, n):
                    then(V.tensor_reduce(mx, x, AX.X, ALU.max), "route")
                    then(V.tensor_tensor(eq, x, B(mx, n), ALU.is_equal), "route")
                    then(V.tensor_scalar(eq, eq, -64.0, None, ALU.mult), "route")
                    then(V.tensor_tensor(eq, eq, iota(n), ALU.add), "route")
                    then(V.tensor_reduce(idx, eq, AX.X, ALU.min), "route")
                    then(V.tensor_tensor(hot, eq, B(idx, n), ALU.is_equal), "route")

                lg = logit[:, :, 0:G]
                first_max(lg, S(0), R(1, G), S(1), R(3, G), G)
                V.tensor_tensor(R(0, G), lg, B(S(0), G), ALU.subtract).then_inc(hot_ready, 1)
                then(V.tensor_scalar(R(5, G), R(3, G), -NEG, NEG, ALU.mult, ALU.add), "route")
                then(V.tensor_tensor(R(6).rearrange("p t (g e) -> p t g e", g=G),
                                     logit[:, :, G:G + E].rearrange("p t (g e) -> p t g e", g=G),
                                     R(5, G).unsqueeze(3).broadcast_to([P, TT, G, EG]), ALU.add), "route")
                first_max(R(6), S(4), R(1), S(5), R(7), E)
                then(V.tensor_scalar(R(8), R(7), 2 * NEG, None, ALU.mult), "route")
                then(V.tensor_tensor(R(8), R(8), R(6), ALU.add), "route")
                first_max(R(8), S(6), R(1), S(5), R(9), E)
                V.tensor_tensor(S(7), S(6), S(4), ALU.subtract).then_inc(top_ready, 1)
                dve.wait_ge(route_act, 1)
                then(V.tensor_reduce(S(2), R(4, G), AX.X, ALU.add), "route")
                then(V.reciprocal(S(3), S(2)), "route")
                dve.wait_ge(route_act, 2)
                then(V.tensor_scalar(S(9), S(8), 1.0, None, ALU.add), "route")
                then(V.reciprocal(S(10), S(9)), "route")
                then(V.tensor_tensor(S(11), S(10), S(3), ALU.mult), "route")
                then(V.tensor_tensor(S(12), S(11), S(8), ALU.mult), "route")
                then(V.tensor_tensor(R(10), R(7), B(S(11), E), ALU.mult), "route")
                then(V.tensor_tensor(R(11), R(9), B(S(12), E), ALU.mult), "route")
                then(V.tensor_tensor(comb[:, :, :], R(10), R(11), ALU.add), "route")
                dve.wait_ge(perm_pe, 2)
                then(V.tensor_copy(gcount[:, 0, :], bank[1][:, 2 * G:3 * G]), "route")
                then(V.memset(gcount[:, 1, :], 0.0), "route")
                for g in range(1, G):
                    then(V.tensor_tensor(gcount[:, 1, g:g + 1], gcount[:, 1, g - 1:g], gcount[:, 0, g - 1:g], ALU.add), "route")
                then(V.tensor_reduce(gcount[:, 2, 0:1], gcount[:, 0, :], AX.X, ALU.max), "route")
                then(V.tensor_scalar(win[:, 0:G], gcount[:, 1, :], float(T - WIN), None, ALU.min), "route")
                V.tensor_scalar(win[:, G:G + 1], gcount[:, 2, 0:1], float(WIN), None, ALU.is_le).then_inc(win_ready, 1)
                for t in range(TT):
                    then(V.tensor_tensor(rt[:, 4, t, 0:G], bank[1][:, t * G:(t + 1) * G], gcount[:, 1, :], ALU.add), "route")
                then(V.tensor_tensor(R(4, G), R(4, G), R(3, G), ALU.mult), "route")
                then(V.tensor_reduce(S(13), R(4, G), AX.X, ALU.add), "route")
                for t in range(TT):
                    m = V.tensor_scalar(place[:, t, :], cst("iota"), small[:, 13, t:t + 1], None, ALU.is_equal)
                m.then_inc(place_ready, 1)
                dve.wait_ge(perm_pe, 3)
                V.tensor_copy(combT[:, :], bank[0][0:E, 0:T]).then_inc(comb_ready, 1)
                dve.wait_ge(perm_pe, 4)
                for b in range(2, 4):
                    m = V.tensor_copy(hS[:, 2 * b:2 * b + 2, :], pair_of(bank[4 + b]))
                m.then_inc(perm_dve, 1)
                dve.wait_ge(comb_ready, 1)

                V.memset(ysum[:, :, :], 0.0).then_inc(win_zero, 1)

                def window(g):
                    return dve.value_load(win[0:1, g:g + 1], min_val=0, max_val=T - WIN)

                def gather(g, at):
                    V.tensor_copy(comb_e[:, 0:WIN], combT[:, bass.ds(at, WIN)]).then_inc(comb_sel, 1)
                    dve.wait_ge(win_hi, g + 1)
                    V.tensor_tensor(part["hW"][g % 2][1], hS[:, :, bass.ds(at, WIN)], part["hW"][g % 2][0].bitcast(F32),
                                    ALU.subtract).then_inc(win_in, 1)
                    dve.wait_ge(w_turned, g + 1)
                    V.tensor_copy(wcomb[0:WIN, g % 2, :], bank[3][0:WIN, 0:E]).then_inc(w_taken, 1)
                    dve.wait_ge(w_taken, g + 1)

                def scatter(g, at):
                    wait_used(dve, FIRST["moe"] + 2, EG * (g + 1) - 1)
                    for b in range(2):
                        m = V.tensor_copy(ywin[:, b * 512:(b + 1) * 512], bank[4 + g % 2 * 2 + b][0:WIN, :])
                    m.then_inc(y_taken, 1)
                    dve.wait_ge(y_turned, g + 1)
                    if g == 0:
                        dve.wait_ge(win_zero, 1)
                    else:
                        dve.wait_ge(win_out, g)
                    for b in range(2):
                        yb = ysum[:, 4 * b:4 * b + 4, bass.ds(at, WIN)]
                        m = V.tensor_tensor(yb, yb, bank[4 + g % 2 * 2 + b][:, 0:4 * WIN].rearrange("p (d n) -> p d n", d=4), ALU.add)
                    m.then_inc(win_out if g < G - 1 else perm_dve, 1)

                def collect(end):
                    if end:
                        wait_used(dve, FIRST["moe"] + 3 * E - 1)
                        for b in range(4):
                            m = V.tensor_copy(ysum[:, 2 * b:2 * b + 2, :], pair_of(bank[4 + b]))
                        m.then_inc(perm_dve, 1)

                def win_expert(e, g):
                    def split(c, f):
                        dve.wait_ge(quarter_hi, 12 * e + 4 * c + f + 1)
                        n = FIRST["moe"] + c
                        V.tensor_tensor(part["quarter"](n, f), full["quarter"](n, f), part["ehi"][f].bitcast(F32), ALU.subtract).then_inc(quarter_lo, 1)

                    for f in range(4):
                        split(0, f)
                    for c in range(2):
                        for f in range(4):
                            if f == 2:
                                dve.wait_ge(e_silu, 2 * e + c + 1)
                                V.scalar_tensor_tensor(gact[c][0:WIN, 1, :], gact[c][0:WIN, 0, :], wcomb[0:WIN, g % 2, bass.ds(e, 1)],
                                                       bank[c][0:WIN, T:2 * T], ALU.mult, ALU.mult).then_inc(e_hidden, 1)
                            split(c + 1, f)
                        dve.wait_ge(e_hi, 2 * e + c + 1)
                        cols = slice(2 * c * WIN, 2 * (c + 1) * WIN)
                        V.tensor_tensor(part["hidT"][1][:, cols], bank[2][:, cols], part["hidT"][0][:, cols].bitcast(F32),
                                        ALU.subtract).then_inc(e_lo, 1)

                def expert(e):
                    V.tensor_scalar(comb_e[:, :], combT[:, :], const[0:E, bass.ds(CONST["ident"][0] + e, 1)], None,
                                    ALU.mult).then_inc(comb_sel, 1)
                    for f in range(FT_E):
                        dve.wait_ge(moe_silu, 4 * e + f + 1)
                        V.tensor_tensor(gact[f % 3][:, 1, :], gact[f % 3][:, 0, :], bank[f % 3][:, T:2 * T], ALU.mult).then_inc(moe_mul, 1)
                        dve.wait_ge(moe_mul, 4 * e + f + 1)
                        if f == 0:
                            dve.wait_ge(comb_bc, e + 1)
                            wait_used(dve, FIRST["moe"] + 2 - RING, e)
                        V.tensor_tensor(hid[:, f, :], gact[f % 3][:, 1, :], bank[3][:, 0:T], ALU.mult).then_inc(moe_hid, 1)

                moe_branches(dve, expert, win_expert, window, gather, scatter, collect)
                dve.wait_ge(perm_pe, 5)
                for b in range(2, 4):
                    m = V.tensor_copy(htok[:, b // 2, b % 2 * 512:(b % 2 + 1) * 512], bank[b][:, :])
                m.then_inc(perm_dve, 1)
                for d in range(KT):
                    dve.wait_ge(unperm, d // 2 + 1)
                    V.scalar_tensor_tensor(xT[:, d, :], bank[4 + d // 2][:, (d % 2) * T:(d % 2 + 1) * T],
                                           mod[:, 5 * KT + d:5 * KT + d + 1], xT[:, d, :], ALU.mult, ALU.add).then_inc(x_done, 1)
                normalise(3)

            def take_mods(i, half):
                if i not in layers:
                    return
                dve.wait_ge(mods_done, 2 * i + half + 1)
                lo = 3 * KT * half
                then(V.tensor_tensor(mod[:, lo:lo + 3 * KT], bank[6][:, 0:3 * KT], vc("b_ada2", MODS * i + lo, 3 * KT), ALU.add), "mods")
                V.scalar_tensor_tensor(gain[:, 2 * half, :], mod[:, lo + KT:lo + 2 * KT], 1.0, vc("gains2", (2 * i + half) * KT, KT),
                                       ALU.add, ALU.mult).then_inc(mods_ready, 1)

            take_mods(0, 0)
            for i in layers:
                normalise(4 + 2 * i)
                take_mods(i, 1)
                n0 = FIRST[f"pair_{i}"]
                base = epoch(i)

                def values(k, step, r, j, first):
                    if not first:
                        dve.wait_ge(k["o_done"], j)
                    wait_used(dve, n0 + step, r)
                    V.tensor_copy(vv[:, 0:2, :], bank[1][:, 0:T].rearrange("p (t n) -> p t n", t=TT)).then_inc(k["v_ready"], 1)

                def sb_pair(step, r, first=False, last=False):
                    j = step + RING * r + base
                    mask = cst("mask_sb")
                    if not first:
                        dve.wait_ge(sk["scores"], j)
                        for h in range(2):
                            m = V.scalar_tensor_tensor(soft[:, h, 0:TRI], bank[4 + h][:, 0:TRI], SCALE, mask, ALU.mult, ALU.add)
                        m.then_inc(sk["zm_ready"], 1)
                        dve.wait_ge(sk["ln"], j)
                        V.scalar_tensor_tensor(soft[:, 2:4, 0:TRI], soft[:, 0:2, 0:TRI], 0.0, prob[:, 0:2, 0:TRI],
                                               ALU.max, ALU.add).then_inc(sk["sp_ready"], 1)
                        dve.wait_ge(sk["suffix"], j)
                        for h in range(2):
                            m = V.tensor_tensor(prob[:, 2 + h, 0:TRI], soft[:, h, 0:TRI], bank[6 + h][:, 0:TRI], ALU.subtract)
                        m.then_inc(sk["w_ready"], 1)
                    if not last:
                        values(sk, step, r, j, first)

                def sf_pair(step, r, first=False, last=False):
                    j = step + RING * r + base
                    kind = KINDS[i]
                    mask = cst("mask_" + kind)
                    if not first:
                        dve.wait_ge(sf["scores"], j)
                        for h in range(2):
                            m = V.scalar_tensor_tensor(soft[:, h, 0:TRI], bank[4 + h][:, 0:TRI], SCALE, mask, ALU.mult, ALU.add)
                        m.then_inc(sf["s_ready"], 1)
                        dve.wait_ge(sf["s_ready"], j)
                        V.tensor_reduce(stat[:, 6, 0:4:2], soft[:, 0:2, 0:P], AX.X, ALU.max)
                        V.tensor_reduce(stat[:, 6, 1:4:2], soft[:, 0:2, P:TRI], AX.X, ALU.max).then_inc(sf["mx"], 1)
                        dve.wait_ge(sf["mx"], j)
                        sink = (j - 1 - base) * 4
                        snk = vec[:, bass.ds(VEC["sinks"][0] + 4 * PAIRS * (kind == "moba") + sink, 4)]
                        V.tensor_tensor(stat[:, 0, :], stat[:, 6, :], snk, ALU.max).then_inc(sf["rs"], 1)
                        dve.wait_ge(sf["rs"], 3 * j - 2)
                        V.tensor_scalar(stat[:, 1, :], stat[:, 0, :], -1.0, None, ALU.mult).then_inc(sf["m_ready"], 1)
                        V.tensor_tensor(stat[:, 4, :], snk, stat[:, 0, :], ALU.subtract).then_inc(sf["sink_in"], 1)
                        dve.wait_ge(sf["e_ready"], j)
                        V.tensor_tensor(stat[:, 7, :], stat[:, 2, :], stat[:, 5, :], ALU.add).then_inc(sf["rs"], 1)
                        dve.wait_ge(sf["rs"], 3 * j - 1)
                        V.reciprocal(stat[:, 3, :], stat[:, 7, :]).then_inc(sf["rs"], 1)
                        dve.wait_ge(sf["rs"], 3 * j)
                        for h in range(2):
                            V.tensor_scalar(prob[:, h, 0:P], prob[:, h, 0:P], stat[:, 3, 2 * h:2 * h + 1], None, ALU.mult)
                            m = V.tensor_scalar(prob[:, h, P:TRI], prob[:, h, P:TRI], stat[:, 3, 2 * h + 1:2 * h + 2], None, ALU.mult)
                        m.then_inc(sf["p_ready"], 1)
                    if not last:
                        dve.wait_ge(sf["rinv"], j + 1)
                        for c in range(2):
                            V.scalar_tensor_tensor(qn[:, c * T:(c + 1) * T], qk[:, c * T:(c + 1) * T], vc("qk_" + kind, c, 1),
                                                   xn[:, 2 + c, :], ALU.mult, ALU.mult).then_inc(sf["qn_ready"], 1)
                        dve.wait_ge(sf["qn_ready"], 2 * j + 2)
                        V.tensor_tensor(xn[:, 4:6, :], qn[:, :].rearrange("p (c n) -> p c n", c=2),
                                        cst("cos").unsqueeze(1).broadcast_to([P, 2, T]), ALU.mult).then_inc(sf["rope"], 1)
                    if not first:
                        dve.wait_ge(sf["t_done"], j)
                        V.tensor_copy(probT[:, 1, 0:TRI], bank[7][:, 0:TRI]).then_inc(sf["pt_dve"], 1)
                    if not last:
                        dve.wait_ge(sf["rot"], j + 1)
                        V.tensor_tensor(xn[:, 6:8, :], bank[2][:, :].rearrange("p (c n) -> p c n", c=2),
                                        cst("sin").unsqueeze(1).broadcast_to([P, 2, T]), ALU.mult).then_inc(sf["rope"], 1)
                        dve.wait_ge(sf["rope"], 2 * j + 2)
                        V.tensor_tensor(qr[:, :].rearrange("p (c n) -> p c n", c=2), xn[:, 4:6, :], xn[:, 6:8, :],
                                        ALU.add).then_inc(sf["qr_ready"], 1)
                        values(sf, step, r, j, first)

                pair = sb_pair if KINDS[i] == "sb" else sf_pair
                pair(0, 0, first=True)
                steps(dve, 1, PAIRS, pair)
                pair(PAIRS, 0, last=True)
                for c in range(2):
                    for f in range(4):
                        update(c, f, FIRST[f"out_{i + 1}"] + c, 1 + i, 2)
                if 3 + 2 * i >= subs:
                    break
                def split(step, r, f, down=False):
                    dve.wait_ge(w_hi, 4 * split_count(i, step, down) + f + 1 + 4 * RING * r)
                    n = FIRST[f"down_{i}" if down else f"gu_{i}"] + step
                    if down:
                        m = V.tensor_tensor(part["w_down"](n, f), full["w_down"](n, f), part["whd"][f].bitcast(F32), ALU.subtract)
                    else:
                        m = V.tensor_tensor(part["w_gu"](n, f), full["w_gu"](n, f), part["whi"][f].bitcast(F32), ALU.subtract)
                    m.then_inc(w_lo, 1)

                def product(step, r):
                    s = step % RING
                    dve.wait_ge(ffn_silu, GU * i + step + 1 + RING * r)
                    V.tensor_tensor(hid[:, bass.ds(2 * step + 2 * RING * r, 2), :], gact[s][:, :, :],
                                    bank[2 * s + 1][:, :].rearrange("p (t n) -> p t n", t=2), ALU.mult).then_inc(ffn_hid, 1)

                def gate_up(step, r):
                    for f in range(4):
                        if f == 2:
                            product(step - 1, r)
                        split(step, r, f)

                for f in range(2):
                    split(0, 0, f)
                normalise(5 + 2 * i)
                for k in range(KT):
                    dve.wait_ge(h_hi, KT * i + k + 1)
                    V.tensor_tensor(part["hT"][:, k, :], hT[:, k, :], part["xsq"][:, k, :].bitcast(F32), ALU.subtract).then_inc(h_lo, 1)
                for f in range(2, 4):
                    split(0, 0, f)
                take_mods(i + 1, 0)
                for step in range(1, RING):
                    gate_up(step, 0)
                steps(dve, RING, GU, gate_up)

                def hidden(p):
                    dve.wait_ge(f_hi, GU * i + p + 1)
                    two = slice(2 * p, 2 * p + 2)
                    V.tensor_tensor(part["hid"][:, two, :], hid[:, two, :], part["hid_hi"][p].bitcast(F32), ALU.subtract).then_inc(f_lo, 1)

                for p in range(3):
                    hidden(p)
                for f in range(2):
                    split(0, 0, f, True)
                product(GU - 1, 0)
                for p in range(3, GU):
                    hidden(p)
                    if p == 6:
                        for f in range(2, 4):
                            split(0, 0, f, True)

                def gated(step, r):
                    wait_used(dve, FIRST[f"down_{i}"] + step, r)
                    d = step + RING * r
                    x = xT[:, bass.ds(d, 1), :]
                    V.scalar_tensor_tensor(x, bank[5 + step % RING][:, 0:T].unsqueeze(1), mod[:, bass.ds(5 * KT + d, 1)], x,
                                           ALU.mult, ALU.add).then_inc(x_done, 1)

                def down(step, r):
                    for f in range(4):
                        if f == 2:
                            gated(step - 1, r)
                        split(step, r, f, True)

                down(1, 0)
                steps(dve, 2, KT, down)
                gated(KT - 1, 0)


def constants():
    i, t = np.arange(P), np.arange(T)
    col = {}
    col["ident"] = np.eye(P)
    col["ones"] = np.ones((P, P))
    col["headones"] = i[:, None] // HD == i[None, :] // HD
    half, d = HD // 2, i % HD
    rot = np.zeros((P, P))
    lo = i[d < half]
    rot[lo + half, lo] = -1.0
    rot[lo, lo + half] = 1.0
    col["rot"] = rot
    col["suffix"] = i[:, None] >= i[None, :]
    f = np.float32
    inv = f(1.0) / (f(10000.0) ** (np.arange(0, HD, 2, dtype=f) / f(HD)))
    ang = (t.astype(f)[:, None] * inv[None, :]).astype(f)
    col["cos"] = np.cos(ang)[:, d % half].T
    col["sin"] = np.sin(ang)[:, d % half].T
    k, q = i[:, None], t[None, :]
    sb = [k < q, k + P < q[:, P:]]
    col["mask_sb"] = np.where(np.concatenate(sb, 1), 0.0, NEG)
    rows = [(i[:, None] + a, np.arange(n)[None, :]) for a, n in ((0, P), (P, T))]
    col["mask_moba"] = np.where(np.concatenate([kk <= qq for qq, kk in rows], 1), 0.0, NEG)
    col["mask_swa"] = np.where(np.concatenate([(kk <= qq) & (qq - kk < P) for qq, kk in rows], 1), 0.0, NEG)
    qc, kc = i[:, None] % GRID_W, t[None, :] % GRID_W
    start = np.clip(qc - NA_KW // 2, 0, GRID_W - NA_KW)
    col["mask_na"] = np.where((kc >= start) & (kc < start + NA_KW), 0.0, NEG)
    w = 2 * np.pi * ((t[:, None] * t[None, :]) % T) / T
    dft = np.stack([np.cos(w), np.sin(w)], 1).reshape(TT, P, 2, T)
    col["dft"] = dft.transpose(1, 0, 2, 3).reshape(P, -1)
    same = i[:, None] // HD == i[None, :] // HD
    w = 2 * np.pi * ((d[:, None] * d[None, :]) % HD) / HD
    norm = 1.0 / np.sqrt(T * HD)
    col["cd"] = np.where(same, np.cos(w) * norm, 0.0)
    col["sd"] = np.where(same, -np.sin(w) * norm, 0.0)
    col["iota"] = np.broadcast_to(np.arange(T), (P, T))
    col["before"] = i[:, None] < i[None, :]
    col["eps"] = np.full((P, 1), EPS)
    col["zero"] = np.zeros((P, 1))
    out = np.zeros((P, N_CONST), np.float32)
    for name, (a, b) in CONST.items():
        out[:, a:b] = col[name]
    return out


def cols(v):
    v = np.asarray(v)
    return np.ascontiguousarray(np.moveaxis(v.reshape(*v.shape[:-1], -1, P), -1, 0)).reshape(P, -1)


def by_row(w, lo, n):
    return w[:, lo:lo + n].reshape(-1, P, n).transpose(1, 0, 2)


def lay_out(a):
    f = {k: np.asarray(v) for k, v in a.items()}
    o = {"const": constants()}
    rep = lambda v: np.broadcast_to(v, (P,) + v.shape)
    sinks = np.repeat(f["swa_sinks_2"][0], 2)
    o["vec"] = np.concatenate([
        np.stack([cols(f["c"][0]), cols(f["c_ctx"])], 2).reshape(P, -1), cols(f["c_2"][0]),
        cols(f["norm1"][0]), cols(f["norm2"][0]), cols(f["norm_final"]),
        f["w_conv"][0].reshape(3, 2, P).transpose(2, 1, 0).reshape(P, -1), cols(f["b_ada"][0]),
        cols(f["norm_gain_2"]), cols(f["ada_b_2"]),
        np.tile(f["moba_qk_gain_2"][0].T, (2, 1)), np.tile(f["swa_qk_gain_2"][0].T, (2, 1)),
        rep(sinks), np.full((P, 4 * PAIRS), NEG, np.float32),
        rep(np.concatenate([f["b_rg"][0], f["b_re"][0]]))], 1)
    o["xT"] = f["x"][0].T.reshape(KT, P, T).transpose(1, 0, 2)
    o["ctxT"] = f["ctx"][0].T.reshape(KT, P, T).transpose(1, 0, 2)
    ada = [by_row(f["w_ada"][0], 512 * n, 512) for n in range(MODS // 4)]
    o["ada_head"] = np.stack(ada[:N_HEAD])
    w = f["w_in"][0]
    q, k, v, gb, gc, h = (256, 768, 1280, 1792, 2048, 2304)
    o["mix"] = np.stack([np.concatenate([by_row(w, a_, 256), by_row(w, b_, 256)], 2) for a_, b_ in ((0, gb), (gc, h))])
    na = []
    for j in range(NA_PAIRS):
        pair = np.concatenate([by_row(w, at + P * j, P) for at in (q, k, v)], 2).reshape(P, -1)
        na += [np.concatenate([pair, np.zeros((P, SLOT - pair.shape[1]), np.float32)], 1)]
        na += [x.reshape(P, -1) for x in ada[N_HEAD + 2 * j:N_HEAD + 2 * j + 2]]
    o["na"] = np.stack(na)
    outs = [f["w_out"][0], f["sb_w_out_2"][0], f["moba_w_out_2"][0], f["swa_w_out_2"][0], f["sb_w_out_2"][1]]
    for n, w in enumerate(outs):
        o[f"out_{n}"] = np.stack([by_row(w, 512 * c, 512) for c in range(2)])
    o["wf"] = by_row(f["w_fourier"][0], 0, 256)
    o["wr"] = np.concatenate([by_row(f["w_rg"][0], 0, G), by_row(f["w_re"][0], 0, E)], 2)
    t = np.arange(T)
    row = t[None, :] // GRID_W - t[:, None] // GRID_W + NA_KH - 1
    coff = np.clip(t[None, :] % GRID_W - t[:, None] % GRID_W + NA_KW - 1, 0, 2 * NA_KW - 2)
    o["bias"] = f["rpb"][0][:, row, coff].reshape(NA_HEADS, TT, P, T).transpose(2, 1, 0, 3)
    o["moe"] = np.stack([x for e in range(E) for x in (
        *(np.concatenate([by_row(f[n][0, e], 2 * P * c, 2 * P) for n in ("w_gate", "w_up")], 2).reshape(P, -1) for c in range(2)),
        by_row(f["w_down"][0, e], 0, D).reshape(P, -1))])
    o["ada2"] = np.stack([by_row(f["ada_w_2"][i], 512 * n, 512) for i in range(LAYERS) for n in range(12)])
    swa = f["swa_w_in_2"][0]
    for i, kind in enumerate(KINDS):
        ch = []
        for j in range(PAIRS):
            if kind == "swa":
                g = j * 2 // PAIRS
                kk, vv_ = by_row(swa, D + HD * g, HD), by_row(swa, D + P + HD * g, HD)
                parts = [by_row(swa, P * j, P), kk, kk, vv_, vv_]
            else:
                w = f["moba_w_in_2"][0] if kind == "moba" else f["sb_w_in_2"][i // 3]
                parts = [by_row(w, at + P * j, P) for at in (0, D, 2 * D)]
            ch.append(np.concatenate(parts, 2))
        o[f"pair_{i}"] = np.stack(ch)
        g_, u_, d_ = f["ffn_w_gate_2"][i], f["ffn_w_up_2"][i], f["ffn_w_down_2"][i]
        o[f"gu_{i}"] = np.stack([np.concatenate([by_row(g_, 256 * n, 256), by_row(u_, 256 * n, 256)], 2) for n in range(GU)])
        o[f"down_{i}"] = np.stack([by_row(d_, P * n, P) for n in range(KT)])
    shape = {name: (n, P, width) for name, n, width in PHASES}
    shape["ada2"] = (LAYERS * 12, P, SLOT)
    return {k: np.ascontiguousarray(v.reshape(shape.get(k, v.shape))) for k, v in o.items()}


def kernel(**inputs):
    import concourse.bacc as bacc
    from concourse.bass_utils import run_bass_kernel_spmd

    nc = bacc.Bacc("TRN2", target_bir_lowering=False, num_devices=1)
    arrays = {f"in_{k}": v for k, v in lay_out(inputs).items()}
    ins = {k: nc.dram_tensor("in_" + k, arrays["in_" + k].shape, F32, kind="ExternalInput").ap() for k in
           [n[3:] for n in arrays]}
    out = nc.dram_tensor("out_xT", (P, KT, T), F32, kind="ExternalOutput").ap()
    build(nc, ins, out)
    r = run_bass_kernel_spmd(nc, [arrays], core_ids=[0])
    y = np.asarray(r.results[0]["out_xT"])
    return np.ascontiguousarray(y.transpose(2, 1, 0)).reshape(1, T, D)
```
